# Optimizing a Trainium2 kernel written in Bass

```python
import jax
import jax.numpy as jnp
from jax import lax
import numpy as np
import jax, jax.numpy as jnp

D_MODEL = 1024
BATCH = 1
SEQ = 256
DEPTH = 2

GRID_W = 64
CTX_LEN = 256
N_MIXERS = 2
N_ATTN_LAYERS = (DEPTH + N_MIXERS - 1) // N_MIXERS
N_RET_LAYERS = DEPTH // N_MIXERS

HEAD_DIM = 64
N_HEADS = D_MODEL // HEAD_DIM
N_KV_HEADS = N_HEADS // 4
GQA_GROUP = N_HEADS // N_KV_HEADS
WINDOW = 128
ATTN_BLOCK = 128
ATTN_PROJ = (N_HEADS + 2 * N_KV_HEADS) * HEAD_DIM

RET_HEADS = D_MODEL // 256
RET_QK_DIM = D_MODEL // RET_HEADS
RET_V_DIM = 2 * D_MODEL // RET_HEADS
RET_VWIDTH = 2 * D_MODEL
RET_CHUNK = 128
RET_PROJ = 2 * D_MODEL + 2 * RET_VWIDTH

D_FF = -(-8 * D_MODEL // (3 * 256)) * 256

ROPE_BASE = 10000.0
EPS = 1e-6
NEG_INF = -1e30


def rms_norm(x, g):
    xf = x.astype(jnp.float32)
    y = xf * lax.rsqrt(jnp.mean(xf * xf, axis=-1, keepdims=True) + EPS)
    return (y * g.astype(jnp.float32)).astype(x.dtype)

def modulate(h, shift, scale):
    return h * (1 + scale) + shift

def grid_positions(n):
    rows = n // GRID_W
    row = jnp.broadcast_to(jnp.arange(rows, dtype=jnp.int32)[:, None], (rows, GRID_W)).reshape(n)
    col = jnp.broadcast_to(jnp.arange(GRID_W, dtype=jnp.int32)[None, :], (rows, GRID_W)).reshape(n)
    return row, col

def rope_tables(n, head_dim):
    row, col = grid_positions(n)
    axis_dim = head_dim // 2
    inv = ROPE_BASE ** (-jnp.arange(0, axis_dim, 2, dtype=jnp.float32) / axis_dim)
    ang_r = row.astype(jnp.float32)[:, None] * inv
    ang_c = col.astype(jnp.float32)[:, None] * inv
    return jnp.cos(ang_r), jnp.sin(ang_r), jnp.cos(ang_c), jnp.sin(ang_c)

def rotate_axis(x, cos, sin):
    x1, x2 = jnp.split(x, 2, axis=-1)
    cos = cos[:, None, :]
    sin = sin[:, None, :]
    return jnp.concatenate([x1 * cos - x2 * sin, x1 * sin + x2 * cos], axis=-1)

def rope_2d(x, tables):
    cos_r, sin_r, cos_c, sin_c = tables
    xr, xc = jnp.split(x.astype(jnp.float32), 2, axis=-1)
    out = jnp.concatenate([rotate_axis(xr, cos_r, sin_r), rotate_axis(xc, cos_c, sin_c)], axis=-1)
    return out.astype(x.dtype)

def swiglu(h, w_in, w_out):
    gate, up = jnp.split(h @ w_in, 2, axis=-1)
    return (jax.nn.silu(gate) * up) @ w_out

def windowed_gqa_sink(h_x, h_c, w_qkv, q_gain, k_gain, sink, w_o, need_ctx_out):
    B, S, _ = h_x.shape
    L = h_c.shape[1]
    nb = S // ATTN_BLOCK
    band = ATTN_BLOCK + 2 * WINDOW
    scale = HEAD_DIM ** -0.5
    qd = N_HEADS * HEAD_DIM
    kvd = N_KV_HEADS * HEAD_DIM
    tables = rope_tables(S, HEAD_DIM)
    sink_g = sink.astype(jnp.float32).reshape(N_KV_HEADS, GQA_GROUP)[None, :, :, None, None]

    q_x, k_x, v_x = jnp.split(h_x @ w_qkv, [qd, qd + kvd], axis=-1)
    q_x = rope_2d(rms_norm(q_x.reshape(B, S, N_HEADS, HEAD_DIM), q_gain), tables)
    q_x = q_x.reshape(B, S, N_KV_HEADS, GQA_GROUP, HEAD_DIM)
    k_x = rope_2d(rms_norm(k_x.reshape(B, S, N_KV_HEADS, HEAD_DIM), k_gain), tables)
    v_x = v_x.reshape(B, S, N_KV_HEADS, HEAD_DIM)
    k_c, v_c = jnp.split(h_c @ w_qkv[:, qd:], 2, axis=-1)
    k_c = rms_norm(k_c.reshape(B, L, N_KV_HEADS, HEAD_DIM), k_gain)
    v_c = v_c.reshape(B, L, N_KV_HEADS, HEAD_DIM)

    pad = ((0, 0), (WINDOW, WINDOW), (0, 0), (0, 0))
    k_pad = jnp.pad(k_x, pad)
    v_pad = jnp.pad(v_x, pad)
    r_idx = jnp.arange(ATTN_BLOCK, dtype=jnp.int32)[:, None]
    n_idx = jnp.arange(band, dtype=jnp.int32)[None, :]
    in_window = (n_idx >= r_idx) & (n_idx - r_idx <= 2 * WINDOW)

    def block(b):
        start = b * ATTN_BLOCK
        qb = lax.dynamic_slice_in_dim(q_x, start, ATTN_BLOCK, axis=1)
        kb = lax.dynamic_slice_in_dim(k_pad, start, band, axis=1)
        vb = lax.dynamic_slice_in_dim(v_pad, start, band, axis=1)
        key_pos = start - WINDOW + n_idx
        valid = in_window & (key_pos >= 0) & (key_pos < S)
        s_ctx = jnp.einsum('bqkgd,bnkd->bkgqn', qb, k_c, preferred_element_type=jnp.float32) * scale
        s_loc = jnp.einsum('bqkgd,bnkd->bkgqn', qb, kb, preferred_element_type=jnp.float32) * scale
        s_loc = jnp.where(valid, s_loc, NEG_INF)
        sink_col = jnp.broadcast_to(sink_g, s_ctx.shape[:-1] + (1,))
        p = jax.nn.softmax(jnp.concatenate([s_ctx, s_loc, sink_col], axis=-1), axis=-1).astype(vb.dtype)
        return (jnp.einsum('bkgqn,bnkd->bqkgd', p[..., :L], v_c)
                + jnp.einsum('bkgqn,bnkd->bqkgd', p[..., L:L + band], vb))

    o_x = jnp.moveaxis(lax.map(block, jnp.arange(nb, dtype=jnp.int32)), 0, 1).reshape(B, S, qd)
    out_x = o_x @ w_o

    out_c = None
    if need_ctx_out:
        q_c = rms_norm((h_c @ w_qkv[:, :qd]).reshape(B, L, N_HEADS, HEAD_DIM), q_gain)
        q_c = q_c.reshape(B, L, N_KV_HEADS, GQA_GROUP, HEAD_DIM)
        s_c = jnp.einsum('bqkgd,bnkd->bkgqn', q_c, k_c, preferred_element_type=jnp.float32) * scale
        sink_col = jnp.broadcast_to(sink_g, s_c.shape[:-1] + (1,))
        p_c = jax.nn.softmax(jnp.concatenate([s_c, sink_col], axis=-1), axis=-1).astype(v_c.dtype)
        o_c = jnp.einsum('bkgqn,bnkd->bqkgd', p_c[..., :L], v_c)
        out_c = o_c.reshape(B, L, qd) @ w_o
    return out_c, out_x

def retention_chunked(q, k, v, log_gamma, state0):
    B, T, H, _ = q.shape
    nc = T // RET_CHUNK
    pos = jnp.arange(RET_CHUNK, dtype=jnp.float32)
    diff = pos[:, None] - pos[None, :]
    intra = jnp.where(diff >= 0, jnp.exp(log_gamma[:, None, None] * jnp.maximum(diff, 0.0)), 0.0)
    q_decay = jnp.exp(log_gamma[None, :] * (pos + 1.0)[:, None])[None, :, :, None]
    k_decay = jnp.exp(log_gamma[None, :] * (RET_CHUNK - 1.0 - pos)[:, None])[None, :, :, None]
    chunk_decay = jnp.exp(log_gamma * RET_CHUNK)[None, :, None, None]

    def to_chunks(a):
        return jnp.moveaxis(a.reshape(B, nc, RET_CHUNK, H, a.shape[-1]), 1, 0)

    def step(state, inp):
        qc, kc, vc = inp
        scores = jnp.einsum('bnhd,bmhd->bhnm', qc, kc) * intra
        inner = jnp.einsum('bhnm,bmhe->bnhe', scores, vc)
        cross = jnp.einsum('bnhd,bhde->bnhe', qc, state) * q_decay
        new_state = state * chunk_decay + jnp.einsum('bmhd,bmhe->bhde', kc * k_decay, vc)
        return new_state, inner + cross

    state, out = lax.scan(step, state0, (to_chunks(q), to_chunks(k), to_chunks(v)))
    return jnp.moveaxis(out, 0, 1).reshape(B, T, H, v.shape[-1]), state

def retention_final_state(k, v, log_gamma):
    T = k.shape[1]
    pos = jnp.arange(T, dtype=jnp.float32)
    decay = jnp.exp(log_gamma[None, :] * (T - 1.0 - pos)[:, None])[None, :, :, None]
    return jnp.einsum('bthd,bthe->bhde', k * decay, v)

def bidir_retention(h_x, h_c, w_qkvg, decay_logit, gn_gain, w_o, need_ctx_out):
    B, S, _ = h_x.shape
    L = h_c.shape[1]
    qk = RET_HEADS * RET_QK_DIM
    f32 = jnp.float32
    tables = rope_tables(S, RET_QK_DIM)
    log_g = jax.nn.log_sigmoid(decay_logit.astype(f32))
    k_scale = RET_QK_DIM ** -0.5

    q_x, k_x, v_x, g_x = jnp.split(h_x @ w_qkvg, [qk, 2 * qk, 2 * qk + RET_VWIDTH], axis=-1)
    q_x = rope_2d(q_x.reshape(B, S, RET_HEADS, RET_QK_DIM), tables).astype(f32)
    k_x = rope_2d(k_x.reshape(B, S, RET_HEADS, RET_QK_DIM), tables).astype(f32) * k_scale
    v_x = v_x.reshape(B, S, RET_HEADS, RET_V_DIM).astype(f32)
    k_c, v_c = jnp.split(h_c @ w_qkvg[:, qk:2 * qk + RET_VWIDTH], [qk], axis=-1)
    k_c = k_c.reshape(B, L, RET_HEADS, RET_QK_DIM).astype(f32) * k_scale
    v_c = v_c.reshape(B, L, RET_HEADS, RET_V_DIM).astype(f32)

    def flip(a):
        return jnp.flip(a, axis=1)

    def gated_out(o, g):
        mu = jnp.mean(o, axis=-1, keepdims=True)
        var = jnp.mean(jnp.square(o - mu), axis=-1, keepdims=True)
        y = ((o - mu) * lax.rsqrt(var + EPS)).reshape(o.shape[0], o.shape[1], RET_VWIDTH) * gn_gain.astype(f32)
        return (jax.nn.silu(g) * y.astype(g.dtype)) @ w_o

    out_c = None
    if need_ctx_out:
        q_c = (h_c @ w_qkvg[:, :qk]).reshape(B, L, RET_HEADS, RET_QK_DIM).astype(f32)
        g_c = h_c @ w_qkvg[:, 2 * qk + RET_VWIDTH:]
        zero_state = jnp.zeros((B, RET_HEADS, RET_QK_DIM, RET_V_DIM), f32)
        oc_f, state_f = retention_chunked(q_c, k_c, v_c, log_g[0], zero_state)
        oc_b, state_b = retention_chunked(flip(q_c), flip(k_c), flip(v_c), log_g[1], zero_state)
        out_c = gated_out(oc_f + flip(oc_b), g_c)
    else:
        state_f = retention_final_state(k_c, v_c, log_g[0])
        state_b = retention_final_state(flip(k_c), flip(v_c), log_g[1])

    ox_f, _ = retention_chunked(q_x, k_x, v_x, log_g[0], state_f)
    ox_b, _ = retention_chunked(flip(q_x), flip(k_x), flip(v_x), log_g[1], state_b)
    out_x = gated_out(ox_f + flip(ox_b), g_x)
    return out_c, out_x

def first_inputs(seed: int = 0) -> dict:
    key = jax.random.key(seed)
    ks = jax.random.split(key, 19)
    f32 = jnp.float32

    def nrm(k, shape, scale):
        return jax.random.normal(k, shape, f32) * scale

    gamma = 1.0 - 2.0 ** (-5.0 - np.arange(RET_HEADS))
    decay_init = jnp.asarray(np.log(gamma / (1.0 - gamma)), dtype=f32)
    return {
        'x': nrm(ks[0], (BATCH, SEQ, D_MODEL), 1.0),
        'c': nrm(ks[1], (BATCH, D_MODEL), 1.0),
        'ctx': nrm(ks[2], (BATCH, CTX_LEN, D_MODEL), 1.0),
        'c_ctx': nrm(ks[3], (D_MODEL,), 1.0),
        'ada_w': nrm(ks[4], (DEPTH, D_MODEL, 6 * D_MODEL), 0.5 * D_MODEL ** -0.5),
        'ada_b': nrm(ks[5], (DEPTH, 6 * D_MODEL), 0.02),
        'norm1_g': 1.0 + nrm(ks[6], (DEPTH, D_MODEL), 0.02),
        'norm2_g': 1.0 + nrm(ks[7], (DEPTH, D_MODEL), 0.02),
        'ffn_w_in': nrm(ks[8], (DEPTH, D_MODEL, 2 * D_FF), D_MODEL ** -0.5),
        'ffn_w_out': nrm(ks[9], (DEPTH, D_FF, D_MODEL), D_FF ** -0.5),
        'attn_w_qkv': nrm(ks[10], (N_ATTN_LAYERS, D_MODEL, ATTN_PROJ), D_MODEL ** -0.5),
        'attn_q_norm': 1.0 + nrm(ks[11], (N_ATTN_LAYERS, HEAD_DIM), 0.02),
        'attn_k_norm': 1.0 + nrm(ks[12], (N_ATTN_LAYERS, HEAD_DIM), 0.02),
        'attn_sink': nrm(ks[13], (N_ATTN_LAYERS, N_HEADS), 0.5),
        'attn_w_o': nrm(ks[14], (N_ATTN_LAYERS, N_HEADS * HEAD_DIM, D_MODEL), (N_HEADS * HEAD_DIM) ** -0.5),
        'ret_w_qkvg': nrm(ks[15], (N_RET_LAYERS, D_MODEL, RET_PROJ), D_MODEL ** -0.5),
        'ret_decay_logit': decay_init[None, None, :] + nrm(ks[16], (N_RET_LAYERS, 2, RET_HEADS), 0.01),
        'ret_gn_g': 1.0 + nrm(ks[17], (N_RET_LAYERS, RET_VWIDTH), 0.02),
        'ret_w_o': nrm(ks[18], (N_RET_LAYERS, RET_VWIDTH, D_MODEL), RET_VWIDTH ** -0.5),
    }

def first_block(x, c, ctx, c_ctx, ada_w, ada_b, norm1_g, norm2_g, ffn_w_in, ffn_w_out,
              attn_w_qkv, attn_q_norm, attn_k_norm, attn_sink, attn_w_o,
              ret_w_qkvg, ret_decay_logit, ret_gn_g, ret_w_o):
    c_act = jax.nn.silu(c)[:, None, :]
    cc_act = jax.nn.silu(c_ctx)[None, None, :]
    y_ctx = ctx
    for i in range(DEPTH):
        need_ctx_out = i < DEPTH - 1
        mx = jnp.split(c_act @ ada_w[i] + ada_b[i], 6, axis=-1)
        mc = jnp.split(cc_act @ ada_w[i] + ada_b[i], 6, axis=-1)
        h_x = modulate(rms_norm(x, norm1_g[i]), mx[0], mx[1])
        h_c = modulate(rms_norm(y_ctx, norm1_g[i]), mc[0], mc[1])
        j = i // N_MIXERS
        if i % N_MIXERS == 0:
            out_c, out_x = windowed_gqa_sink(h_x, h_c, attn_w_qkv[j], attn_q_norm[j], attn_k_norm[j],
                                             attn_sink[j], attn_w_o[j], need_ctx_out)
        else:
            out_c, out_x = bidir_retention(h_x, h_c, ret_w_qkvg[j], ret_decay_logit[j], ret_gn_g[j],
                                           ret_w_o[j], need_ctx_out)
        x = x + mx[2] * out_x
        x = x + mx[5] * swiglu(modulate(rms_norm(x, norm2_g[i]), mx[3], mx[4]), ffn_w_in[i], ffn_w_out[i])
        if need_ctx_out:
            y_ctx = y_ctx + mc[2] * out_c
            y_ctx = y_ctx + mc[5] * swiglu(modulate(rms_norm(y_ctx, norm2_g[i]), mc[3], mc[4]),
                                           ffn_w_in[i], ffn_w_out[i])
    return x


CHUNK = 64
WIN_CHUNKS = WINDOW // CHUNK
BAND = (WIN_CHUNKS + 1) * CHUNK
ATTN_WIDTH = D_MODEL // 2
N_Q_HEADS = ATTN_WIDTH // HEAD_DIM
N_KV_HEADS_2 = N_Q_HEADS // 4
KV_WIDTH = N_KV_HEADS_2 * HEAD_DIM
LRU_WIDTH = D_MODEL
LRU_BLOCKS = 16
LRU_BLOCK = LRU_WIDTH // LRU_BLOCKS
CONV_WIDTH = 4
LRU_C = 8.0
N_MEM = 256
MEM_HEADS = 4
MEM_WIDTH = D_MODEL // 2
MEM_HEAD_DIM = MEM_WIDTH // MEM_HEADS
N_BRANCH = 3
D_FF_2 = 11 * D_MODEL // 4
IN_WIDTH = ATTN_WIDTH + 2 * KV_WIDTH + 2 * LRU_WIDTH + MEM_WIDTH + N_BRANCH * D_MODEL


def rmsnorm(x, g):
    x32 = x.astype(jnp.float32)
    y = x32 * lax.rsqrt(jnp.mean(x32 * x32, axis=-1, keepdims=True) + EPS)
    return (y * g.astype(jnp.float32)).astype(x.dtype)

def swiglu_2(h, w_gate, w_up, w_down):
    return (jax.nn.silu(h @ w_gate) * (h @ w_up)) @ w_down

def alibi_slopes(n):
    return jnp.asarray(np.array([2.0 ** (-8.0 * (i + 1) / n) for i in range(n)], dtype=np.float32))

def window_attention(q, k, v, sinks):
    B, S = q.shape[0], q.shape[1]
    nc = S // CHUNK
    G = N_Q_HEADS // N_KV_HEADS_2
    pad = WIN_CHUNKS * CHUNK
    kp = jnp.pad(k, ((0, 0), (pad, 0), (0, 0), (0, 0))).reshape(B, nc + WIN_CHUNKS, CHUNK, N_KV_HEADS_2, HEAD_DIM)
    vp = jnp.pad(v, ((0, 0), (pad, 0), (0, 0), (0, 0))).reshape(B, nc + WIN_CHUNKS, CHUNK, N_KV_HEADS_2, HEAD_DIM)
    kb = jnp.concatenate([kp[:, j:j + nc] for j in range(WIN_CHUNKS + 1)], axis=2)
    vb = jnp.concatenate([vp[:, j:j + nc] for j in range(WIN_CHUNKS + 1)], axis=2)
    qb = q.reshape(B, nc, CHUNK, N_KV_HEADS_2, G, HEAD_DIM)
    s = jnp.einsum('bcqkgd,bcskd->bckgqs', qb, kb).astype(jnp.float32) * (HEAD_DIM ** -0.5)
    qi = jnp.arange(CHUNK) + pad
    kj = jnp.arange(BAND)
    dist = jnp.abs(qi[:, None] - kj[None, :]).astype(jnp.float32)
    slopes = alibi_slopes(N_Q_HEADS).reshape(N_KV_HEADS_2, G)
    s = s - slopes[:, :, None, None] * dist
    key_chunk = jnp.arange(nc)[:, None] - WIN_CHUNKS + kj[None, :] // CHUNK
    valid = key_chunk >= 0
    s = jnp.where(valid[None, :, None, None, None, :], s, -jnp.inf)
    sink = sinks.astype(jnp.float32).reshape(N_KV_HEADS_2, G)[None, None, :, :, None, None]
    m = jnp.maximum(jnp.max(s, axis=-1, keepdims=True), sink)
    p = jnp.exp(s - m)
    p = p / (jnp.sum(p, axis=-1, keepdims=True) + jnp.exp(sink - m))
    o = jnp.einsum('bckgqs,bcskd->bcqkgd', p.astype(v.dtype), vb)
    return o.reshape(B, S, ATTN_WIDTH)

def rglru_branch(xr, yr, conv_w, conv_b, wa, ba, wx, bx, lam):
    B, S = xr.shape[0], xr.shape[1]
    xc = lax.conv_general_dilated(xr, conv_w[:, None, :].astype(xr.dtype), window_strides=(1,),
                                  padding=[(CONV_WIDTH - 1, 0)],
                                  dimension_numbers=('NWC', 'WIO', 'NWC'),
                                  feature_group_count=LRU_WIDTH) + conv_b
    xb = xc.reshape(B, S, LRU_BLOCKS, LRU_BLOCK)
    r = jax.nn.sigmoid((jnp.einsum('bshi,hij->bshj', xb, wa).reshape(B, S, LRU_WIDTH) + ba).astype(jnp.float32))
    gi = jax.nn.sigmoid((jnp.einsum('bshi,hij->bshj', xb, wx).reshape(B, S, LRU_WIDTH) + bx).astype(jnp.float32))
    log_a = -LRU_C * r * jax.nn.softplus(-lam.astype(jnp.float32))
    a = jnp.exp(log_a)
    mult = jnp.sqrt(jnp.maximum(1.0 - jnp.exp(2.0 * log_a), 0.0))
    mult = jnp.where(jnp.arange(S)[None, :, None] == 0, 1.0, mult)
    b = mult * gi * xc.astype(jnp.float32)

    def combine(left, right):
        al, bl = left
        ar, br = right
        return al * ar, ar * bl + br

    _, h = lax.associative_scan(combine, (a, b), axis=1)
    return h.astype(xr.dtype) * jax.nn.gelu(yr)

def memory_attention(cq, mem_n, w_mem_kv):
    B, S = cq.shape[0], cq.shape[1]
    M = mem_n.shape[1]
    kv = mem_n @ w_mem_kv
    k = kv[..., :MEM_WIDTH].reshape(B, M, MEM_HEADS, MEM_HEAD_DIM)
    v = kv[..., MEM_WIDTH:].reshape(B, M, MEM_HEADS, MEM_HEAD_DIM)
    q = cq.reshape(B, S, MEM_HEADS, MEM_HEAD_DIM)
    s = jnp.einsum('bshd,bmhd->bhsm', q, k).astype(jnp.float32) * (MEM_HEAD_DIM ** -0.5)
    p = jax.nn.softmax(s, axis=-1).astype(v.dtype)
    return jnp.einsum('bhsm,bmhd->bshd', p, v).reshape(B, S, MEM_WIDTH)

def second_inputs(seed: int = 0) -> dict:
    key = jax.random.key(seed)
    ks = jax.random.split(key, 32)
    f32 = jnp.float32

    def nrm(k, shape, fan_in):
        return jax.random.normal(k, shape, f32) * (fan_in ** -0.5)

    def gain(k, shape):
        return 1.0 + 0.05 * jax.random.normal(k, shape, f32)

    u = jax.random.uniform(ks[20], (DEPTH, LRU_WIDTH), f32, 0.9, 0.999)
    a0 = u ** (1.0 / LRU_C)
    lam = jnp.log(a0) - jnp.log1p(-a0)
    return {
        'x': jax.random.normal(ks[0], (BATCH, SEQ, D_MODEL), f32),
        'mem': jax.random.normal(ks[1], (BATCH, N_MEM, D_MODEL), f32),
        'ffn1_norm': gain(ks[2], (DEPTH, D_MODEL)),
        'ffn1_w_gate': nrm(ks[3], (DEPTH, D_MODEL, D_FF_2), D_MODEL),
        'ffn1_w_up': nrm(ks[4], (DEPTH, D_MODEL, D_FF_2), D_MODEL),
        'ffn1_w_down': nrm(ks[5], (DEPTH, D_FF_2, D_MODEL), D_FF_2),
        'mix_norm': gain(ks[6], (DEPTH, D_MODEL)),
        'w_in': nrm(ks[7], (DEPTH, D_MODEL, IN_WIDTH), D_MODEL),
        'gate_bias': 0.1 * jax.random.normal(ks[8], (DEPTH, N_BRANCH * D_MODEL), f32),
        'attn_sinks': 0.5 * jax.random.normal(ks[9], (DEPTH, N_Q_HEADS), f32),
        'w_attn_out': nrm(ks[10], (DEPTH, ATTN_WIDTH, D_MODEL), ATTN_WIDTH),
        'conv_w': nrm(ks[11], (DEPTH, CONV_WIDTH, LRU_WIDTH), CONV_WIDTH),
        'conv_b': 0.02 * jax.random.normal(ks[12], (DEPTH, LRU_WIDTH), f32),
        'lru_wa': nrm(ks[13], (DEPTH, LRU_BLOCKS, LRU_BLOCK, LRU_BLOCK), LRU_BLOCK),
        'lru_ba': 0.1 * jax.random.normal(ks[14], (DEPTH, LRU_WIDTH), f32),
        'lru_wx': nrm(ks[15], (DEPTH, LRU_BLOCKS, LRU_BLOCK, LRU_BLOCK), LRU_BLOCK),
        'lru_bx': 0.1 * jax.random.normal(ks[16], (DEPTH, LRU_WIDTH), f32),
        'lru_lambda': lam,
        'w_lru_out': nrm(ks[17], (DEPTH, LRU_WIDTH, D_MODEL), LRU_WIDTH),
        'mem_norm': gain(ks[18], (DEPTH, D_MODEL)),
        'w_mem_kv': nrm(ks[19], (DEPTH, D_MODEL, 2 * MEM_WIDTH), D_MODEL),
        'w_mem_out': nrm(ks[21], (DEPTH, MEM_WIDTH, D_MODEL), MEM_WIDTH),
        'w_out': nrm(ks[22], (DEPTH, D_MODEL, D_MODEL), D_MODEL),
        'ffn2_norm': gain(ks[23], (DEPTH, D_MODEL)),
        'ffn2_w_gate': nrm(ks[24], (DEPTH, D_MODEL, D_FF_2), D_MODEL),
        'ffn2_w_up': nrm(ks[25], (DEPTH, D_MODEL, D_FF_2), D_MODEL),
        'ffn2_w_down': nrm(ks[26], (DEPTH, D_FF_2, D_MODEL), D_FF_2),
        'final_norm': gain(ks[27], (D_MODEL,)),
    }

def second_block(x, mem, ffn1_norm, ffn1_w_gate, ffn1_w_up, ffn1_w_down, mix_norm, w_in, gate_bias,
              attn_sinks, w_attn_out, conv_w, conv_b, lru_wa, lru_ba, lru_wx, lru_bx, lru_lambda,
              w_lru_out, mem_norm, w_mem_kv, w_mem_out, w_out, ffn2_norm, ffn2_w_gate, ffn2_w_up,
              ffn2_w_down, final_norm):
    B, S = x.shape[0], x.shape[1]
    o1 = ATTN_WIDTH
    o2 = o1 + KV_WIDTH
    o3 = o2 + KV_WIDTH
    o4 = o3 + LRU_WIDTH
    o5 = o4 + LRU_WIDTH
    o6 = o5 + MEM_WIDTH
    for l in range(DEPTH):
        x = x + 0.5 * swiglu_2(rmsnorm(x, ffn1_norm[l]), ffn1_w_gate[l], ffn1_w_up[l], ffn1_w_down[l])
        h = rmsnorm(x, mix_norm[l])
        proj = h @ w_in[l]
        q = proj[..., :o1].reshape(B, S, N_Q_HEADS, HEAD_DIM)
        k = proj[..., o1:o2].reshape(B, S, N_KV_HEADS_2, HEAD_DIM)
        v = proj[..., o2:o3].reshape(B, S, N_KV_HEADS_2, HEAD_DIM)
        xr = proj[..., o3:o4]
        yr = proj[..., o4:o5]
        cq = proj[..., o5:o6]
        g = jax.nn.sigmoid((proj[..., o6:] + gate_bias[l]).astype(jnp.float32)).astype(x.dtype)
        g = g.reshape(B, S, N_BRANCH, D_MODEL)
        br_attn = window_attention(q, k, v, attn_sinks[l]) @ w_attn_out[l]
        br_lru = rglru_branch(xr, yr, conv_w[l], conv_b[l], lru_wa[l], lru_ba[l], lru_wx[l], lru_bx[l],
                              lru_lambda[l]) @ w_lru_out[l]
        br_mem = memory_attention(cq, rmsnorm(mem, mem_norm[l]), w_mem_kv[l]) @ w_mem_out[l]
        merged = g[:, :, 0] * br_attn + g[:, :, 1] * br_lru + g[:, :, 2] * br_mem
        x = x + merged @ w_out[l]
        x = x + 0.5 * swiglu_2(rmsnorm(x, ffn2_norm[l]), ffn2_w_gate[l], ffn2_w_up[l], ffn2_w_down[l])
    return rmsnorm(x, final_norm)


def setup_inputs(seed=0):
    out = dict(first_inputs(seed))
    for name, value in second_inputs(seed + 1).items():
        if name != "x":
            out[name + "_2"] = value
    return out


def reference(
    x, c, ctx, c_ctx, ada_w, ada_b, norm1_g, norm2_g, ffn_w_in, ffn_w_out, attn_w_qkv,
    attn_q_norm, attn_k_norm, attn_sink, attn_w_o, ret_w_qkvg, ret_decay_logit, ret_gn_g,
    ret_w_o, mem_2, ffn1_norm_2, ffn1_w_gate_2, ffn1_w_up_2, ffn1_w_down_2, mix_norm_2, w_in_2,
    gate_bias_2, attn_sinks_2, w_attn_out_2, conv_w_2, conv_b_2, lru_wa_2, lru_ba_2, lru_wx_2,
    lru_bx_2, lru_lambda_2, w_lru_out_2, mem_norm_2, w_mem_kv_2, w_mem_out_2, w_out_2,
    ffn2_norm_2, ffn2_w_gate_2, ffn2_w_up_2, ffn2_w_down_2, final_norm_2,
):
    x = first_block(
        x, c, ctx, c_ctx, ada_w, ada_b, norm1_g, norm2_g, ffn_w_in, ffn_w_out, attn_w_qkv,
        attn_q_norm, attn_k_norm, attn_sink, attn_w_o, ret_w_qkvg, ret_decay_logit, ret_gn_g,
        ret_w_o,
    )
    return second_block(
        x, mem_2, ffn1_norm_2, ffn1_w_gate_2, ffn1_w_up_2, ffn1_w_down_2, mix_norm_2, w_in_2,
        gate_bias_2, attn_sinks_2, w_attn_out_2, conv_w_2, conv_b_2, lru_wa_2, lru_ba_2,
        lru_wx_2, lru_bx_2, lru_lambda_2, w_lru_out_2, mem_norm_2, w_mem_kv_2, w_mem_out_2,
        w_out_2, ffn2_norm_2, ffn2_w_gate_2, ffn2_w_up_2, ffn2_w_down_2, final_norm_2,
    )


_drawn_inputs = setup_inputs


def setup_inputs(seed=0):
    import zlib

    import numpy as np

    out = dict(_drawn_inputs(seed))
    spreads = {}
    factors = {'norm1_g': 6.348,
     'norm2_g': 5.336,
     'attn_q_norm': 8.0,
     'attn_k_norm': 8.0,
     'attn_sink': 8.0,
     'ret_gn_g': 8.0,
     'gate_bias_2': 3.754,
     'attn_sinks_2': 200.0,
     'lru_ba_2': 64.0,
     'lru_bx_2': 200.0,
     'mem_norm_2': 8.0,
     'ffn1_norm_2': 8.0,
     'w_attn_out_2': 12.498,
     'conv_w_2': 7.709,
     'conv_b_2': 64.0,
     'lru_wa_2': 8.0,
     'lru_wx_2': 24.435,
     'lru_lambda_2': 8.0,
     'ffn2_norm_2': 8.0,
     'w_lru_out_2': 2.852}
    for name, (base, spread) in spreads.items():
        noise = np.random.default_rng([zlib.crc32(name.encode()), seed]).standard_normal(out[name].shape)
        drawn = base * np.exp(spread * noise) if base else spread * noise
        out[name] = jnp.asarray(drawn.astype(out[name].dtype))
    for name, factor in factors.items():
        out[name] = (out[name] * factor).astype(out[name].dtype)
    return out
```

```python
from contextlib import ExitStack

import numpy as np

import concourse.bass as bass
from concourse import mybir

F32 = mybir.dt.float32
F32R = mybir.dt.float32r
ALU = mybir.AluOpType
ACT = mybir.ActivationFunctionType

P = 128
D = 1024
DC = D // P
S = 256
FF = 2816
FC = FF // P
COLS = 256
KCH = 4
SLOTS = 4
LAG = 3
EPS = 1e-6
MASKED = -1e30
HEADS, HD, GROUP = 16, 64, 4
RH, RQ, RV = 4, 256, 512
WH = 8
MH = 4
LAYERS2 = 2
ROPE_BASE = 10000.0
GRID_W = 64



def shape_constants():
    tok = np.arange(S)
    row, col = (tok // GRID_W).astype(np.float32), (tok % GRID_W).astype(np.float32)

    def rope(head_dim, d):
        axis = head_dim // 2
        half = axis // 2
        inv = (np.float32(ROPE_BASE) ** (-np.arange(0, axis, 2, dtype=np.float32) / np.float32(axis))).astype(np.float32)
        pos = np.where((d // axis == 0)[:, None], row[None, :], col[None, :]).astype(np.float32)
        ang = (pos * inv[d % half][:, None]).astype(np.float32)
        sign = np.where(d % axis < half, -1.0, 1.0)[:, None]
        return np.cos(ang), np.sin(ang) * sign

    p = np.arange(P)
    cos_a, sin_a = rope(HD, p % HD)
    rc, rs = zip(*[rope(RQ, p + P * c) for c in range(2)])
    q = p[:, None, None] + P * np.arange(2)[None, :, None]
    k = np.arange(S)[None, None, :]
    window = np.concatenate([np.where(np.abs(k - q) <= P, 0.0, MASKED), np.zeros((P, 2, S))], axis=2)
    back = q // 64 - k // 64
    alibi = np.where((back >= 0) & (back <= 2), np.abs(q - k), -MASKED)
    m = q
    n = k
    parts = {
        "ident": np.eye(P), "ones": np.ones((P, P)), "alibi": alibi.reshape(P, -1),
        "slopes": np.tile(-(2.0 ** -np.arange(1.0, WH + 1)) * HD ** 0.5, (P, 1)),
        "sel": np.repeat(np.eye(2), 2, axis=0)[np.minimum(p, 3)] * (p < 4)[:, None],
        "headones": (p[:, None] // HD == p[None, :] // HD), "partner": (p[:, None] == (p[None, :] ^ (HD // 4))),
        "cos_a": cos_a, "sin_a": sin_a, "window": window.reshape(P, -1),
        "cos_r": np.concatenate(rc, 1), "sin_r": np.concatenate(rs, 1),
        "ahead": np.maximum(n - m, 0).reshape(P, -1), "behind": np.maximum(m - n, 0).reshape(P, -1),
        "since": (n + S - m).reshape(P, -1),
    }
    at, width = {}, 0
    for name, a in parts.items():
        at[name] = (width, a.shape[1])
        width += a.shape[1]
    return np.concatenate([np.asarray(a, np.float32) for a in parts.values()], axis=1), at




class Job:

    def __init__(self, unit_chunks, ends, iters, acts_from=0):
        self.unit_chunks = unit_chunks
        self.ends = ends
        self.iters = iters
        self.body = len(unit_chunks)
        self.per = len(ends)
        self.unit0 = self.block0 = self.unit_step = self.block_step = 0
        assert self.body % SLOTS == 0 and self.per % 2 == 0

    def unit(self, l, it, p):
        return self.unit0 + p + it * self.body + (l * self.unit_step if self.unit_step else 0)

    def block(self, l, it, b):
        return self.block0 + b + it * self.per + (l * self.block_step if self.block_step else 0)

    def taken(self, l, it, b):
        return self.block(l, it, b) + 3

    def done(self, l=None):
        return self.taken(l, self.iters - 1, self.per - 1)

    def loaded(self, l, it, p):
        return 16 * (self.unit0 // SLOTS + p // SLOTS + 1) + it * (16 * self.body // SLOTS) \
            + (l * (16 * self.unit_step // SLOTS) if self.unit_step else 0)


def columns(k_chunks, n):
    per_block = [KCH] * (k_chunks // KCH) + ([k_chunks % KCH] if k_chunks % KCH else [])
    blocks = 2
    while len(per_block) * blocks % SLOTS:
        blocks += 2
    units = per_block * blocks
    return Job(units, [len(per_block) * (b + 1) - 1 for b in range(blocks)], n // COLS // blocks)


FIRST = ["ada0", "q0", "kv0", "wo0", "gu0", "dn0", "ada1", "rq", "rk", "rv", "rg", "rwo", "gu1", "dn1"]
SECOND = ["gua", "dna", "memk", "memv", "xr", "yr", "gates", "kvlru", "q", "cq", "attn_out", "lru_out",
          "mem_out", "w_out", "gub", "dnb"]


def plan():
    two = lambda n: columns(DC, n)
    jobs = {
        "ada0": two(6 * D), "q0": two(D), "kv0": two(512), "wo0": two(D), "gu0": two(2 * FF), "dn0": columns(FC, D),
        "ada1": two(6 * D), "rq": two(D), "rk": two(D), "rv": two(2 * D), "rg": two(2 * D), "rwo": columns(16, D),
        "gu1": two(2 * FF), "dn1": columns(FC, D),
        "gua": two(2 * FF), "dna": columns(FC, D), "memk": two(512), "memv": two(512), "xr": two(D), "yr": two(D),
        "gates": two(3 * D), "kvlru": Job([4, 4, 2, 2], [1, 1, 2, 2, 3, 3], 1), "q": two(512), "cq": two(512),
        "attn_out": columns(4, D), "lru_out": two(D), "mem_out": columns(4, D), "w_out": two(D),
        "gub": two(2 * FF), "dnb": columns(FC, D),
    }
    u = b = 0
    for name in FIRST + SECOND:
        if name == SECOND[0]:
            u2, b2 = u, b
        jobs[name].unit0, jobs[name].block0 = u, b
        u += jobs[name].iters * jobs[name].body
        b += jobs[name].iters * jobs[name].per
    for name in SECOND:
        jobs[name].unit_step, jobs[name].block_step = u - u2, b - b2
    return jobs


JOBS = plan()

NORMS1 = 7
NORM_LAST = NORMS1 + 4 * LAYERS2
X_START, X_MEM = 8, 12
ITEMS0, ITEMS_WIN, ITEMS_MEM = 4 * HEADS, 2 * WH, 2 * MH
PAIRS0, PAIRS_WIN, PAIRS_MEM = HEADS // 2, WH // 2, MH

ADA_B, C_COL, CC_COL, NORM1 = 0, 96, 104, 112
GATE_B, CONV_W, FFN1_N, MIX_N, CONV_B, BA, BX, LAM, MEM_N, FFN2_N, CUR = 0, 24, 56, 64, 72, 80, 88, 96, 104, 112, 120
PRM_DMAS = 2 * 10 + 3 + 4 + 3
NORM2, FINAL_N, GN_G, Q_N, K_N, PRM3 = 0, 16, 24, 40, 41, 42


def build(nc, a, out, const_at):
    J = JOBS
    st = ExitStack()
    with st:
        def sb(name, shape, dt=F32, on=st):
            return on.enter_context(nc.sbuf_tensor(name, shape, dt))

        def sem(name):
            return st.enter_context(nc.semaphore(name))

        raw = sb("raw", [P, SLOTS, KCH, COLS])
        w_hi = sb("w_hi", [P, SLOTS, KCH, COLS], F32R)
        w_lo = sb("w_lo", [P, SLOTS, KCH, COLS], F32R)
        xT = sb("xT", [P, DC, 2 * S])
        h_hi = sb("h_hi", [P, DC, 2 * S], F32R)
        h_lo = sb("h_lo", [P, DC, 2 * S], F32R)
        rows = sb("rows", [P, 2 * D])
        prm = sb("prm", [P, 4, P])
        cur = sb("cur", [P, CUR + 16])
        mod = sb("mod", [P, 48, 2])
        gain = sb("gain", [P, 2, DC, 2])
        ident = sb("ident", [P, P])
        ones = sb("ones", [P, P])
        alibi = sb("alibi", [P, 2 * S])
        nomask = sb("nomask", [P, S])
        sel = sb("sel", [P, 2])
        slopes = sb("slopes", [P, WH])
        c_parts = sb("c_parts", [P, DC, 4], F32R)
        c_act = sb("c_act", [P, 16])
        std = sb("std", [P, S])
        rstd = sb("rstd", [P, S])
        act_buf = sb("act_buf", [P, 2, 2 * S])
        eps = sb("eps", [P, 1])
        soft_in = sb("soft_in", [P, 24])
        soft_e = sb("soft_e", [P, 24])
        soft_t = sb("soft_t", [P, 24])
        soft_w = sb("soft_w", [P, 24])
        soft_p = sb("soft_p", [P, 24])
        soft = sb("soft", [P, 24])
        decay = sb("decay", [P, 3, 8])
        lam_s = sb("lam_s", [P, 2, 2, 8])
        sinks = sb("sinks", [P, 16 + 16])
        sink_l = sb("sink_l", [P, WH])
        smx, snm, ssum, ses, sden, srec = [sb(f"soft_{k}", [P, 8]) for k in ("mx", "nm", "sum", "es", "den", "rec")]
        passed = sb("passed", [P, 8])
        stats = sb("stats", [P, 2, 6])
        mv = sb("mv", [P, 2, 2])
        gstd = sb("gstd", [P, 2])

        def arena(*parts):
            with ExitStack() as on:
                return [sb(n, s, d, on) for n, s, d in parts]

        hid_hi, hid_lo = arena(("hid_hi", [P, FC, 2 * S], F32R), ("hid_lo", [P, FC, 2 * S], F32R))
        nf, ada_s, rows_c, prm_rows = arena(
            ("nf", [P, DC, S], F32), ("ada_s", [4, 6 * D], F32), ("rows_c", [P, 2 * D], F32), ("prm_rows", [P, 4, P], F32))
        (qk, v_tok, k_dup, probs, probs_t, sq_b, sd_b, rot_b, headones, partner, cos_a, sin_a, window) = arena(
            ("qk", [P, 10, 2 * S], F32), ("v_tok", [P, 4, 256], F32), ("k_dup", [P, 4, 2 * S], F32),
            ("probs", [P, 2, 2 * S], F32), ("probs_t", [P, 2, 4, S], F32), ("sq_b", [P, 2, 2 * S], F32),
            ("sd_b", [P, 2, 2 * S], F32), ("rot_b", [P, 2, 2, S], F32),
            ("headones", [P, P], F32), ("partner", [P, P], F32), ("cos_a", [P, S], F32), ("sin_a", [P, S], F32),
            ("window", [P, 2, 2 * S], F32))
        r_q, r_k, r_v, r_g, cos_r, sin_r, swp, rot, r_d, r_p = arena(
            ("r_q", [P, DC, S], F32), ("r_k", [P, DC, 2 * S], F32), ("r_v", [P, 4, 2 * D], F32), ("r_g", [P, 16, S], F32),
            ("cos_r", [P, 2, S], F32), ("sin_r", [P, 2, S], F32), ("swp", [P, 2, S], F32), ("rot", [P, 2, S], F32),
            ("r_d", [P, 4, S], F32), ("r_p", [P, 4, S], F32))
        r_y = arena(("r_skip", [P, 72 * S + 4 * S], F32), ("r_y", [P, 2, 2 * S], F32))[1]
        (gates, gy, XR, XC, R, GI, v_T, k_d, v_2, km, vm, probs2, probs_t2, bias2) = arena(
            ("gates", [P, 24, S], F32), ("gy", [P, DC, S], F32), ("XR", [P, DC, S + 4], F32), ("XC", [P, DC, S], F32),
            ("R", [P, DC, S], F32), ("GI", [P, DC, S], F32), ("v_T", [P, S], F32), ("k_d", [P, 2, S], F32),
            ("v_2", [P, 2, P], F32), ("km", [P, MH, S], F32), ("vm", [P, 2, 512], F32), ("probs2", [P, 2, S], F32),
            ("probs_t2", [P, 2, 2, S], F32), ("bias2", [P, 2, 2 * S], F32))
        tabs = rows[:, 0:3 * 2 * S].rearrange("p (t m n) -> p t m n", t=3, m=2)
        ahead, behind, since = tabs[:, 0], tabs[:, 1], tabs[:, 2]
        q_2 = rows[:, 0:D].rearrange("p (c t) -> p c t", c=4)
        cq_2 = rows[:, D:2 * D].rearrange("p (c t) -> p c t", c=4)
        z_hi = h_hi[:].rearrange("p c (u t) -> p (c u) t", u=2)
        z_lo = h_lo[:].rearrange("p c (u t) -> p (c u) t", u=2)

        acc = st.enter_context(nc.psum_tensor("acc", [P, 2, 2, 512], F32))
        wk = st.enter_context(nc.psum_tensor("wk", [P, 4, 512], F32))

        load = [sem(f"load{k}") for k in range(SLOTS)]
        hi_done = sem("hi_done")
        lo_done = sem("lo_done")
        units_used = sem("units_used")
        acc_free = sem("acc_free")
        x_done = sem("x_done")
        in_x, in_c, in_m = sem("in_x"), sem("in_c"), sem("in_m")
        in_prm0, in_prm, in_const = sem("in_prm0"), sem("in_prm"), sem("in_const")
        in_attn, in_tabs, in_rope = sem("in_attn"), sem("in_tabs"), sem("in_rope")
        setup = sem("setup")
        prm_t, prm_ok = sem("prm_t"), sem("prm_ok")
        turned = sem("turned")
        c_ok, c_hi_ok, c_lo_ok = sem("c_ok"), sem("c_hi_ok"), sem("c_lo_ok")
        soft_a, soft_v = sem("soft_a"), sem("soft_v")
        ada_sum, mod_ok, gain_ok = sem("ada_sum"), sem("mod_ok"), sem("gain_ok")
        sq_ok = sem("sq_ok")
        ss_ok = sem("ss_ok")
        std_ok, rstd_ok = sem("std_ok"), sem("rstd_ok")
        nf_ok, nh_ok, h_ok = sem("nf_ok"), sem("nh_ok"), sem("h_ok")
        hsq, hss, hstd, hrec, hn, hperm, hrot, hqk, kd_ok = [sem(k) for k in (
            "hsq", "hss", "hstd", "hrec", "hn", "hperm", "hrot", "hqk", "kd_ok")]
        s_ok, m_raw, m_ok, p_ok, den_ok, rec_ok, pn_ok, t_ok, pt_ok = [sem(k) for k in (
            "s_ok", "m_raw", "m_ok", "p_ok", "den_ok", "rec_ok", "pn_ok", "t_ok", "pt_ok")]
        o_ok, o_hi_ok, o_done = sem("o_ok"), sem("o_hi_ok"), sem("o_done")
        hid_hi_ok, hid_ok = sem("hid_hi_ok"), sem("hid_ok")
        swp_ok, rot_ok, rope_ok = sem("swp_ok"), sem("rot_ok"), sem("rope_ok")
        dx_in, dx_e, dc_e, d_ok, rs_ok, rp_ok, ro_ok = [sem(k) for k in ("dx_in", "dx_e", "dc_e", "d_ok", "rs_ok", "rp_ok", "ro_ok")]
        dx_a, bn_ok, mv_ok, gs_ok, gr_ok, y_ok, yt_ok, z_ok, zh_ok, z_done = [sem(k) for k in (
            "dx_a", "bn_ok", "mv_ok", "gs_ok", "gr_ok", "y_ok", "yt_ok", "z_ok", "zh_ok", "z_done")]
        cur_ok, conv_ok, xch_ok, xc_ok, zero_ok = [sem(k) for k in ("cur_ok", "conv_ok", "xch_ok", "xc_ok", "zero_ok")]
        e2_ok, cl_ok, mu_ok, b_ok, scan_ok, lru_ok, lruh_ok, lru_done = [sem(k) for k in (
            "e2_ok", "cl_ok", "mu_ok", "b_ok", "scan_ok", "lru_ok", "lruh_ok", "lru_done")]
        vt_ok, v2_ok, bias_ok = sem("vt_ok"), sem("v2_ok"), sem("bias_ok")
        sum2_ok, mg_ok, mgh_ok, mg_done = [sem(k) for k in ("sum2_ok", "mg_ok", "mgh_ok", "mg_done")]
        clear_ok, soft_ok, pad_ok, z_part = [sem(k) for k in ("clear_ok", "soft_ok", "pad_ok", "z_part")]
        fin_t, fin_ok, stored = sem("fin_t"), sem("fin_ok"), sem("stored")

        def const(name):
            o, n = const_at[name]
            return a["shape_constants"][:, o:o + n]

        def chunks(w, k0, nk):
            return w[k0 * P:(k0 + nk) * P, :].rearrange("(k p) n -> p k n", p=P)

        def groups_first():
            gs = []
            for h in range(HEADS):
                for ctx in range(2):
                    half = slice(64 * (h % 2), 64 * (h % 2) + 64)
                    keys = slice(S, 2 * S) if ctx else slice(0, 2 * S)
                    tiles = range(2, 4) if ctx else range(4)
                    gs.append(dict(
                        q=[qk[half, h // 2, ctx * S + r * P:ctx * S + (r + 1) * P] for r in range(2)],
                        k=k_dup[half, h // GROUP, keys], nk=keys.stop - keys.start,
                        mask=[window[:, r, keys] for r in range(2)], sink=sinks[:, h:h + 1], scale=HD ** -0.5,
                        v=[v_tok[:, t, 64 * (h // GROUP):64 * (h // GROUP) + 64] for t in tiles],
                        out=wk[half, 3, ctx * S:(ctx + 1) * S], pair=h // 2, last=(h % 2 and ctx),
                        probs=probs, probs_t=probs_t, acc=wk[:, 3, 0:2 * S],
                        hi=h_hi[:, h // 2, :], lo=h_lo[:, h // 2, :]))
            return gs

        def groups_window():
            gs = []
            for h in range(WH):
                half = slice(64 * (h % 2), 64 * (h % 2) + 64)
                gs.append(dict(
                    q=[q_2[half, h // 2, r * P:(r + 1) * P] for r in range(2)], k=k_d[half, h // 4, :], nk=S,
                    mask=[bias2[:, h % 2, r * S:(r + 1) * S] for r in range(2)], bias=True, sink=sink_l[:, h:h + 1],
                    scale=HD ** -0.5, v=[v_2[:, t, 64 * (h // 4):64 * (h // 4) + 64] for t in range(2)],
                    out=wk[half, 3, 0:S], pair=h // 2, last=h % 2, probs=probs2, probs_t=probs_t2,
                    acc=wk[:, 3, 0:S], hi=h_hi[:, h // 2, 0:S], lo=h_lo[:, h // 2, 0:S]))
            return gs

        def groups_memory():
            gs = []
            for h in range(MH):
                gs.append(dict(
                    q=[cq_2[:, h, r * P:(r + 1) * P] for r in range(2)], k=km[:, h, :], nk=S, mask=[nomask[:, :]] * 2,
                    sink=None, scale=P ** -0.5, v=[vm[:, t, P * h:P * h + P] for t in range(2)],
                    out=wk[:, 3, 0:S], pair=h, last=True, probs=probs2, probs_t=probs_t2, acc=wk[:, 3, 0:S],
                    hi=h_hi[:, 4 + h, 0:S], lo=h_lo[:, 4 + h, 0:S]))
            return gs

        def attn_base(which, l):
            per_i, per_p = ITEMS_WIN + ITEMS_MEM, PAIRS_WIN + PAIRS_MEM
            if which == "first":
                return 0, 0
            if which == "window":
                return ITEMS0 + l * per_i, PAIRS0 + l * per_p
            return ITEMS0 + ITEMS_WIN + l * per_i, PAIRS0 + PAIRS_WIN + l * per_p

        block = st.enter_context(nc.Block())

        @block.sync
        def _(sp):
            def stream(name, src, l=None):
                job = J[name]

                def one(it):
                    for p in range(job.body):
                        sp.wait_ge(lo_done, job.unit(l, it, p) + 1)
                        s = src(l, it, p)
                        slot = raw[:, p % SLOTS]
                        dst = slot[:, 0:s.shape[1], :] if s.shape[2] == COLS else \
                            slot[:, 0:2, :].rearrange("p k n -> p (k n)").rearrange("p (c j) -> p c j", j=64)
                        sp.dma_start(dst, s).then_inc(load[p % SLOTS], 16)

                if job.iters == 1:
                    one(0)
                else:
                    with sp.Fori(0, job.iters) as it:
                        one(it)

            def plain(w, k_chunks, col0=0, n=None):
                per = -(-k_chunks // KCH)
                n = n or w.shape[-1]

                def src(l, it, p):
                    m = w if l is None else w[l]
                    b, u = divmod(p, per)
                    blocks = 2
                    while per * blocks % SLOTS:
                        blocks += 2
                    k0 = u * KCH
                    view = chunks(m, k0, min(KCH, k_chunks - k0))[:, :, col0:col0 + n]
                    wide = view[:, :, bass.ts(it, blocks * COLS)]
                    return wide[:, :, b * COLS:(b + 1) * COLS]
                return src

            def gate_up(gate, up):
                def src(l, it, p):
                    b, u = divmod(p, 2)
                    m = (gate, up)[b] if l is None else (gate, up)[b][l]
                    return chunks(m, u * KCH, KCH)[:, :, bass.ts(it, COLS)]
                return src

            sp.dma_start(prm_rows[0:96, 0, :], a["ada_b"].rearrange("l (r f) -> (l r) f", f=P)).then_inc(in_prm0, 16)
            sp.dma_start(prm_rows[96:104, 0, :], a["c"].rearrange("l (r f) -> (l r) f", f=P)).then_inc(in_prm0, 16)
            sp.dma_start(prm_rows[104:112, 0, :], a["c_ctx"].rearrange("(r f) -> r f", f=P)).then_inc(in_prm0, 16)
            sp.dma_start(prm_rows[112:128, 0, :], a["norm1_g"].rearrange("l (r f) -> (l r) f", f=P)).then_inc(in_prm0, 16)
            stream("ada0", plain(a["ada_w"][0], DC))
            wqkv = a["attn_w_qkv"][0]
            stream("q0", plain(wqkv, DC, 0, D))
            stream("kv0", plain(wqkv, DC, D, 512))
            stream("wo0", plain(a["attn_w_o"][0], DC))
            stream("gu0", gate_up(a["ffn_w_in"][0][:, 0:FF], a["ffn_w_in"][0][:, FF:2 * FF]))
            stream("dn0", plain(a["ffn_w_out"][0], FC))
            stream("ada1", plain(a["ada_w"][1], DC))
            wr = a["ret_w_qkvg"][0]
            stream("rq", plain(wr, DC, 0, D))
            stream("rk", plain(wr, DC, D, D))
            stream("rv", plain(wr, DC, 2 * D, 2 * D))
            stream("rg", plain(wr, DC, 4 * D, 2 * D))
            stream("rwo", plain(a["ret_w_o"][0], 16))
            stream("gu1", gate_up(a["ffn_w_in"][1][:, 0:FF], a["ffn_w_in"][1][:, FF:2 * FF]))
            stream("dn1", plain(a["ffn_w_out"][1], FC))
            with sp.Fori(0, LAYERS2) as l:
                stream("gua", gate_up(a["ffn1_w_gate_2"], a["ffn1_w_up_2"]), l)
                stream("dna", plain(a["ffn1_w_down_2"], FC), l)
                stream("memk", plain(a["w_mem_kv_2"], DC, 0, 512), l)
                stream("memv", plain(a["w_mem_kv_2"], DC, 512, 512), l)
                w_in = a["w_in_2"]
                stream("xr", plain(w_in, DC, 768, D), l)
                stream("yr", plain(w_in, DC, 768 + D, D), l)
                stream("gates", plain(w_in, DC, 1280 + 2 * D, 3 * D), l)

                def kvlru(l, it, p):
                    if p < 2:
                        return chunks(w_in[l], p * KCH, KCH)[:, :, 512:768]
                    return a[("lru_wa_2", "lru_wx_2")[p - 2]][l].rearrange("(c two) i j -> (two i) c j", two=2)
                stream("kvlru", kvlru, l)

                def q_unit(l, it, p):
                    rows_l = w_in.rearrange("l k n -> (l k) n")[bass.ds(l * D + p % 2 * KCH * P, KCH * P), :]
                    return chunks(rows_l, 0, KCH)[:, :, p // 2 * COLS:(p // 2 + 1) * COLS]
                stream("q", q_unit, l)
                stream("cq", plain(w_in, DC, 768 + 2 * D, 512), l)
                stream("attn_out", plain(a["w_attn_out_2"], 4), l)
                stream("lru_out", plain(a["w_lru_out_2"], DC), l)
                stream("mem_out", plain(a["w_mem_out_2"], 4), l)
                stream("w_out", plain(a["w_out_2"], DC), l)
                stream("gub", gate_up(a["ffn2_w_gate_2"], a["ffn2_w_up_2"]), l)
                stream("dnb", plain(a["ffn2_w_down_2"], FC), l)
            for r in range(2):
                sp.wait_ge(fin_ok, 2 * (r + 1))
                sp.dma_start(out[0, r * P:(r + 1) * P, :], rows[:, r * D:(r + 1) * D]).then_inc(stored, 16)
            sp.wait_ge(stored, 32)

        @block.gpsimd
        def _(pool):
            def tokens(dst, src, s):
                for r in range(2):
                    pool.dma_start(dst[:, r * D:(r + 1) * D], src[0, r * P:(r + 1) * P, :]).then_inc(s, 16)

            for name, t in (("ident", ident), ("ones", ones), ("alibi", alibi), ("sel", sel), ("slopes", slopes)):
                pool.dma_start(t[:, :], const(name)).then_inc(in_const, 16)
            tokens(rows, a["x"], in_x)
            tokens(rows_c, a["ctx"], in_c)
            for l in range(LAYERS2):
                at = 0
                for name, n in (("gate_bias_2", 24), ("conv_w_2", 32), ("ffn1_norm_2", 8), ("mix_norm_2", 8), ("conv_b_2", 8),
                                ("lru_ba_2", 8), ("lru_bx_2", 8), ("lru_lambda_2", 8), ("mem_norm_2", 8), ("ffn2_norm_2", 8)):
                    src = a[name][l].rearrange("w (r f) -> (w r) f", f=P) if name == "conv_w_2" else \
                        a[name][l].rearrange("(r f) -> r f", f=P)
                    pool.dma_start(prm_rows[at:at + n, 1 + l, :], src).then_inc(in_prm, 16)
                    at += n
            pool.dma_start(prm_rows[NORM2:NORM2 + 16, 3, :], a["norm2_g"].rearrange("l (r f) -> (l r) f", f=P)).then_inc(in_prm, 16)
            pool.dma_start(prm_rows[FINAL_N:FINAL_N + 8, 3, :], a["final_norm_2"].rearrange("(r f) -> r f", f=P)).then_inc(in_prm, 16)
            pool.dma_start(prm_rows[GN_G:GN_G + 16, 3, :], a["ret_gn_g"].rearrange("l (r f) -> (l r) f", f=P)).then_inc(in_prm, 16)
            for name, at in (("attn_q_norm", Q_N), ("attn_k_norm", K_N)):
                for half in range(2):
                    pool.dma_start(prm_rows[at:at + 1, 3, half * HD:(half + 1) * HD], a[name]).then_inc(in_prm, 16)
            pool.dma_start(soft_in[:, 0:8], a["ret_decay_logit"].rearrange("o d h -> o (d h)").broadcast_to((P, 8))).then_inc(in_prm, 16)
            pool.dma_start(sinks[:, 0:16], a["attn_sink"].broadcast_to((P, 16))).then_inc(in_prm, 16)
            pool.dma_start(sinks[:, 16:32], a["attn_sinks_2"].rearrange("l (o h) -> o (l h)", o=1).broadcast_to((P, 16))).then_inc(in_prm, 16)
            for name, t in (("headones", headones), ("partner", partner), ("cos_a", cos_a), ("sin_a", sin_a)):
                pool.dma_start(t[:, :], const(name)).then_inc(in_attn, 16)
            pool.dma_start(window[:].rearrange("p r k -> p (r k)"), const("window")).then_inc(in_attn, 16)
            pool.wait_ge(x_done, X_START)
            for n, name in enumerate(("ahead", "behind", "since")):
                pool.dma_start(rows[:, n * 512:(n + 1) * 512], const(name)).then_inc(in_tabs, 16)
            pool.wait_ge(acc_free, J["dn0"].done())
            for name, t in (("cos_r", cos_r), ("sin_r", sin_r)):
                pool.dma_start(t[:].rearrange("p c t -> p (c t)"), const(name)).then_inc(in_rope, 16)
            pool.wait_ge(d_ok, RH)
            tokens(rows, a["mem_2"], in_m)
            with pool.Fori(0, LAYERS2) as l:
                for h in range(WH):
                    first, _ = attn_base("window", l)
                    if h < 2:
                        pool.wait_ge(acc_free, J["memv"].done(l))
                    else:
                        pool.wait_ge(m_raw, first + 2 * (h - 2) + 2)
                    pool.wait_ge(in_const, 16 * 5)
                    pool.tensor_tensor(bias2[:, h % 2, :], alibi[:, :], slopes[:, h:h + 1].broadcast_to((P, 2 * S)), ALU.mult)\
                        .then_inc(bias_ok, 1)

        @block.tensor
        def _(pe):
            def unit_ready(job, l, it, p):
                pe.wait_ge(lo_done, job.unit(l, it, p) + SLOTS + 1)

            def slot_free(job, l, it, b):
                pe.wait_ge(acc_free, job.block(l, it, b) + 1)

            def product(name, l=None, hi=h_hi, lo=h_lo, tok=slice(0, S), rows_of=None, needs=None):
                job = J[name]
                per = job.body // job.per

                def one(it):
                    for p in range(job.body):
                        b, u = divmod(p, per)
                        if u == 0:
                            slot_free(job, l, it, b)
                        if needs and needs(u):
                            pe.wait_ge(*needs(u))
                        unit_ready(job, l, it, p)
                        nk, s, last = job.unit_chunks[p], p % SLOTS, u == per - 1
                        tokens_major = rows_of if not callable(rows_of) else rows_of(b)
                        if tokens_major:
                            for n, r in enumerate(tokens_major):
                                packed = len(tokens_major) > 2
                                o = acc[:, b % 2, n // 2, (n % 2) * S:(n % 2) * S + S] if packed else acc[:, b % 2, n, 0:S]
                                for k in range(nk):
                                    x = slice(r * P, (r + 1) * P)
                                    kk = u * KCH + k
                                    for i, (xs, ws) in enumerate(((hi, w_hi), (hi, w_lo), (lo, w_hi))):
                                        mm = pe.matmul(o, xs[:, kk, x], ws[:, s, k, :],
                                                       start=(u == 0 and k == 0 and i == 0 and not (packed and n % 2)),
                                                       stop=(last and k == nk - 1 and i == 2), skip_group_check=packed)
                        else:
                            t = tok if not callable(tok) else tok(b)
                            for cb in range(2):
                                o = acc[:, b % 2, cb, 0:t.stop - t.start]
                                for k in range(nk):
                                    kk = u * KCH + k
                                    c = slice(cb * P, (cb + 1) * P)
                                    for i, (ws, xs) in enumerate(((w_hi, hi), (w_hi, lo), (w_lo, hi))):
                                        mm = pe.matmul(o, ws[:, s, k, c], xs[:, kk, t],
                                                       start=(u == 0 and k == 0 and i == 0),
                                                       stop=(last and k == nk - 1 and i == 2))
                        mm.then_inc(units_used, 1)

                if job.iters == 1:
                    one(0)
                else:
                    with pe.Fori(0, job.iters) as it:
                        one(it)

            def modulation(name, i):
                job = J[name]
                pe.wait_ge(c_lo_ok, 1)
                with pe.Fori(0, job.iters) as it:
                    for p in range(job.body):
                        b, u = divmod(p, 2)
                        if u == 0:
                            slot_free(job, None, it, b)
                        unit_ready(job, None, it, p)
                        for k in range(KCH):
                            four = c_parts[:, u * KCH + k, :]
                            for i2, ws in enumerate((w_hi, w_lo)):
                                mm = pe.matmul(acc[0:4, b % 2, 0, 0:S], four, ws[:, p % SLOTS, k, :],
                                               start=(u == 0 and k == 0 and i2 == 0), stop=(u == 1 and k == KCH - 1 and i2 == 1))
                        mm.then_inc(units_used, 1)
                pe.wait_ge(acc_free, job.done())
                for c in range(48):
                    mm = pe.matmul(wk[:, 2, 2 * c:2 * c + 2], ada_s[0:4, c * P:(c + 1) * P], sel[0:4, :], start=True, stop=True)
                mm.then_inc(ada_sum, 1)

            def norm(n, half):
                pe.wait_ge(sq_ok, n + 1)
                for c in range(DC):
                    mm = pe.matmul(wk[:, 3, 0:S], ones[:, :], nf[:, c, :], start=(c == 0), stop=(c == DC - 1))
                mm.then_inc(ss_ok, 1)

            def turn_in(src, s, bank0):
                pe.wait_ge(s, 32)
                for g in range(4):
                    dst = (wk[:, g] if bank0 == 0 else acc[:, g // 2, g % 2]).rearrange("p (c t) -> p c t", c=2)
                    for c in range(2):
                        for r in range(2):
                            f = r * D + (2 * g + c) * P
                            mm = pe.transpose(dst[:, c, r * P:(r + 1) * P], src[:, f:f + P], ident[:, :])
                    mm.then_inc(turned, 1)

            def attention(which, groups, l=None):
                first, pair0 = attn_base(which, l)
                items = [(g, r) for g in range(len(groups)) for r in range(2)]
                behind_by = 2
                for i in range(len(items) + behind_by):
                    if i < len(items):
                        g, r = items[i]
                        G = groups[g]
                        if i >= 2 or which != "first":
                            pe.wait_ge(m_raw, first + i - 1)
                        pe.matmul(wk[:, i % 2, 0:G["nk"]], G["q"][r], G["k"], start=True, stop=True).then_inc(s_ok, 1)
                    j = i - behind_by
                    if j >= 0:
                        g, r = items[j]
                        G = groups[g]
                        tiles = G["nk"] // P
                        pe.wait_ge(pn_ok, first + j + 1)
                        if j or which != "first":
                            pe.wait_ge(pt_ok, first + j)
                        for t in range(tiles):
                            mm = pe.transpose(wk[:, 2, t * P:(t + 1) * P], G["probs"][:, j % 2, t * P:(t + 1) * P], ident[:, :])
                        mm.then_inc(t_ok, 1)
                        if r == 1:
                            pe.wait_ge(pt_ok, first + j + 1)
                            if which != "first":
                                pe.wait_ge(o_done, pair0 + G["pair"])
                            elif G["pair"]:
                                pe.wait_ge(o_done, G["pair"])
                            for t in range(tiles):
                                mm = pe.matmul(G["out"], G["v"][t], G["probs_t"][:, g % 2, t, :], start=(t == 0),
                                               stop=(t == tiles - 1), skip_group_check=True)
                            mm.then_inc(o_ok, 1)

            pe.wait_ge(in_const, 16 * 5)
            pe.wait_ge(in_prm0, 64)
            pe.wait_ge(in_prm, 16 * PRM_DMAS)
            pe.wait_ge(setup, 2)
            for t, n in enumerate((P, CUR, CUR, PRM3)):
                mm = pe.transpose(wk[:, 3, t * P:t * P + n], prm_rows[0:n, t, :], ident[0:n, 0:n])
            mm.then_inc(prm_t, 1)
            turn_in(rows, in_x, 1)
            pe.wait_ge(x_done, 4)
            turn_in(rows_c, in_c, 1)
            pe.wait_ge(x_done, X_START)
            modulation("ada0", 0)
            norm(0, 0)
            norm(1, 1)
            both = slice(0, 2 * S)
            product("q0", tok=both, needs=lambda u: (h_ok, 16))
            product("kv0", tok=both, rows_of=lambda b: range(4) if b else None)
            pe.wait_ge(in_attn, 80)
            for c in range(10):
                pe.wait_ge(hsq, c + 1)
                if c >= 2:
                    pe.wait_ge(hstd, c - 1)
                pe.matmul(wk[:, c % 2, :], headones[:, :], sq_b[:, c % 2, :], start=True, stop=True).then_inc(hss, 1)
                if c >= 1:
                    pe.wait_ge(hn, c)
                    if c >= 3:
                        pe.wait_ge(hrot, c - 2)
                    pe.matmul(wk[:, 2 + (c - 1) % 2, 0:S], partner[:, :], qk[:, c - 1, 0:S], start=True, stop=True).then_inc(hperm, 1)
            pe.wait_ge(hn, 10)
            pe.wait_ge(hrot, 8)
            pe.matmul(wk[:, 3, 0:S], partner[:, :], qk[:, 9, 0:S], start=True, stop=True).then_inc(hperm, 1)
            pe.wait_ge(hqk, 10)
            pe.wait_ge(kd_ok, 8)
            pe.wait_ge(acc_free, J["kv0"].done())
            attention("first", groups_first())
            product("wo0", tok=both, needs=lambda u: (o_done, PAIRS0))
            norm(2, 0)
            norm(3, 1)
            product("gu0", tok=both, needs=lambda u: (h_ok, 8 * 4))
            product("dn0", hi=hid_hi, lo=hid_lo, tok=both, needs=lambda u: (hid_ok, 11))
            modulation("ada1", 1)
            norm(4, 0)
            norm(5, 1)
            product("rq", needs=lambda u: (h_ok, 8 * 6))
            product("rk", tok=both)
            product("rv", rows_of=range(4))
            product("rg")

            def scores(h):
                pe.wait_ge(rope_ok, 8)
                for kt in range(4):
                    if h and kt % 2 == 0:
                        pe.wait_ge(rp_ok, 2 * (h - 1) + kt // 2 + 1)
                    for d in range(2):
                        mm = pe.matmul(wk[:, kt // 2, (kt % 2) * S:(kt % 2) * S + S], r_k[:, 2 * h + d, kt * P:(kt + 1) * P],
                                       r_q[:, 2 * h + d, :], start=(d == 0), stop=(d == 1))
                    if kt % 2:
                        mm.then_inc(rs_ok, 1)

            def values(h):
                pe.wait_ge(acc_free, J["rv"].done())
                pe.wait_ge(rp_ok, 2 * h + 2)
                for r in range(2):
                    if h:
                        pe.wait_ge(y_ok, 2 * (h - 1) + r + 1)
                    for kt in range(4):
                        mm = pe.matmul(wk[:, 2 + r, :], r_p[:, kt, r * P:(r + 1) * P], r_v[:, kt, RV * h:RV * (h + 1)],
                                       start=(kt == 0), stop=(kt == 3))
                    mm.then_inc(ro_ok, 1)

            def turn_y(h):
                if h:
                    pe.wait_ge(z_ok, h)
                else:
                    pe.wait_ge(acc_free, J["rg"].block(None, J["rg"].iters - 1, 1) + 3)
                for r in range(2):
                    pe.wait_ge(y_ok, 2 * h + r + 1)
                    for c in range(4):
                        o = acc[:, 0, c // 2, (c % 2) * S + r * P:(c % 2) * S + (r + 1) * P]
                        mm = pe.transpose(o, r_y[:, r, c * P:(c + 1) * P], ident[:, :])
                mm.then_inc(yt_ok, 1)

            for h in range(RH):
                scores(h)
                if h:
                    turn_y(h - 1)
                values(h)
            turn_y(RH - 1)
            product("rwo", hi=z_hi, lo=z_lo, needs=lambda u: (z_done, RH))
            norm(6, 0)
            product("gu1", needs=lambda u: (h_ok, 8 * 7))
            product("dn1", hi=hid_hi, lo=hid_lo, needs=lambda u: (hid_ok, 22))
            pe.wait_ge(acc_free, J["dn1"].done())
            turn_in(rows, in_m, 1)
            pe.wait_ge(x_done, X_MEM)

            mem = slice(S, 2 * S)
            with pe.Fori(0, LAYERS2) as l:
                n0 = NORMS1 + l * 4
                norm(n0, 0)
                product("gua", l, needs=lambda u: (h_ok, 8 * (NORMS1 + 1) + l * 32))
                product("dna", l, hi=hid_hi, lo=hid_lo, needs=lambda u: (hid_ok, 33 + l * 22))
                norm(n0 + 1, 0)
                norm(n0 + 2, 1)
                product("memk", l, tok=mem, needs=lambda u: (h_ok, 8 * (NORMS1 + 3) + l * 32))
                product("memv", l, rows_of=range(2, 4))
                product("xr", l)
                product("yr", l)
                product("gates", l)
                job = J["kvlru"]
                slot_free(job, l, 0, 0)
                slot_free(job, l, 0, 1)
                for p in range(2):
                    unit_ready(job, l, 0, p)
                    for cb in range(2):
                        for k in range(KCH):
                            for i, (ws, xs) in enumerate(((w_hi, h_hi), (w_hi, h_lo), (w_lo, h_hi))):
                                mm = pe.matmul(acc[:, cb, 0, 0:S], ws[:, p, k, cb * P:(cb + 1) * P], xs[:, p * KCH + k, 0:S],
                                               start=(p == 0 and k == 0 and i == 0), stop=(p == 1 and k == KCH - 1 and i == 2))
                    mm.then_inc(units_used, 1)
                pe.wait_ge(xc_ok, 1 + l)
                for p in range(2, 4):
                    unit_ready(job, l, 0, p)
                    wh, wl = [w[:, p].rearrange("p k n -> p (k n)") for w in (w_hi, w_lo)]
                    for c in range(DC):
                        b = 2 * (p - 1) + c // 4
                        if c % 4 == 0:
                            slot_free(job, l, 0, b)
                        o = acc[:, b % 2, (c % 4) // 2, (c % 2) * S:(c % 2) * S + S]
                        for i, (w, x) in enumerate(((wh, h_hi), (wh, h_lo), (wl, h_hi))):
                            mm = pe.matmul(o, w[:, c * P:(c + 1) * P], x[:, c, mem], start=(i == 0), stop=(i == 2))
                    mm.then_inc(units_used, 1)
                product("q", l)
                product("cq", l)
                pe.wait_ge(acc_free, J["cq"].done(l))
                for r in range(2):
                    mm = pe.transpose(wk[:, 3, r * P:(r + 1) * P], v_T[:, r * P:(r + 1) * P], ident[:, :])
                mm.then_inc(vt_ok, 1)
                pe.wait_ge(v2_ok, 1 + l)
                attention("window", groups_window(), l)
                attention("memory", groups_memory(), l)
                _, pair0 = attn_base("window", l)
                product("attn_out", l, needs=lambda u: (o_done, pair0 + PAIRS_WIN))
                product("lru_out", l, tok=mem, needs=lambda u: (lru_done, 1 + l))
                product("mem_out", l, hi=h_hi[:, 4:8, :], lo=h_lo[:, 4:8, :],
                        needs=lambda u: (o_done, pair0 + PAIRS_WIN + PAIRS_MEM))
                product("w_out", l, tok=mem, needs=lambda u: (mg_done, 4 + l * 4))
                norm(n0 + 3, 0)
                product("gub", l, needs=lambda u: (h_ok, 8 * (NORMS1 + 4) + l * 32))
                product("dnb", l, hi=hid_hi, lo=hid_lo, needs=lambda u: (hid_ok, 44 + l * 22))
            norm(NORM_LAST, 0)
            pe.wait_ge(nf_ok, 8 * (NORM_LAST + 1))
            for r in range(2):
                for c in range(DC):
                    g = 2 * r + c // 4
                    mm = pe.transpose(wk[:, g, (c % 4) * P:(c % 4 + 1) * P] if g < 3 else acc[:, 0, 0, (c % 4) * P:(c % 4 + 1) * P],
                                      nf[:, c, r * P:(r + 1) * P], ident[:, :])
                    if c % 4 == 3:
                        mm.then_inc(fin_t, 1)

        @block.scalar
        def _(act):
            def split(job, l, it, p):
                s, nk = p % SLOTS, job.unit_chunks[p]
                act.wait_ge(load[s], job.loaded(l, it, p))
                act.wait_ge(units_used, job.unit(l, it, p) + 1)
                act.copy(w_hi[:, s, 0:nk, :], raw[:, s, 0:nk, :]).then_inc(hi_done, 1)

            def split_diag(job, l, p):
                act.wait_ge(load[p], job.loaded(l, 0, p))
                act.wait_ge(zero_ok, 1 + (p - 2) + l * 2)
                src = raw[:, p, 0:2, :].rearrange("p k n -> p (k n)").rearrange("p (c j) -> p c j", j=64)
                dst = w_hi[:, p].rearrange("p k n -> p (k n)").rearrange("p (c j) -> p c j", j=P)
                act.copy(dst[0:64, :, 0:64], src[0:64])
                act.copy(dst[64:128, :, 64:128], src[64:128]).then_inc(hi_done, 1)

            def block_done(job, l, it, b):
                act.wait_ge(units_used, job.unit(l, it, job.ends[b]) + SLOTS + 1)

            def ending(job, e):
                return [b for b in range(job.per) if job.ends[b] == e]

            def step(name, evac, l, it, p):
                job = J[name]
                if name == "kvlru" and p >= 2:
                    split_diag(job, l, p)
                else:
                    split(job, l, it, p)

            def evacuate(name, evac, l, it, e):
                for b in ending(J[name], e):
                    if evac:
                        block_done(J[name], l, it, b)
                        evac(l, it, b)

            def head(name, l=None, prev=None, prev_evac=None):
                for p in range(LAG):
                    step(name, None, l, 0, p)
                    if prev:
                        evacuate(prev, prev_evac, l, J[prev].iters - 1, J[prev].body + p - LAG)

            def rest(name, evac, l=None):
                job = J[name]
                for p in range(LAG, job.body):
                    step(name, evac, l, 0, p)
                    evacuate(name, evac, l, 0, p - LAG)
                if job.iters > 1:
                    with act.Fori(1, job.iters) as it:
                        for p in range(job.body):
                            step(name, evac, l, it, p)
                            if p < LAG:
                                evacuate(name, evac, l, it - 1, job.body + p - LAG)
                            else:
                                evacuate(name, evac, l, it, p - LAG)

            def tail(prev, evac, l=None):
                for p in range(LAG):
                    evacuate(prev, evac, l, J[prev].iters - 1, J[prev].body + p - LAG)

            def norm(n, half, x_from, shift=None, split_out=True):
                t = slice(half * S, half * S + S)
                act.wait_ge(*x_from)
                if not (isinstance(n, int) and n == 0):
                    act.wait_ge(h_ok, 8 * n)
                act.activation(nf[:], xT[:, :, t], ACT.Square).then_inc(sq_ok, 1)
                act.wait_ge(ss_ok, n + 1)
                act.activation(std[:], wk[:, 3, 0:S], ACT.Sqrt, bias=eps[:, 0:1], scale=1.0 / D).then_inc(std_ok, 1)
                if split_out:
                    for c in range(DC):
                        act.wait_ge(nf_ok, n * 8 + c + 1)
                        if shift is not None:
                            act.activation(h_hi[:, c, t], nf[:, c, :], ACT.Identity, bias=mod[:, shift * 8 + c, half:half + 1])\
                                .then_inc(nh_ok, 1)
                        else:
                            act.copy(h_hi[:, c, t], nf[:, c, :]).then_inc(nh_ok, 1)

            def attention(which, groups, l=None):
                first, pair0 = attn_base(which, l)
                items = [(g, r) for g in range(len(groups)) for r in range(2)]
                for i in range(len(items) + 2):
                    if i < len(items):
                        g, r = items[i]
                        G = groups[g]
                        act.wait_ge(m_ok, first + i + 1)
                        pr = G["probs"][:, i % 2, 0:G["nk"]]
                        act.activation(pr, pr, ACT.Exp, bias=snm[:, i % 8:i % 8 + 1], accum_out=ssum[:, i % 8:i % 8 + 1])\
                            .then_inc(p_ok, 1)
                        if G["sink"] is not None:
                            act.activation(ses[:, i % 8:i % 8 + 1], G["sink"], ACT.Exp, bias=snm[:, i % 8:i % 8 + 1]).then_inc(p_ok, 1)
                        else:
                            act.activation(ses[:, i % 8:i % 8 + 1], nomask[:, 0:1], ACT.Copy).then_inc(p_ok, 1)
                    j = i - 2
                    if j >= 0:
                        g, r = items[j]
                        G = groups[g]
                        tiles = G["nk"] // P
                        act.wait_ge(t_ok, first + j + 1)
                        if g >= 2:
                            n = G_done(which, first, g - 2)
                            act.wait_ge(o_ok, n)
                        act.copy(G["probs_t"][:, g % 2, 0:tiles, r * P:(r + 1) * P],
                                 wk[:, 2, 0:tiles * P].rearrange("p (t q) -> p t q", q=P)).then_inc(pt_ok, 1)
                        if r == 1 and G["last"]:
                            act.wait_ge(o_ok, G_done(which, first, g))
                            act.copy(G["hi"], G["acc"]).then_inc(o_hi_ok, 1)

            def G_done(which, first, g):
                if which == "first":
                    return g + 1
                return ITEMS0 // 2 + g + 1 + (0 if which == "window" else ITEMS_WIN // 2) + first_l[0] * ((ITEMS_WIN + ITEMS_MEM) // 2)

            first_l = [0]

            def q0(l, it, b):
                act.copy(qk[:, bass.ts(it, 4), :][:, 2 * b:2 * b + 2, :], acc[:, b % 2]).then_inc(acc_free, 1)

            def kv0(l, it, b):
                if b == 0:
                    act.copy(qk[:, 8:10, :], acc[:, 0]).then_inc(acc_free, 1)
                else:
                    act.copy(v_tok[:].rearrange("p t n -> p (t n)"), acc[:, 1].rearrange("p a n -> p (a n)"))\
                        .then_inc(acc_free, 1)

            def gate_up(name, T, n0):
                def evac(l, it, b):
                    n = n0 + it + (l * 22 if l is not None else 0)
                    buf = act_buf[:, :, 0:T]
                    if b == 0:
                        if not (isinstance(n, int) and n == 0):
                            act.wait_ge(hid_ok, n)
                        act.activation(buf, acc[:, 0, :, 0:T], ACT.Silu).then_inc(acc_free, 1)
                    else:
                        act.wait_ge(acc_free, J[name].taken(l, it, 1))
                        act.copy(hid_hi[:, bass.ts(it, 2), 0:T], buf).then_inc(hid_hi_ok, 1)
                return evac

            def rope(n0, keys):
                def evac(l, it, b):
                    o = acc[:, b % 2]
                    n = n0 + 2 * it + b
                    if keys:
                        act.copy(r_k[:, bass.ts(it, 4), S:2 * S][:, 2 * b:2 * b + 2, :], o[:, :, S:2 * S])
                    if not (isinstance(n, int) and n == 0):
                        act.wait_ge(rope_ok, n)
                    act.copy(swp[0:64], o[64:128, :, 0:S])
                    act.copy(swp[64:128], o[0:64, :, 0:S]).then_inc(swp_ok, 1)
                return evac

            def rv(l, it, b):
                act.wait_ge(rope_ok, 8)
                act.copy(r_v[:, :, bass.ts(it, 2 * COLS)][:, :, b * COLS:(b + 1) * COLS],
                         acc[:, b % 2].rearrange("p a (r n) -> p (a r) n", r=2)).then_inc(acc_free, 1)

            def rg(l, it, b):
                act.activation(r_g[:, bass.ts(it, 4), :][:, 2 * b:2 * b + 2, :], acc[:, b % 2, :, 0:S], ACT.Silu)\
                    .then_inc(acc_free, 1)

            def memk(l, it, b):
                act.copy(km[:, 2 * b:2 * b + 2, :], acc[:, b, :, 0:S]).then_inc(acc_free, 1)

            def memv(l, it, b):
                act.copy(vm[:, :, b * COLS:(b + 1) * COLS], acc[:, b, :, 0:S]).then_inc(acc_free, 1)

            def xr(l, it, b):
                act.copy(XR[:, bass.ts(it, 4), 4:4 + S][:, 2 * b:2 * b + 2, :], acc[:, b, :, 0:S]).then_inc(acc_free, 1)

            def yr(l, it, b):
                act.activation(gy[:, bass.ts(it, 4), :][:, 2 * b:2 * b + 2, :], acc[:, b, :, 0:S], ACT.Gelu_apprx_tanh)\
                    .then_inc(acc_free, 1)

            def gates_e(l, it, b):
                for cb in range(2):
                    col = cur[:, bass.ts(it, 4)][:, 2 * b + cb:2 * b + cb + 1]
                    ins = act.activation(gates[:, bass.ts(it, 4), :][:, 2 * b + cb, :], acc[:, b, cb, 0:S], ACT.Sigmoid, bias=col)
                ins.then_inc(acc_free, 1)

            def kvlru(l, it, b):
                if b == 0:
                    for g in range(2):
                        for half in range(2):
                            ins = act.copy(k_d[64 * half:64 * half + 64, g, :], acc[64 * g:64 * g + 64, 0, 0, 0:S])
                    ins.then_inc(acc_free, 1)
                elif b == 1:
                    act.copy(v_T[:], acc[:, 1, 0, 0:S]).then_inc(acc_free, 1)
                else:
                    dst, bias = (R, BA) if b < 4 else (GI, BX)
                    for c in range(4):
                        cc = 4 * (b % 2) + c
                        ins = act.activation(dst[:, cc, :], acc[:, b % 2, c // 2, (c % 2) * S:(c % 2) * S + S], ACT.Sigmoid,
                                             bias=cur[:, bias + cc:bias + cc + 1])
                    ins.then_inc(acc_free, 1)

            def q_e(l, it, b):
                act.copy(q_2[:, 2 * b:2 * b + 2, :], acc[:, b, :, 0:S]).then_inc(acc_free, 1)

            def cq_e(l, it, b):
                act.copy(cq_2[:, 2 * b:2 * b + 2, :], acc[:, b, :, 0:S]).then_inc(acc_free, 1)

            def mem_out(l, it, b):
                act.wait_ge(mg_ok, 1 + b + l * 4)
                act.copy(h_hi[:, 2 * b:2 * b + 2, S:2 * S], gates[:, 2 * b:2 * b + 2, :]).then_inc(mgh_ok, 1)

            act.wait_ge(setup, 2)
            act.wait_ge(prm_ok, 3)
            act.activation(c_act[:], prm[:, 0, C_COL:C_COL + 16], ACT.Silu).then_inc(c_ok, 1)
            act.wait_ge(c_ok, 1)
            cc = c_act[:].rearrange("p (w k) -> p k w", w=2)
            act.copy(c_parts[:].rearrange("p k (w s) -> p k w s", s=2)[:, :, :, 0], cc).then_inc(c_hi_ok, 1)
            head("ada0")
            act.wait_ge(soft_v, 1)
            act.activation(soft_e[:], soft_t[:], ACT.Exp).then_inc(soft_a, 1)
            rest("ada0", None)
            head("q0", None, "ada0", None)
            norm(0, 0, (x_done, X_START), 0)
            norm(1, 1, (x_done, X_START), 0)
            rest("q0", q0)
            head("kv0", None, "q0", q0)
            rest("kv0", kv0)
            head("wo0", None, "kv0", kv0)
            for c in range(10):
                act.wait_ge(acc_free, J["kv0"].taken(None, 0, 0))
                if c >= 2:
                    act.wait_ge(hss, c - 1)
                act.activation(sq_b[:, c % 2, :], qk[:, c, :], ACT.Square).then_inc(hsq, 1)
                act.wait_ge(hss, c + 1)
                if c >= 2:
                    act.wait_ge(hn, c - 1)
                act.activation(sd_b[:, c % 2, :], wk[:, c % 2, :], ACT.Sqrt, bias=eps[:, 0:1], scale=1.0 / HD).then_inc(hstd, 1)
            for c in range(2):
                act.wait_ge(hqk, 9 + c)
                for g in range(2):
                    for half in range(2):
                        act.copy(k_dup[64 * half:64 * half + 64, 2 * c + g, :], qk[64 * g:64 * g + 64, 8 + c, :]).then_inc(kd_ok, 1)
            attention("first", groups_first())
            rest("wo0", None)
            head("gu0", None, "wo0", None)
            norm(2, 0, (acc_free, J["wo0"].done()), 3)
            norm(3, 1, (acc_free, J["wo0"].done()), 3)
            rest("gu0", gate_up("gu0", 2 * S, 0))
            head("dn0", None, "gu0", gate_up("gu0", 2 * S, 0))
            rest("dn0", None)
            head("ada1", None, "dn0", None)
            rest("ada1", None)
            head("rq", None, "ada1", None)
            norm(4, 0, (acc_free, J["dn0"].done()), 0)
            norm(5, 1, (acc_free, J["dn0"].done()), 0)
            rest("rq", rope(0, False))
            head("rk", None, "rq", rope(0, False))
            rest("rk", rope(4, True))
            head("rv", None, "rk", rope(4, True))
            rest("rv", rv)
            head("rg", None, "rv", rv)
            rest("rg", rg)
            head("rwo", None, "rg", rg)

            def decays(h):
                act.wait_ge(dx_in, h + 1)
                act.activation(r_d[:, 0:2, :], r_d[:, 0:2, :], ACT.Exp).then_inc(dx_e, 1)
                act.activation(r_d[:, 2:4, :], since, ACT.Exp, scale=decay[:, 0, h:h + 1]).then_inc(dc_e, 1)
                if h:
                    act.wait_ge(z_done, h)
                act.activation(act_buf[:, 0, :].rearrange("p (m n) -> p m n", m=2), since, ACT.Exp,
                               scale=decay[:, 1, 4 + h:5 + h], bias=decay[:, 2, 4 + h:5 + h]).then_inc(dc_e, 1)

            def gn(h):
                for r in range(2):
                    act.wait_ge(mv_ok, 2 * h + r + 1)
                    act.activation(gstd[:, r:r + 1], mv[:, r, 1:2], ACT.Sqrt, bias=eps[:, 0:1]).then_inc(gs_ok, 1)

            def z_high(h):
                act.wait_ge(z_ok, h + 1)
                act.copy(z_hi[:, 4 * h:4 * h + 4, :], act_buf[:].rearrange("p a (b t) -> p (a b) t", b=2)).then_inc(zh_ok, 1)

            act.wait_ge(in_tabs, 48)
            for h in range(RH):
                decays(h)
                gn(h)
                z_high(h)
            rest("rwo", None)
            head("gu1", None, "rwo", None)
            norm(6, 0, (acc_free, J["rwo"].done()), 3)
            rest("gu1", gate_up("gu1", S, 11))
            head("dn1", None, "gu1", gate_up("gu1", S, 11))
            rest("dn1", None)
            tail("dn1", None)

            with act.Fori(0, LAYERS2) as l:
                first_l[0] = l
                n0 = NORMS1 + l * 4
                head("gua", l)
                norm(n0, 0, (acc_free, J["gua"].taken(l, 0, 0) - 1))
                rest("gua", gate_up("gua", S, 22), l)
                head("dna", l, "gua", gate_up("gua", S, 22))
                rest("dna", None, l)
                head("memk", l, "dna", None)
                norm(n0 + 1, 0, (acc_free, J["dna"].done(l)))
                norm(n0 + 2, 1, (acc_free, J["dna"].done(l)))
                rest("memk", memk, l)
                head("memv", l, "memk", memk)
                rest("memv", memv, l)
                head("xr", l, "memv", memv)
                rest("xr", xr, l)
                head("yr", l, "xr", xr)
                rest("yr", yr, l)
                head("gates", l, "yr", yr)
                act.wait_ge(conv_ok, 32 + l * 32)
                act.copy(h_hi[:, :, S:2 * S], XC[:]).then_inc(xch_ok, 1)
                rest("gates", gates_e, l)
                head("kvlru", l, "gates", gates_e)
                rest("kvlru", kvlru, l)
                head("q", l, "kvlru", kvlru)
                rest("q", q_e, l)
                head("cq", l, "q", q_e)
                rest("cq", cq_e, l)
                head("attn_out", l, "cq", cq_e)
                for c in range(DC):
                    act.activation(XR[:, c, 0:S], R[:, c, :], ACT.Exp, scale=cur[:, CUR + 8 + c:CUR + 9 + c]).then_inc(e2_ok, 1)
                    act.activation(R[:, c, :], R[:, c, :], ACT.Exp, scale=cur[:, CUR + c:CUR + c + 1]).then_inc(e2_ok, 1)
                act.wait_ge(cl_ok, 1 + l)
                act.activation(XR[:, :, 0:S], XR[:, :, 0:S], ACT.Sqrt, scale=-1.0, bias=ones[:, 0:1]).then_inc(mu_ok, 1)
                act.wait_ge(lru_ok, 1 + l)
                act.copy(h_hi[:, :, S:2 * S], XC[:]).then_inc(lruh_ok, 1)
                attention("window", groups_window(), l)
                attention("memory", groups_memory(), l)
                rest("attn_out", None, l)
                head("lru_out", l, "attn_out", None)
                rest("lru_out", None, l)
                head("mem_out", l, "lru_out", None)
                rest("mem_out", mem_out, l)
                head("w_out", l, "mem_out", mem_out)
                rest("w_out", None, l)
                head("gub", l, "w_out", None)
                norm(n0 + 3, 0, (acc_free, J["w_out"].done(l)))
                rest("gub", gate_up("gub", S, 33), l)
                head("dnb", l, "gub", gate_up("gub", S, 33))
                rest("dnb", None, l)
                tail("dnb", None, l)
            norm(NORM_LAST, 0, (acc_free, J["dnb"].done(LAYERS2 - 1)), split_out=False)

        @block.vector
        def _(dve):
            def split(job, l, it, p):
                s, nk = p % SLOTS, job.unit_chunks[p]
                dve.wait_ge(hi_done, job.unit(l, it, p) + 1)
                dve.tensor_tensor(w_lo[:, s, 0:nk, :], raw[:, s, 0:nk, :], w_hi[:, s, 0:nk, :], ALU.subtract).then_inc(lo_done, 1)

            def split_diag(job, l, p):
                dve.wait_ge(units_used, job.unit(l, 0, p) + 1)
                dve.memset(w_hi[:, p].bitcast(F32), 0.0).then_inc(zero_ok, 1)
                dve.memset(w_lo[:, p].bitcast(F32), 0.0).then_inc(clear_ok, 1)
                src = raw[:, p, 0:2, :].rearrange("p k n -> p (k n)").rearrange("p (c j) -> p c j", j=64)
                hi, lo = [w[:, p].rearrange("p k n -> p (k n)").rearrange("p (c j) -> p c j", j=P) for w in (w_hi, w_lo)]
                dve.wait_ge(hi_done, job.unit(l, 0, p) + 1)
                dve.wait_ge(clear_ok, 1 + (p - 2) + l * 2)
                dve.tensor_tensor(lo[0:64, :, 0:64], src[0:64], hi[0:64, :, 0:64], ALU.subtract)
                dve.tensor_tensor(lo[64:128, :, 64:128], src[64:128], hi[64:128, :, 64:128], ALU.subtract).then_inc(lo_done, 1)

            def block_done(job, l, it, b):
                dve.wait_ge(units_used, job.unit(l, it, job.ends[b]) + SLOTS + 1)

            def ending(job, e):
                return [b for b in range(job.per) if job.ends[b] == e]

            def step(name, l, it, p):
                job = J[name]
                if name == "kvlru" and p >= 2:
                    split_diag(job, l, p)
                else:
                    split(job, l, it, p)

            def evacuate(name, evac, l, it, e):
                for b in ending(J[name], e):
                    if evac:
                        block_done(J[name], l, it, b)
                        evac(l, it, b)

            def head(name, l=None, prev=None, prev_evac=None):
                for p in range(LAG):
                    step(name, l, 0, p)
                    if prev:
                        evacuate(prev, prev_evac, l, J[prev].iters - 1, J[prev].body + p - LAG)

            def rest(name, evac, l=None):
                job = J[name]
                for p in range(LAG, job.body):
                    step(name, l, 0, p)
                    evacuate(name, evac, l, 0, p - LAG)
                if job.iters > 1:
                    with dve.Fori(1, job.iters) as it:
                        for p in range(job.body):
                            step(name, l, it, p)
                            if p < LAG:
                                evacuate(name, evac, l, it - 1, job.body + p - LAG)
                            else:
                                evacuate(name, evac, l, it, p - LAG)

            def tail(prev, evac, l=None):
                for p in range(LAG):
                    evacuate(prev, evac, l, J[prev].iters - 1, J[prev].body + p - LAG)

            def norm(n, half, gain_of, shift=None, split_out=True):
                t = slice(half * S, half * S + S)
                dve.wait_ge(std_ok, n + 1)
                dve.reciprocal(rstd[:], std[:]).then_inc(rstd_ok, 1)
                dve.wait_ge(rstd_ok, n + 1)

                def normed(c):
                    dve.scalar_tensor_tensor(nf[:, c, :], xT[:, c, t], gain_of(c), rstd[:], ALU.mult, ALU.mult).then_inc(nf_ok, 1)

                def low(c):
                    dve.wait_ge(nh_ok, n * 8 + c + 1)
                    if shift is not None:
                        dve.scalar_tensor_tensor(h_lo[:, c, t], nf[:, c, :], mod[:, shift * 8 + c, half:half + 1], h_hi[:, c, t],
                                                 ALU.add, ALU.subtract).then_inc(h_ok, 1)
                    else:
                        dve.tensor_tensor(h_lo[:, c, t], nf[:, c, :], h_hi[:, c, t], ALU.subtract).then_inc(h_ok, 1)

                for c in range(DC):
                    normed(c)
                    if c and split_out:
                        low(c - 1)
                if split_out:
                    low(DC - 1)

            def attention(which, groups, l=None):
                first, pair0 = attn_base(which, l)
                items = [(g, r) for g in range(len(groups)) for r in range(2)]
                for i in range(len(items) + 2):
                    if i < len(items):
                        g, r = items[i]
                        G = groups[g]
                        c = i % 8
                        dve.wait_ge(s_ok, first + i + 1)
                        if i >= 2 or which != "first":
                            dve.wait_ge(t_ok, first + i - 1)
                        if G.get("bias"):
                            dve.wait_ge(bias_ok, 1 + g + l * WH)
                        if which != "first":
                            dve.memset(passed[:, c:c + 1], 0.0)
                        dve.tensor_tensor_reduce(G["probs"][:, i % 2, 0:G["nk"]], wk[:, i % 2, 0:G["nk"]], G["mask"][r], G["scale"],
                                                 -3.0e38, ALU.add, ALU.max, smx[:, c:c + 1]).then_inc(m_raw, 1)
                        dve.wait_ge(m_raw, first + i + 1)
                        if G["sink"] is not None:
                            dve.tensor_scalar(snm[:, c:c + 1], smx[:, c:c + 1], G["sink"], -1.0, ALU.max, ALU.mult).then_inc(m_ok, 1)
                        else:
                            dve.tensor_scalar(snm[:, c:c + 1], smx[:, c:c + 1], -1.0, None, ALU.mult).then_inc(m_ok, 1)
                    j = i - 1
                    if 0 <= j < len(items):
                        g, r = items[j]
                        G = groups[g]
                        c = j % 8
                        dve.wait_ge(p_ok, first * 2 + 2 * j + 2)
                        dve.tensor_tensor(sden[:, c:c + 1], ssum[:, c:c + 1], ses[:, c:c + 1], ALU.add).then_inc(den_ok, 1)
                        dve.wait_ge(den_ok, first + j + 1)
                        dve.reciprocal(srec[:, c:c + 1], sden[:, c:c + 1]).then_inc(rec_ok, 1)
                        dve.wait_ge(rec_ok, first + j + 1)
                        pr = G["probs"][:, j % 2, 0:G["nk"]]
                        dve.tensor_scalar(pr, pr, srec[:, c:c + 1], None, ALU.mult).then_inc(pn_ok, 1)
                    j = i - 2
                    if j >= 0:
                        g, r = items[j]
                        G = groups[g]
                        if r == 1 and G["last"]:
                            dve.wait_ge(o_hi_ok, pair0 + G["pair"] + 1)
                            dve.tensor_tensor(G["lo"], G["acc"], G["hi"], ALU.subtract).then_inc(o_done, 1)

            def ada(i):
                def evac(l, it, b):
                    dve.tensor_copy(ada_s[0:4, bass.ts(it, 2 * COLS)][:, b * COLS:(b + 1) * COLS], acc[0:4, b, 0, 0:S])\
                        .then_inc(acc_free, 1)
                return evac

            def residual(gate, both, bpi):
                def evac(l, it, b):
                    x = xT[:, bass.ts(it, 2 * bpi), :]
                    for cb in range(2):
                        for half in range(2 if both else 1):
                            t = slice(half * S, half * S + S)
                            col = mod[:, bass.ds(gate * 8 + it * 2 * bpi + 2 * b + cb, 1), half]
                            ins = dve.scalar_tensor_tensor(x[:, 2 * b + cb, t], acc[:, b % 2, cb, t], col, x[:, 2 * b + cb, t],
                                                           ALU.mult, ALU.add)
                    ins.then_inc(acc_free, 1)
                return evac

            def residual2(factor, bpi):
                def evac(l, it, b):
                    x = xT[:, bass.ts(it, 2 * bpi), 0:S][:, 2 * b:2 * b + 2, :]
                    dve.scalar_tensor_tensor(x, acc[:, b % 2, :, 0:S], factor, x, ALU.mult, ALU.add)\
                        .then_inc(acc_free, 1)
                return evac

            def gate_up(name, T, n0):
                def evac(l, it, b):
                    if b == 0:
                        return
                    n = n0 + it + (l * 22 if l is not None else 0)
                    buf = act_buf[:, :, 0:T]
                    dve.wait_ge(acc_free, J[name].taken(l, it, 0))
                    dve.tensor_tensor(buf, buf, acc[:, 1, :, 0:T], ALU.mult).then_inc(acc_free, 1)
                    dve.wait_ge(hid_hi_ok, n + 1)
                    dve.tensor_tensor(hid_lo[:, bass.ts(it, 2), 0:T], buf, hid_hi[:, bass.ts(it, 2), 0:T], ALU.subtract).then_inc(hid_ok, 1)
                return evac

            def rope(n0, dst):
                def evac(l, it, b):
                    n = n0 + 2 * it + b
                    dve.wait_ge(swp_ok, n + 1)
                    dve.tensor_tensor(rot[:], acc[:, b % 2, :, 0:S], cos_r[:], ALU.mult).then_inc(acc_free, 1)
                    dve.tensor_tensor(swp[:], swp[:], sin_r[:], ALU.mult).then_inc(rot_ok, 1)
                    dve.wait_ge(rot_ok, n + 1)
                    dve.tensor_tensor(dst[:, bass.ts(it, 4), 0:S][:, 2 * b:2 * b + 2, :], rot[:], swp[:], ALU.add).then_inc(rope_ok, 1)
                return evac

            def branch(i):
                job = J[("attn_out", "lru_out", "mem_out")[i]]

                def evac(l, it, b):
                    bb = (lambda k: gates[:, 8 * k + 2 * b:8 * k + 2 * b + 2, :]) if job.iters == 1 else \
                        (lambda k: gates[:, 8 * k:8 * k + 8, :][:, bass.ts(it, 4), :][:, 2 * b:2 * b + 2, :])
                    dve.tensor_tensor(bb(i), bb(i), acc[:, b % 2, :, 0:S], ALU.mult).then_inc(acc_free, 1)
                    if i:
                        dve.wait_ge(acc_free, job.taken(l, it, b))
                        if i == 2:
                            dve.wait_ge(sum2_ok, 4 + l * 4)
                        dve.tensor_tensor(bb(0), bb(0), bb(i), ALU.add).then_inc(mg_ok if i == 2 else sum2_ok, 1)
                        if i == 2:
                            dve.wait_ge(mgh_ok, 1 + b + l * 4)
                            dve.tensor_tensor(h_lo[:, 2 * b:2 * b + 2, S:2 * S], bb(0), h_hi[:, 2 * b:2 * b + 2, S:2 * S],
                                              ALU.subtract).then_inc(mg_done, 1)
                return evac

            dve.memset(eps[:], EPS).then_inc(setup, 1)
            dve.memset(nomask[:], 0.0).then_inc(setup, 1)
            dve.memset(smx[:], 0.0).then_inc(lo_done, SLOTS)
            dve.memset(snm[:], 0.0).then_inc(units_used, SLOTS)
            dve.memset(sden[:], 0.0).then_inc(acc_free, 2)
            dve.wait_ge(prm_t, 1)
            dve.tensor_copy(prm[:, 0, :], wk[:, 3, 0:P]).then_inc(prm_ok, 1)
            dve.tensor_copy(prm[:, 1:3, 0:CUR], wk[:, 3, P:3 * P].rearrange("p (t n) -> p t n", t=2)[:, :, 0:CUR]).then_inc(prm_ok, 1)
            dve.tensor_copy(prm[:, 3, 0:PRM3], wk[:, 3, 3 * P:3 * P + PRM3]).then_inc(prm_ok, 1)

            def turned_in(n0, half):
                for g in range(4):
                    dve.wait_ge(turned, n0 + g + 1)
                    dve.tensor_copy(xT[:, 2 * g:2 * g + 2, half * S:(half + 1) * S],
                                    acc[:, g // 2, g % 2].rearrange("p (c t) -> p c t", c=2)).then_inc(x_done, 1)

            turned_in(0, 0)
            turned_in(4, 1)
            dve.wait_ge(c_hi_ok, 1)
            parts = c_parts[:].rearrange("p k (w s) -> p k w s", s=2)
            dve.tensor_tensor(parts[:, :, :, 1], c_act[:].rearrange("p (w k) -> p k w", w=2), parts[:, :, :, 0], ALU.subtract)\
                .then_inc(c_lo_ok, 1)
            dve.wait_ge(prm_ok, 3)
            dve.tensor_copy(soft_in[:, 8:24].rearrange("p (l n) -> p l n", l=2), prm[:, 1:3, LAM:LAM + 8]).then_inc(soft_ok, 1)
            dve.wait_ge(in_prm, 16 * PRM_DMAS)
            dve.wait_ge(soft_ok, 1)
            dve.scalar_tensor_tensor(soft_t[:], soft_in[:], -1.0, soft_in[:], ALU.mult, ALU.min).then_inc(soft_v, 1)
            head("ada0")
            dve.wait_ge(soft_a, 1)
            n = [1]

            def chained(ins):
                ins.then_inc(soft_ok, 1)
                n[0] += 1
                dve.wait_ge(soft_ok, n[0])

            chained(dve.tensor_scalar(soft_w[:], soft_e[:], 2.0, None, ALU.add))
            chained(dve.reciprocal(soft_p[:], soft_w[:]))
            chained(dve.tensor_tensor(soft_w[:], soft_e[:], soft_p[:], ALU.mult))
            chained(dve.tensor_tensor(soft_e[:], soft_w[:], soft_w[:], ALU.mult))
            chained(dve.tensor_scalar(soft_p[:], soft_e[:], 1.0 / 15, 1.0 / 13, ALU.mult, ALU.add))
            for k in (11, 9, 7, 5, 3, 1):
                chained(dve.tensor_tensor(soft_p[:], soft_p[:], soft_e[:], ALU.mult))
                chained(dve.tensor_scalar(soft_p[:], soft_p[:], 1.0 / k, None, ALU.add))
            chained(dve.tensor_tensor(soft_p[:], soft_p[:], soft_w[:], ALU.mult))
            chained(dve.tensor_scalar(soft_t[:], soft_in[:], -1.0, 0.0, ALU.mult, ALU.max))
            chained(dve.scalar_tensor_tensor(soft[:], soft_p[:], 2.0, soft_t[:], ALU.mult, ALU.add))
            dve.tensor_scalar(decay[:, 0, :], soft[:, 0:8], -1.0, None, ALU.mult)
            dve.tensor_copy(decay[:, 1, :], soft[:, 0:8])
            dve.tensor_scalar(decay[:, 2, :], soft[:, 0:8], -2.0 * S, None, ALU.mult)
            lam = soft[:, 8:24].rearrange("p (l n) -> p l n", l=2)
            dve.tensor_scalar(lam_s[:, :, 0, :], lam, -8.0, None, ALU.mult)
            chained(dve.tensor_scalar(lam_s[:, :, 1, :], lam, -16.0, None, ALU.mult))

            def modulations(i):
                dve.wait_ge(ada_sum, i + 1)
                dve.tensor_tensor(mod[:], wk[:, 2, 0:96].rearrange("p (c w) -> p c w", w=2),
                                  prm[:, 0, 48 * i:48 * i + 48].unsqueeze(2).broadcast_to((P, 48, 2)), ALU.add).then_inc(mod_ok, 1)
                dve.wait_ge(mod_ok, i + 1)
                for k, norm_g in ((0, prm[:, 0, NORM1 + 8 * i:NORM1 + 8 * i + 8]), (1, prm[:, 3, NORM2 + 8 * i:NORM2 + 8 * i + 8])):
                    dve.scalar_tensor_tensor(gain[:, k], mod[:, 8 + 24 * k:16 + 24 * k, :], 1.0,
                                             norm_g.unsqueeze(2).broadcast_to((P, DC, 2)), ALU.add, ALU.mult).then_inc(gain_ok, 1)
                dve.wait_ge(gain_ok, 2 * i + 2)

            def gain_at(k, half):
                return lambda c: gain[:, k, c, half:half + 1]

            rest("ada0", ada(0))
            head("q0", None, "ada0", ada(0))
            modulations(0)
            norm(0, 0, gain_at(0, 0), 0)
            norm(1, 1, gain_at(0, 1), 0)
            rest("q0", None)
            head("kv0", None, "q0", None)
            rest("kv0", None)
            head("wo0", None, "kv0", None)
            dve.wait_ge(in_attn, 80)
            for c in range(11):
                if c < 10:
                    dve.wait_ge(hstd, c + 1)
                    dve.reciprocal(sd_b[:, c % 2, :], sd_b[:, c % 2, :]).then_inc(hrec, 1)
                    dve.wait_ge(hrec, c + 1)
                    col = Q_N if c < 8 else K_N
                    dve.scalar_tensor_tensor(qk[:, c, :], qk[:, c, :], prm[:, 3, col:col + 1], sd_b[:, c % 2, :], ALU.mult, ALU.mult)\
                        .then_inc(hn, 1)
                if c:
                    b = c - 1
                    dve.wait_ge(hperm, b + 1)
                    dve.tensor_tensor(rot_b[:, b % 2, 0, :], qk[:, b, 0:S], cos_a[:, :], ALU.mult)
                    dve.tensor_tensor(rot_b[:, b % 2, 1, :], wk[:, 2 + b % 2, 0:S], sin_a[:, :], ALU.mult).then_inc(hrot, 1)
                    dve.wait_ge(hrot, b + 1)
                    dve.tensor_tensor(qk[:, b, 0:S], rot_b[:, b % 2, 0, :], rot_b[:, b % 2, 1, :], ALU.add).then_inc(hqk, 1)
            attention("first", groups_first())
            rest("wo0", residual(2, True, 2))
            head("gu0", None, "wo0", residual(2, True, 2))
            norm(2, 0, gain_at(1, 0), 3)
            norm(3, 1, gain_at(1, 1), 3)
            rest("gu0", gate_up("gu0", 2 * S, 0))
            head("dn0", None, "gu0", gate_up("gu0", 2 * S, 0))
            rest("dn0", residual(5, True, 2))
            head("ada1", None, "dn0", residual(5, True, 2))
            rest("ada1", ada(1))
            head("rq", None, "ada1", ada(1))
            modulations(1)
            norm(4, 0, gain_at(0, 0), 0)
            norm(5, 1, gain_at(0, 1), 0)
            dve.wait_ge(in_rope, 32)
            rest("rq", rope(0, r_q))
            head("rk", None, "rq", rope(0, r_q))
            rest("rk", rope(4, r_k))
            head("rv", None, "rk", rope(4, r_k))
            rest("rv", None)
            head("rg", None, "rv", None)
            rest("rg", None)
            head("rwo", None, "rg", None)
            dve.wait_ge(in_tabs, 48)
            for h in range(RH):
                dve.tensor_scalar(r_d[:, 0:2, :], ahead, decay[:, 0, h:h + 1], None, ALU.mult).then_inc(dx_a, 1)
                dve.wait_ge(dx_a, h + 1)
                dve.scalar_tensor_tensor(r_d[:, 0:2, :], behind, decay[:, 0, 4 + h:5 + h], r_d[:, 0:2, :], ALU.mult, ALU.add)\
                    .then_inc(dx_in, 1)
                dve.wait_ge(dx_e, h + 1)
                for kt in range(2):
                    diag = r_d[:, kt, kt * P:(kt + 1) * P]
                    dve.tensor_tensor(diag, diag, ident[:, :], ALU.add)
                dve.wait_ge(dc_e, 2 * h + 2)
                dve.tensor_tensor(r_d[:, 2:4, :], r_d[:, 2:4, :], act_buf[:, 0, :].rearrange("p (m n) -> p m n", m=2), ALU.add)\
                    .then_inc(d_ok, 1)
                dve.wait_ge(d_ok, h + 1)
                for b in range(2):
                    dve.wait_ge(rs_ok, 2 * h + b + 1)
                    if h:
                        dve.wait_ge(ro_ok, 2 * h)
                    dve.scalar_tensor_tensor(r_p[:, 2 * b:2 * b + 2, :], wk[:, b, :].rearrange("p (k n) -> p k n", k=2), RQ ** -0.5,
                                             r_d[:, 2 * b:2 * b + 2, :], ALU.mult, ALU.mult).then_inc(rp_ok, 1)
                for r in range(2):
                    i = 2 * h + r + 1
                    dve.wait_ge(ro_ok, i)
                    dve.bn_stats(stats[:, r, :], wk[:, 2 + r, :]).then_inc(bn_ok, 1)
                    dve.wait_ge(bn_ok, i)
                    dve.bn_aggr(mv[:, r, :], stats[:, r, :]).then_inc(mv_ok, 1)
                for r in range(2):
                    i = 2 * h + r + 1
                    dve.wait_ge(gs_ok, i)
                    dve.reciprocal(gstd[:, r:r + 1], gstd[:, r:r + 1]).then_inc(gr_ok, 1)
                    dve.wait_ge(gr_ok, i)
                    if h:
                        dve.wait_ge(yt_ok, h)
                    dve.tensor_scalar(r_y[:, r, :], wk[:, 2 + r, :], mv[:, r, 0:1], gstd[:, r:r + 1], ALU.subtract, ALU.mult)\
                        .then_inc(y_ok, 1)
                dve.wait_ge(acc_free, J["rg"].done())
                dve.wait_ge(yt_ok, h + 1)
                z = act_buf[:].rearrange("p a (b t) -> p (a b) t", b=2)
                for c in range(4):
                    dve.scalar_tensor_tensor(z[:, c, :], acc[:, 0, c // 2, (c % 2) * S:(c % 2 + 1) * S],
                                             prm[:, 3, GN_G + 4 * h + c:GN_G + 4 * h + c + 1], r_g[:, 4 * h + c, :],
                                             ALU.mult, ALU.mult).then_inc(z_ok if c == 3 else z_part, 1)
                dve.wait_ge(zh_ok, h + 1)
                dve.tensor_tensor(z_lo[:, 4 * h:4 * h + 4, :], z, z_hi[:, 4 * h:4 * h + 4, :], ALU.subtract).then_inc(z_done, 1)
            rest("rwo", residual(2, False, 2))
            head("gu1", None, "rwo", residual(2, False, 2))
            norm(6, 0, gain_at(1, 0), 3)
            rest("gu1", gate_up("gu1", S, 11))
            head("dn1", None, "gu1", gate_up("gu1", S, 11))
            rest("dn1", residual(5, False, 2))
            tail("dn1", residual(5, False, 2))
            turned_in(8, 1)

            with dve.Fori(0, LAYERS2) as l:
                n0 = NORMS1 + l * 4
                dve.tensor_copy(cur[:, 0:CUR], prm[:, bass.ds(l + 1, 1), 0:CUR].rearrange("p o n -> p (o n)")).then_inc(cur_ok, 1)
                dve.tensor_copy(cur[:, CUR:CUR + 16], lam_s[:, bass.ds(l, 1)].rearrange("p o w c -> p (o w c)")).then_inc(cur_ok, 1)
                dve.tensor_copy(sink_l[:], sinks[:, 16:32].rearrange("p (l h) -> p l h", l=2)[:, bass.ds(l, 1), :]
                                .rearrange("p o h -> p (o h)")).then_inc(cur_ok, 1)
                dve.wait_ge(cur_ok, 3 + l * 3)

                def gain_in(col):
                    return lambda c: cur[:, col + c:col + c + 1]

                head("gua", l)
                norm(n0, 0, gain_in(FFN1_N))
                rest("gua", gate_up("gua", S, 22), l)
                head("dna", l, "gua", gate_up("gua", S, 22))
                rest("dna", residual2(0.5, 2), l)
                head("memk", l, "dna", residual2(0.5, 2))
                norm(n0 + 1, 0, gain_in(MIX_N))
                norm(n0 + 2, 1, gain_in(MEM_N))
                rest("memk", None, l)
                head("memv", l, "memk", None)
                rest("memv", None, l)
                head("xr", l, "memv", None)
                rest("xr", None, l)
                head("yr", l, "xr", None)

                def conv(w):
                    for c in range(DC):
                        src, tap = XR[:, c, 1 + w:1 + w + S], cur[:, CONV_W + 8 * w + c:CONV_W + 8 * w + c + 1]
                        if w == 0:
                            ins = dve.tensor_scalar(XC[:, c, :], src, tap, cur[:, CONV_B + c:CONV_B + c + 1], ALU.mult, ALU.add)
                        else:
                            dve.wait_ge(conv_ok, 8 * (w - 1) + c + 1 + l * 32)
                            ins = dve.scalar_tensor_tensor(XC[:, c, :], src, tap, XC[:, c, :], ALU.mult, ALU.add)
                        ins.then_inc(conv_ok, 1)

                dve.memset(XR[:, :, 0:4], 0.0).then_inc(pad_ok, 1)
                dve.wait_ge(pad_ok, 1 + l)
                dve.wait_ge(acc_free, J["xr"].done(l))
                conv(0)
                conv(1)
                rest("yr", None, l)
                head("gates", l, "yr", None)
                conv(2)
                conv(3)
                dve.wait_ge(xch_ok, 1 + l)
                dve.tensor_tensor(h_lo[:, :, S:2 * S], XC[:], h_hi[:, :, S:2 * S], ALU.subtract).then_inc(xc_ok, 1)
                rest("gates", None, l)
                head("kvlru", l, "gates", None)
                rest("kvlru", None, l)
                head("q", l, "kvlru", None)
                rest("q", None, l)
                head("cq", l, "q", None)
                rest("cq", None, l)
                head("attn_out", l, "cq", None)
                dve.wait_ge(vt_ok, 1 + l)
                dve.tensor_copy(v_2[:].rearrange("p r n -> p (r n)"), wk[:, 3, 0:S]).then_inc(v2_ok, 1)
                dve.wait_ge(e2_ok, 16 + l * 16)
                dve.tensor_scalar(XR[:, :, 0:S], XR[:, :, 0:S], 1.0, None, ALU.min).then_inc(cl_ok, 1)
                dve.wait_ge(mu_ok, 1 + l)
                dve.memset(XR[:, :, 0:1], 1.0).then_inc(b_ok, 1)
                dve.wait_ge(b_ok, 1 + l * 3)
                dve.tensor_tensor(GI[:], GI[:], XR[:, :, 0:S], ALU.mult).then_inc(b_ok, 1)
                dve.wait_ge(b_ok, 2 + l * 3)
                dve.tensor_tensor(GI[:], GI[:], XC[:], ALU.mult).then_inc(b_ok, 1)
                dve.wait_ge(b_ok, 3 + l * 3)
                for c in range(DC):
                    dve.tensor_tensor_scan(XR[:, c, 0:S], R[:, c, :], GI[:, c, :], 0.0, ALU.mult, ALU.add).then_inc(scan_ok, 1)
                dve.wait_ge(scan_ok, 8 + l * 8)
                dve.tensor_tensor(XC[:], XR[:, :, 0:S], gy[:], ALU.mult).then_inc(lru_ok, 1)
                dve.wait_ge(lruh_ok, 1 + l)
                dve.tensor_tensor(h_lo[:, :, S:2 * S], XC[:], h_hi[:, :, S:2 * S], ALU.subtract).then_inc(lru_done, 1)
                attention("window", groups_window(), l)
                attention("memory", groups_memory(), l)
                rest("attn_out", branch(0), l)
                head("lru_out", l, "attn_out", branch(0))
                rest("lru_out", branch(1), l)
                head("mem_out", l, "lru_out", branch(1))
                rest("mem_out", branch(2), l)
                head("w_out", l, "mem_out", branch(2))
                rest("w_out", residual2(1.0, 2), l)
                head("gub", l, "w_out", residual2(1.0, 2))
                norm(n0 + 3, 0, gain_in(FFN2_N))
                rest("gub", gate_up("gub", S, 33), l)
                head("dnb", l, "gub", gate_up("gub", S, 33))
                rest("dnb", residual2(0.5, 2), l)
                tail("dnb", residual2(0.5, 2), l)
            norm(NORM_LAST, 0, lambda c: prm[:, 3, FINAL_N + c:FINAL_N + c + 1], split_out=False)
            for g in range(4):
                dve.wait_ge(fin_t, g + 1)
                dve.tensor_copy(rows[:, g * 512:(g + 1) * 512], wk[:, g, :] if g < 3 else acc[:, 0, 0, :]).then_inc(fin_ok, 1)



INS = ["x", "c", "ctx", "c_ctx", "ada_w", "ada_b", "norm1_g", "norm2_g", "ffn_w_in", "ffn_w_out", "attn_w_qkv",
       "attn_q_norm", "attn_k_norm", "attn_sink", "attn_w_o", "ret_w_qkvg", "ret_decay_logit", "ret_gn_g", "ret_w_o",
       "mem_2", "ffn1_norm_2", "ffn1_w_gate_2", "ffn1_w_up_2", "ffn1_w_down_2", "mix_norm_2", "w_in_2", "gate_bias_2",
       "attn_sinks_2", "w_attn_out_2", "conv_w_2", "conv_b_2", "lru_wa_2", "lru_ba_2", "lru_wx_2", "lru_bx_2",
       "lru_lambda_2", "w_lru_out_2", "mem_norm_2", "w_mem_kv_2", "w_mem_out_2", "w_out_2", "ffn2_norm_2",
       "ffn2_w_gate_2", "ffn2_w_up_2", "ffn2_w_down_2", "final_norm_2"]


def kernel(**inputs):
    import concourse.bacc as bacc
    from concourse.bass_utils import run_bass_kernel_spmd

    nc = bacc.Bacc("TRN2", target_bir_lowering=False, num_devices=1)
    table, const_at = shape_constants()
    arrays, aps = {}, {}
    for name in INS + ["shape_constants"]:
        data = table if name == "shape_constants" else np.ascontiguousarray(inputs[name])
        arrays[f"in_{name}_dram"] = data
        aps[name] = nc.dram_tensor(f"in_{name}_dram", data.shape, mybir.dt.from_np(data.dtype), kind="ExternalInput").ap()
    out = nc.dram_tensor("out_0_dram", (1, S, D), F32, kind="ExternalOutput").ap()
    build(nc, aps, out, const_at)
    r = run_bass_kernel_spmd(nc, [arrays], core_ids=[0])
    return r.results[0]["out_0_dram"]
```

```python
from contextlib import ExitStack

import numpy as np

import concourse.bass as bass
from concourse import mybir

F32 = mybir.dt.float32
F32R = mybir.dt.float32r
ALU = mybir.AluOpType
ACT = mybir.ActivationFunctionType

P = 128
D = 1024
DC = D // P
S = 256
FF = 2816
FC = FF // P
COLS = 256
KCH = 4
SLOTS = 4
LAG = 3
EPS = 1e-6
MASKED = -1e30
HEADS, HD, GROUP = 16, 64, 4
RH, RQ, RV = 4, 256, 512
WH = 8
MH = 4
LAYERS2 = 2
ROPE_BASE = 10000.0
GRID_W = 64



def shape_constants():
    tok = np.arange(S)
    row, col = (tok // GRID_W).astype(np.float32), (tok % GRID_W).astype(np.float32)

    def rope(head_dim, d):
        axis = head_dim // 2
        half = axis // 2
        inv = (np.float32(ROPE_BASE) ** (-np.arange(0, axis, 2, dtype=np.float32) / np.float32(axis))).astype(np.float32)
        pos = np.where((d // axis == 0)[:, None], row[None, :], col[None, :]).astype(np.float32)
        ang = (pos * inv[d % half][:, None]).astype(np.float32)
        sign = np.where(d % axis < half, -1.0, 1.0)[:, None]
        return np.cos(ang), np.sin(ang) * sign

    p = np.arange(P)
    cos_a, sin_a = rope(HD, p % HD)
    rc, rs = zip(*[rope(RQ, p + P * c) for c in range(2)])
    q = p[:, None, None] + P * np.arange(2)[None, :, None]
    k = np.arange(S)[None, None, :]
    window = np.concatenate([np.where(np.abs(k - q) <= P, 0.0, MASKED), np.zeros((P, 2, S))], axis=2)
    back = q // 64 - k // 64
    alibi = np.where((back >= 0) & (back <= 2), np.abs(q - k), -MASKED)
    m = q
    n = k
    parts = {
        "ident": np.eye(P), "ones": np.ones((P, P)), "alibi": alibi.reshape(P, -1),
        "slopes": np.tile(-(2.0 ** -np.arange(1.0, WH + 1)) * HD ** 0.5, (P, 1)),
        "sel": np.repeat(np.eye(2), 2, axis=0)[np.minimum(p, 3)] * (p < 4)[:, None],
        "headsum": (np.arange(20)[None, None, :] == 2 * np.arange(10)[None, :, None] + p[:, None, None] // HD).reshape(P, -1),
        "headback": (p[:, None, None] == 2 * np.arange(10)[None, :, None] + p[None, None, :] // HD).reshape(P, -1),
        "partner": (p[:, None] == (p[None, :] ^ (HD // 4))),
        "cos_a": cos_a, "sin_a": sin_a, "window": window.reshape(P, -1),
        "cos_r": np.concatenate(rc, 1), "sin_r": np.concatenate(rs, 1),
        "ahead": np.maximum(n - m, 0).reshape(P, -1), "behind": np.maximum(m - n, 0).reshape(P, -1),
        "since": (n + S - m).reshape(P, -1),
    }
    at, width = {}, 0
    for name, a in parts.items():
        at[name] = (width, a.shape[1])
        width += a.shape[1]
    return np.concatenate([np.asarray(a, np.float32) for a in parts.values()], axis=1), at




class Job:

    def __init__(self, unit_chunks, ends, iters, acts_from=0):
        self.unit_chunks = unit_chunks
        self.ends = ends
        self.iters = iters
        self.body = len(unit_chunks)
        self.per = len(ends)
        self.unit0 = self.block0 = self.unit_step = self.block_step = 0
        assert self.body % SLOTS == 0 and self.per % 2 == 0

    def unit(self, l, it, p):
        return self.unit0 + p + it * self.body + (l * self.unit_step if self.unit_step else 0)

    def block(self, l, it, b):
        return self.block0 + b + it * self.per + (l * self.block_step if self.block_step else 0)

    def taken(self, l, it, b):
        return self.block(l, it, b) + 3

    def done(self, l=None):
        return self.taken(l, self.iters - 1, self.per - 1)

    def loaded(self, l, it, p):
        return 16 * (self.unit0 // SLOTS + p // SLOTS + 1) + it * (16 * self.body // SLOTS) \
            + (l * (16 * self.unit_step // SLOTS) if self.unit_step else 0)


def columns(k_chunks, n):
    per_block = [KCH] * (k_chunks // KCH) + ([k_chunks % KCH] if k_chunks % KCH else [])
    blocks = 2
    while len(per_block) * blocks % SLOTS:
        blocks += 2
    units = per_block * blocks
    return Job(units, [len(per_block) * (b + 1) - 1 for b in range(blocks)], n // COLS // blocks)


FIRST = ["ada0a", "q0", "kv0", "ada0b", "ada1", "wo0", "gu0", "dn0", "rq", "rk", "rv", "rg", "rwo", "gu1", "dn1"]
SECOND = ["gua", "dna", "memk", "memv", "xr", "yr", "gates", "kvlru", "q", "cq", "attn_out", "lru_out",
          "mem_out", "w_out", "gub", "dnb"]


def plan():
    two = lambda n: columns(DC, n)
    jobs = {
        "ada0a": two(2 * D), "ada0b": two(4 * D), "q0": two(D), "kv0": two(512), "wo0": two(D), "gu0": two(2 * FF), "dn0": columns(FC, D),
        "ada1": two(6 * D), "rq": two(D), "rk": two(D), "rv": two(2 * D), "rg": two(2 * D), "rwo": columns(16, D),
        "gu1": two(2 * FF), "dn1": columns(FC, D),
        "gua": two(2 * FF), "dna": columns(FC, D), "memk": two(512), "memv": two(512), "xr": two(D), "yr": two(D),
        "gates": two(3 * D), "kvlru": Job([4, 4, 2, 2], [1, 1, 2, 2, 3, 3], 1), "q": two(512), "cq": two(512),
        "attn_out": columns(4, D), "lru_out": two(D), "mem_out": columns(4, D), "w_out": two(D),
        "gub": two(2 * FF), "dnb": columns(FC, D),
    }
    u = b = 0
    for name in FIRST + SECOND:
        if name == SECOND[0]:
            u2, b2 = u, b
        jobs[name].unit0, jobs[name].block0 = u, b
        u += jobs[name].iters * jobs[name].body
        b += jobs[name].iters * jobs[name].per
    for name in SECOND:
        jobs[name].unit_step, jobs[name].block_step = u - u2, b - b2
    return jobs


JOBS = plan()

NORMS1 = 7
NORM_LAST = NORMS1 + 4 * LAYERS2
X_START, X_MEM = 8, 12
SIDE = ("ada0b", "ada1")


def side_unit(k):
    first = JOBS[SIDE[0]]
    name = SIDE[0] if k < first.body * first.iters else SIDE[1]
    k -= 0 if name == SIDE[0] else first.body * first.iters
    return name, k // JOBS[name].body, k % JOBS[name].body


SIDE_UNITS = sum(JOBS[n].body * JOBS[n].iters for n in SIDE)
SIDE_START = 10


def side_step(k):
    return k * 9 // 10 - SIDE_START


def side_turns():
    ready = []
    for k in range(1, SIDE_UNITS, 2):
        name, it, p = side_unit(k)
        c = (16 if name == "ada0b" else 0) + 2 * (it * JOBS[name].per + p // 2)
        ready += [(side_step(k) + 4, name, c), (side_step(k) + 4, name, c + 1)]
    turns = {}
    for item in range(4 * 16):
        if item % 4 >= 2:
            turns[item] = [r[1:] for r in ready if r[0] <= item + 3][:6]
            ready = ready[len(turns[item]):]
    assert not ready
    return turns


SIDE_TURNS = side_turns()

ITEMS0, ITEMS_WIN, ITEMS_MEM = 4 * HEADS, 2 * WH, 2 * MH
PAIRS0, PAIRS_WIN, PAIRS_MEM = HEADS // 2, WH // 2, MH

ADA_B, C_COL, CC_COL, NORM1 = 0, 96, 104, 112
GATE_B, CONV_W, FFN1_N, MIX_N, CONV_B, BA, BX, LAM, MEM_N, FFN2_N, CUR = 0, 24, 56, 64, 72, 80, 88, 96, 104, 112, 120
PRM_DMAS = 2 * 10 + 3 + 4 + 3
NORM2, FINAL_N, GN_G, Q_N, K_N, PRM3 = 0, 16, 24, 40, 41, 42


def build(nc, a, out, const_at):
    J = JOBS
    st = ExitStack()
    with st:
        def sb(name, shape, dt=F32, on=st):
            return on.enter_context(nc.sbuf_tensor(name, shape, dt))

        def sem(name):
            return st.enter_context(nc.semaphore(name))

        raw = sb("raw", [P, SLOTS, KCH, COLS])
        w_hi = sb("w_hi", [P, SLOTS, KCH, COLS], F32R)
        w_lo = sb("w_lo", [P, SLOTS, KCH, COLS], F32R)
        xT = sb("xT", [P, DC, 2 * S])
        h_hi = sb("h_hi", [P, DC, 2 * S], F32R)
        h_lo = sb("h_lo", [P, DC, 2 * S], F32R)
        rows = sb("rows", [P, 2 * D])
        prm = sb("prm", [P, 4, P])
        cur = sb("cur", [P, CUR + 16])
        mod = sb("mod", [P, 2, 48, 2])
        gain = sb("gain", [P, 2, 2, DC, 2])
        ident = sb("ident", [P, P])
        ones = sb("ones", [P, P])
        alibi = sb("alibi", [P, 2 * S])
        nomask = sb("nomask", [P, S])
        sel = sb("sel", [P, 2])
        slopes = sb("slopes", [P, WH])
        c_parts = sb("c_parts", [P, DC, 4], F32R)
        c_act = sb("c_act", [P, 16])
        std = sb("std", [P, S])
        rstd = sb("rstd", [P, S])
        act_buf = sb("act_buf", [P, 2, 2 * S])
        eps = sb("eps", [P, 1])
        soft_in = sb("soft_in", [P, 24])
        soft_e = sb("soft_e", [P, 24])
        soft_t = sb("soft_t", [P, 24])
        soft_w = sb("soft_w", [P, 24])
        soft_p = sb("soft_p", [P, 24])
        soft = sb("soft", [P, 24])
        decay = sb("decay", [P, 3, 8])
        lam_s = sb("lam_s", [P, 2, 2, 8])
        sinks = sb("sinks", [P, 16 + 16])
        sink_l = sb("sink_l", [P, WH])
        smx, snm, ssum, ses, sden, srec = [sb(f"soft_{k}", [P, 8]) for k in ("mx", "nm", "sum", "es", "den", "rec")]
        passed = sb("passed", [P, 8])
        stats = sb("stats", [P, 2, 6])
        mv = sb("mv", [P, 2, 2])
        gstd = sb("gstd", [P, 2])

        def arena(*parts):
            with ExitStack() as on:
                return [sb(n, s, d, on) for n, s, d in parts]

        hid_hi, hid_lo = arena(("hid_hi", [P, FC, 2 * S], F32R), ("hid_lo", [P, FC, 2 * S], F32R))
        nf, rows_c, prm_rows, _, ada_s = arena(
            ("nf", [P, DC, S], F32), ("rows_c", [P, 2 * D], F32), ("prm_rows", [P, 4, P], F32),
            ("ada_skip", [P, 2 * FC * 2 * S - 6 * D - 4 * D - 4 * P], F32), ("ada_s", [4, 6 * D], F32))
        (qk, v_tok, k_dup, probs_t, sq_b, sd_b, rot_b, headsum, headback, partner, cos_a, sin_a) = arena(
            ("qk", [P, 10, 2 * S], F32), ("v_tok", [P, 4, 256], F32), ("k_dup", [P, 4, 2 * S], F32),
            ("probs_t", [P, 2, 4, S], F32), ("sq_b", [P, 2, 2 * S], F32),
            ("sd_b", [P, 2, 2 * S], F32), ("rot_b", [P, 2, 2, S], F32),
            ("headsum", [P, 10, 20], F32), ("headback", [P, 10, P], F32), ("partner", [P, P], F32), ("cos_a", [P, S], F32), ("sin_a", [P, S], F32))
        probs = arena(("p_skip", [P, 10 * 2 * S + 4 * 256 + 4 * 2 * S + 8 * S], F32), ("probs", [P, 4, 2 * S], F32))[1]
        r_q, r_k, r_v, r_g, cos_r, sin_r, swp, rot, r_d, r_p = arena(
            ("r_q", [P, DC, S], F32), ("r_k", [P, DC, 2 * S], F32), ("r_v", [P, 4, 2 * D], F32), ("r_g", [P, 16, S], F32),
            ("cos_r", [P, 2, S], F32), ("sin_r", [P, 2, S], F32), ("swp", [P, 2, S], F32), ("rot", [P, 2, S], F32),
            ("r_d", [P, 4, S], F32), ("r_p", [P, 4, S], F32))
        r_y = arena(("r_skip", [P, 72 * S + 4 * S], F32), ("r_y", [P, 2, 2 * S], F32))[1]
        (gates, gy, XR, XC, R, GI, k_d, v_2, km, vm, probs2, probs_t2, bias2) = arena(
            ("gates", [P, 24, S], F32), ("gy", [P, DC, S], F32), ("XR", [P, DC, S + 4], F32), ("XC", [P, DC, S], F32),
            ("R", [P, DC, S], F32), ("GI", [P, DC, S], F32), ("k_d", [P, 2, S], F32),
            ("v_2", [P, 2, P], F32), ("km", [P, MH, S], F32), ("vm", [P, 2, 512], F32), ("probs2", [P, 4, S], F32),
            ("probs_t2", [P, 2, 2, S], F32), ("bias2", [P, 2, 2 * S], F32))
        tabs = rows[:, 0:3 * 2 * S].rearrange("p (t m n) -> p t m n", t=3, m=2)
        ahead, behind, since = tabs[:, 0], tabs[:, 1], tabs[:, 2]
        q_2 = rows[:, 0:D].rearrange("p (c t) -> p c t", c=4)
        cq_2 = rows[:, D:2 * D].rearrange("p (c t) -> p c t", c=4)
        window = act_buf
        v_T = std
        nf_m = rows[:, 0:2 * D].rearrange("p (c t) -> p c t", t=S)
        z_hi = h_hi[:].rearrange("p c (u t) -> p (c u) t", u=2)
        z_lo = h_lo[:].rearrange("p c (u t) -> p (c u) t", u=2)

        acc = st.enter_context(nc.psum_tensor("acc", [P, 2, 2, 512], F32))
        wk = st.enter_context(nc.psum_tensor("wk", [P, 4, 512], F32))
        sc_ps = [wk[:, 0], wk[:, 1]]
        pt_ps = [wk[:, 2], acc[:, 0, 1]]
        o_ps = [wk[:, 3], acc[:, 1, 1]]

        load = [sem(f"load{k}") for k in range(SLOTS)]
        hi_done = sem("hi_done")
        lo_done = sem("lo_done")
        units_used = sem("units_used")
        acc_free = sem("acc_free")
        x_done = sem("x_done")
        in_x, in_c, in_m = sem("in_x"), sem("in_c"), sem("in_m")
        in_prm0, in_prm, in_const = sem("in_prm0"), sem("in_prm"), sem("in_const")
        in_attn, in_tabs, in_rope = sem("in_attn"), sem("in_tabs"), sem("in_rope")
        setup = sem("setup")
        prm_t, prm_ok = sem("prm_t"), sem("prm_ok")
        turned = sem("turned")
        c_ok, c_hi_ok, c_lo_ok = sem("c_ok"), sem("c_hi_ok"), sem("c_lo_ok")
        soft_a, soft_v = sem("soft_a"), sem("soft_v")
        ada_sum, mod_ok, gain_ok = sem("ada_sum"), sem("mod_ok"), sem("gain_ok")
        sq_ok = sem("sq_ok")
        ss_ok = sem("ss_ok")
        std_ok, rstd_ok = sem("std_ok"), sem("rstd_ok")
        nf_ok, nh_ok, h_ok = sem("nf_ok"), sem("nh_ok"), sem("h_ok")
        hsq, hss, hstd, hrec, hback, hn, hperm, hrot, hqk, kd_ok = [sem(k) for k in (
            "hsq", "hss", "hstd", "hrec", "hback", "hn", "hperm", "hrot", "hqk", "kd_ok")]
        s_ok, m_raw, m_ok, p_ok, den_ok, rec_ok, pn_ok, t_ok, pt_ok = [sem(k) for k in (
            "s_ok", "m_raw", "m_ok", "p_ok", "den_ok", "rec_ok", "pn_ok", "t_ok", "pt_ok")]
        o_ok, o_hi_ok, o_done = sem("o_ok"), sem("o_hi_ok"), sem("o_done")
        hid_hi_ok, hid_ok = sem("hid_hi_ok"), sem("hid_ok")
        swp_ok, rot_ok, rope_ok = sem("swp_ok"), sem("rot_ok"), sem("rope_ok")
        dx_in, dx_e, dc_e, d_ok, rs_ok, rp_ok, ro_ok = [sem(k) for k in ("dx_in", "dx_e", "dc_e", "d_ok", "rs_ok", "rp_ok", "ro_ok")]
        dx_a, bn_ok, mv_ok, gs_ok, gr_ok, y_ok, yt_ok, z_ok, zh_ok, z_done = [sem(k) for k in (
            "dx_a", "bn_ok", "mv_ok", "gs_ok", "gr_ok", "y_ok", "yt_ok", "z_ok", "zh_ok", "z_done")]
        cur_ok, conv_ok, xch_ok, xc_ok, zero_ok = [sem(k) for k in ("cur_ok", "conv_ok", "xch_ok", "xc_ok", "zero_ok")]
        e2_ok, cl_ok, mu_ok, gx_ok, b_ok, scan_ok, lru_ok, lruh_ok, lru_done = [sem(k) for k in (
            "e2_ok", "cl_ok", "mu_ok", "gx_ok", "b_ok", "scan_ok", "lru_ok", "lruh_ok", "lru_done")]
        vt_ok, v2_ok, bias_ok = sem("vt_ok"), sem("v2_ok"), sem("bias_ok")
        sum2_ok, mg_ok, mgh_ok, mg_done = [sem(k) for k in ("sum2_ok", "mg_ok", "mgh_ok", "mg_done")]
        clear_ok, soft_ok, pad_ok, z_part = [sem(k) for k in ("clear_ok", "soft_ok", "pad_ok", "z_part")]
        fin_t, fin_ok, stored = sem("fin_t"), sem("fin_ok"), sem("stored")

        def const(name):
            o, n = const_at[name]
            return a["shape_constants"][:, o:o + n]

        def chunks(w, k0, nk):
            return w[k0 * P:(k0 + nk) * P, :].rearrange("(k p) n -> p k n", p=P)

        def groups_first():
            gs = []
            for h in range(HEADS):
                for ctx in range(2):
                    half = slice(64 * (h % 2), 64 * (h % 2) + 64)
                    keys = slice(S, 2 * S) if ctx else slice(0, 2 * S)
                    tiles = range(2, 4) if ctx else range(4)
                    gs.append(dict(
                        q=[qk[half, h // 2, ctx * S + r * P:ctx * S + (r + 1) * P] for r in range(2)],
                        k=k_dup[half, h // GROUP, keys], nk=keys.stop - keys.start,
                        mask=[window[:, r, keys] for r in range(2)], sink=sinks[:, h:h + 1], scale=HD ** -0.5,
                        v=[v_tok[:, t, 64 * (h // GROUP):64 * (h // GROUP) + 64] for t in tiles],
                        out=o_ps[h // 2 % 2][half, ctx * S:(ctx + 1) * S], pair=h // 2, last=(h % 2 and ctx),
                        probs=probs, probs_t=probs_t, acc=o_ps[h // 2 % 2][:, 0:2 * S],
                        hi=h_hi[:, h // 2, :], lo=h_lo[:, h // 2, :]))
            return gs

        def groups_window():
            gs = []
            for h in range(WH):
                half = slice(64 * (h % 2), 64 * (h % 2) + 64)
                gs.append(dict(
                    q=[q_2[half, h // 2, r * P:(r + 1) * P] for r in range(2)], k=k_d[half, h // 4, :], nk=S,
                    mask=[bias2[:, h % 2, r * S:(r + 1) * S] for r in range(2)], bias=True, sink=sink_l[:, h:h + 1],
                    scale=HD ** -0.5, v=[v_2[:, t, 64 * (h // 4):64 * (h // 4) + 64] for t in range(2)],
                    out=o_ps[h // 2 % 2][half, 0:S], pair=h // 2, last=h % 2, probs=probs2, probs_t=probs_t2,
                    acc=o_ps[h // 2 % 2][:, 0:S], hi=h_hi[:, h // 2, 0:S], lo=h_lo[:, h // 2, 0:S]))
            return gs

        def groups_memory():
            gs = []
            for h in range(MH):
                gs.append(dict(
                    q=[cq_2[:, h, r * P:(r + 1) * P] for r in range(2)], k=km[:, h, :], nk=S, mask=[nomask[:, :]] * 2,
                    sink=None, scale=P ** -0.5, v=[vm[:, t, P * h:P * h + P] for t in range(2)],
                    out=o_ps[h % 2][:, 0:S], pair=PAIRS_WIN + h, last=True, probs=probs2, probs_t=probs_t2, acc=o_ps[h % 2][:, 0:S],
                    hi=h_hi[:, 4 + h, 0:S], lo=h_lo[:, 4 + h, 0:S]))
            return gs

        def attn_base(which, l):
            if which == "first":
                return 0, 0
            return ITEMS0 + l * (ITEMS_WIN + ITEMS_MEM), PAIRS0 + l * (PAIRS_WIN + PAIRS_MEM)

        T_LAG, N_LAG, O_LAG, H_LAG, L_LAG = 3, 2, 5, 7, 8

        def attn_steps(groups):
            return range(2 * len(groups) - 2 + L_LAG + 1)

        def group_at(i, lag, groups):
            return (i - lag) // 2 if (i - lag) % 2 == 0 and 0 <= (i - lag) // 2 < len(groups) else None

        block = st.enter_context(nc.Block())

        @block.sync
        def _(sp):
            def stream(name, src, l=None):
                job = J[name]

                def one(it):
                    for p in range(job.body):
                        sp.wait_ge(lo_done, job.unit(l, it, p) + 1)
                        s = src(l, it, p)
                        slot = raw[:, p % SLOTS]
                        dst = slot[:, 0:s.shape[1], :] if s.shape[2] == COLS else \
                            slot[:, 0:2, :].rearrange("p k n -> p (k n)").rearrange("p (c j) -> p c j", j=64)
                        sp.dma_start(dst, s).then_inc(load[p % SLOTS], 16)

                if job.iters == 1:
                    one(0)
                else:
                    with sp.Fori(0, job.iters) as it:
                        one(it)

            def plain(w, k_chunks, col0=0, n=None):
                per = -(-k_chunks // KCH)
                n = n or w.shape[-1]

                def src(l, it, p):
                    m = w if l is None else w[l]
                    b, u = divmod(p, per)
                    blocks = 2
                    while per * blocks % SLOTS:
                        blocks += 2
                    k0 = u * KCH
                    view = chunks(m, k0, min(KCH, k_chunks - k0))[:, :, col0:col0 + n]
                    wide = view[:, :, bass.ts(it, blocks * COLS)]
                    return wide[:, :, b * COLS:(b + 1) * COLS]
                return src

            def gate_up(gate, up):
                def src(l, it, p):
                    b, u = divmod(p, 2)
                    m = (gate, up)[b] if l is None else (gate, up)[b][l]
                    return chunks(m, u * KCH, KCH)[:, :, bass.ts(it, COLS)]
                return src

            sp.dma_start(prm_rows[0:96, 0, :], a["ada_b"].rearrange("l (r f) -> (l r) f", f=P)).then_inc(in_prm0, 16)
            sp.dma_start(prm_rows[96:104, 0, :], a["c"].rearrange("l (r f) -> (l r) f", f=P)).then_inc(in_prm0, 16)
            sp.dma_start(prm_rows[104:112, 0, :], a["c_ctx"].rearrange("(r f) -> r f", f=P)).then_inc(in_prm0, 16)
            sp.dma_start(prm_rows[112:128, 0, :], a["norm1_g"].rearrange("l (r f) -> (l r) f", f=P)).then_inc(in_prm0, 16)
            stream("ada0a", plain(a["ada_w"][0], DC, 0, 2 * D))
            wqkv = a["attn_w_qkv"][0]
            stream("q0", plain(wqkv, DC, 0, D))
            stream("kv0", plain(wqkv, DC, D, 512))
            stream("ada0b", plain(a["ada_w"][0], DC, 2 * D, 4 * D))
            stream("ada1", plain(a["ada_w"][1], DC))
            stream("wo0", plain(a["attn_w_o"][0], DC))
            stream("gu0", gate_up(a["ffn_w_in"][0][:, 0:FF], a["ffn_w_in"][0][:, FF:2 * FF]))
            stream("dn0", plain(a["ffn_w_out"][0], FC))
            wr = a["ret_w_qkvg"][0]
            stream("rq", plain(wr, DC, 0, D))
            stream("rk", plain(wr, DC, D, D))
            stream("rv", plain(wr, DC, 2 * D, 2 * D))
            stream("rg", plain(wr, DC, 4 * D, 2 * D))
            stream("rwo", plain(a["ret_w_o"][0], 16))
            stream("gu1", gate_up(a["ffn_w_in"][1][:, 0:FF], a["ffn_w_in"][1][:, FF:2 * FF]))
            stream("dn1", plain(a["ffn_w_out"][1], FC))
            with sp.Fori(0, LAYERS2) as l:
                stream("gua", gate_up(a["ffn1_w_gate_2"], a["ffn1_w_up_2"]), l)
                stream("dna", plain(a["ffn1_w_down_2"], FC), l)
                stream("memk", plain(a["w_mem_kv_2"], DC, 0, 512), l)
                stream("memv", plain(a["w_mem_kv_2"], DC, 512, 512), l)
                w_in = a["w_in_2"]
                stream("xr", plain(w_in, DC, 768, D), l)
                stream("yr", plain(w_in, DC, 768 + D, D), l)
                stream("gates", plain(w_in, DC, 1280 + 2 * D, 3 * D), l)

                def kvlru(l, it, p):
                    if p < 2:
                        return chunks(w_in[l], p * KCH, KCH)[:, :, 512:768]
                    return a[("lru_wa_2", "lru_wx_2")[p - 2]][l].rearrange("(c two) i j -> (two i) c j", two=2)
                stream("kvlru", kvlru, l)

                def q_unit(l, it, p):
                    rows_l = w_in.rearrange("l k n -> (l k) n")[bass.ds(l * D + p % 2 * KCH * P, KCH * P), :]
                    return chunks(rows_l, 0, KCH)[:, :, p // 2 * COLS:(p // 2 + 1) * COLS]
                stream("q", q_unit, l)
                stream("cq", plain(w_in, DC, 768 + 2 * D, 512), l)
                stream("attn_out", plain(a["w_attn_out_2"], 4), l)
                stream("lru_out", plain(a["w_lru_out_2"], DC), l)
                stream("mem_out", plain(a["w_mem_out_2"], 4), l)
                stream("w_out", plain(a["w_out_2"], DC), l)
                stream("gub", gate_up(a["ffn2_w_gate_2"], a["ffn2_w_up_2"]), l)
                stream("dnb", plain(a["ffn2_w_down_2"], FC), l)
            for r in range(2):
                sp.wait_ge(fin_ok, 2 * (r + 1))
                sp.dma_start(out[0, r * P:(r + 1) * P, :], rows[:, r * D:(r + 1) * D]).then_inc(stored, 16)
            sp.wait_ge(stored, 32)

        @block.gpsimd
        def _(pool):
            def tokens(dst, src, s):
                for r in range(2):
                    pool.dma_start(dst[:, r * D:(r + 1) * D], src[0, r * P:(r + 1) * P, :]).then_inc(s, 16)

            for name, t in (("ident", ident), ("ones", ones), ("alibi", alibi), ("sel", sel), ("slopes", slopes)):
                pool.dma_start(t[:, :], const(name)).then_inc(in_const, 16)
            tokens(rows, a["x"], in_x)
            tokens(rows_c, a["ctx"], in_c)
            for l in range(LAYERS2):
                at = 0
                for name, n in (("gate_bias_2", 24), ("conv_w_2", 32), ("ffn1_norm_2", 8), ("mix_norm_2", 8), ("conv_b_2", 8),
                                ("lru_ba_2", 8), ("lru_bx_2", 8), ("lru_lambda_2", 8), ("mem_norm_2", 8), ("ffn2_norm_2", 8)):
                    src = a[name][l].rearrange("w (r f) -> (w r) f", f=P) if name == "conv_w_2" else \
                        a[name][l].rearrange("(r f) -> r f", f=P)
                    pool.dma_start(prm_rows[at:at + n, 1 + l, :], src).then_inc(in_prm, 16)
                    at += n
            pool.dma_start(prm_rows[NORM2:NORM2 + 16, 3, :], a["norm2_g"].rearrange("l (r f) -> (l r) f", f=P)).then_inc(in_prm, 16)
            pool.dma_start(prm_rows[FINAL_N:FINAL_N + 8, 3, :], a["final_norm_2"].rearrange("(r f) -> r f", f=P)).then_inc(in_prm, 16)
            pool.dma_start(prm_rows[GN_G:GN_G + 16, 3, :], a["ret_gn_g"].rearrange("l (r f) -> (l r) f", f=P)).then_inc(in_prm, 16)
            for name, at in (("attn_q_norm", Q_N), ("attn_k_norm", K_N)):
                for half in range(2):
                    pool.dma_start(prm_rows[at:at + 1, 3, half * HD:(half + 1) * HD], a[name]).then_inc(in_prm, 16)
            pool.dma_start(soft_in[:, 0:8], a["ret_decay_logit"].rearrange("o d h -> o (d h)").broadcast_to((P, 8))).then_inc(in_prm, 16)
            pool.dma_start(sinks[:, 0:16], a["attn_sink"].broadcast_to((P, 16))).then_inc(in_prm, 16)
            pool.dma_start(sinks[:, 16:32], a["attn_sinks_2"].rearrange("l (o h) -> o (l h)", o=1).broadcast_to((P, 16))).then_inc(in_prm, 16)
            pool.dma_start(headsum[:].rearrange("p c h -> p (c h)"), const("headsum")).then_inc(in_attn, 16)
            pool.dma_start(headback[:].rearrange("p c h -> p (c h)"), const("headback")).then_inc(in_attn, 16)
            for name, t in (("partner", partner), ("cos_a", cos_a), ("sin_a", sin_a)):
                pool.dma_start(t[:, :], const(name)).then_inc(in_attn, 16)
            pool.dma_start(window[:].rearrange("p r k -> p (r k)"), const("window")).then_inc(in_attn, 16)
            pool.wait_ge(x_done, X_START)
            for n, name in enumerate(("ahead", "behind", "since")):
                pool.dma_start(rows[:, n * 512:(n + 1) * 512], const(name)).then_inc(in_tabs, 16)
            pool.wait_ge(acc_free, J["dn0"].done())
            for name, t in (("cos_r", cos_r), ("sin_r", sin_r)):
                pool.dma_start(t[:].rearrange("p c t -> p (c t)"), const(name)).then_inc(in_rope, 16)
            pool.wait_ge(d_ok, RH)
            tokens(rows, a["mem_2"], in_m)
            with pool.Fori(0, LAYERS2) as l:
                pool.wait_ge(acc_free, J["kvlru"].done(l))
                pool.tensor_tensor(GI[:], GI[:], XC[:], ALU.mult).then_inc(gx_ok, 1)
                for h in range(WH):
                    first, _ = attn_base("second", l)
                    if h >= 2:
                        pool.wait_ge(m_raw, first + 2 * (h - 2) + 2)
                    pool.wait_ge(in_const, 16 * 5)
                    pool.tensor_tensor(bias2[:, h % 2, :], alibi[:, :], slopes[:, h:h + 1].broadcast_to((P, 2 * S)), ALU.mult)\
                        .then_inc(bias_ok, 1)
                pool.wait_ge(scan_ok, 8 + l * 8)
                pool.tensor_tensor(XC[:], XR[:, :, 0:S], gy[:], ALU.mult).then_inc(lru_ok, 1)
                pool.wait_ge(lruh_ok, 1 + l)
                pool.tensor_tensor(h_lo[:, :, S:2 * S], XC[:], h_hi[:, :, S:2 * S], ALU.subtract).then_inc(lru_done, 1)

        @block.tensor
        def _(pe):
            def unit_ready(job, l, it, p):
                pe.wait_ge(lo_done, job.unit(l, it, p) + SLOTS + 1)

            def slot_free(job, l, it, b):
                pe.wait_ge(acc_free, job.block(l, it, b) + 1)

            def product(name, l=None, hi=h_hi, lo=h_lo, tok=slice(0, S), rows_of=None, needs=None):
                job = J[name]
                per = job.body // job.per

                def one(it):
                    for p in range(job.body):
                        b, u = divmod(p, per)
                        if u == 0:
                            slot_free(job, l, it, b)
                        if needs and needs(u):
                            pe.wait_ge(*needs(u))
                        unit_ready(job, l, it, p)
                        nk, s, last = job.unit_chunks[p], p % SLOTS, u == per - 1
                        tokens_major = rows_of if not callable(rows_of) else rows_of(b)
                        if tokens_major:
                            for n, r in enumerate(tokens_major):
                                packed = len(tokens_major) > 2
                                o = acc[:, b % 2, n // 2, (n % 2) * S:(n % 2) * S + S] if packed else acc[:, b % 2, n, 0:S]
                                for k in range(nk):
                                    x = slice(r * P, (r + 1) * P)
                                    kk = u * KCH + k
                                    for i, (xs, ws) in enumerate(((hi, w_hi), (hi, w_lo), (lo, w_hi))):
                                        mm = pe.matmul(o, xs[:, kk, x], ws[:, s, k, :],
                                                       start=(u == 0 and k == 0 and i == 0 and not (packed and n % 2)),
                                                       stop=(last and k == nk - 1 and i == 2), skip_group_check=packed)
                        else:
                            t = tok if not callable(tok) else tok(b)
                            for cb in range(2):
                                o = acc[:, b % 2, cb, 0:t.stop - t.start]
                                for k in range(nk):
                                    kk = u * KCH + k
                                    c = slice(cb * P, (cb + 1) * P)
                                    for i, (ws, xs) in enumerate(((w_hi, hi), (w_hi, lo), (w_lo, hi))):
                                        mm = pe.matmul(o, ws[:, s, k, c], xs[:, kk, t],
                                                       start=(u == 0 and k == 0 and i == 0),
                                                       stop=(last and k == nk - 1 and i == 2))
                        mm.then_inc(units_used, 1)

                if job.iters == 1:
                    one(0)
                else:
                    with pe.Fori(0, job.iters) as it:
                        one(it)

            def modulation_unit(name, it, p):
                job = J[name]
                b, u = divmod(p, 2)
                if u == 0:
                    slot_free(job, None, it, b)
                unit_ready(job, None, it, p)
                for k in range(KCH):
                    for i, ws in enumerate((w_hi, w_lo)):
                        mm = pe.matmul(acc[0:4, b % 2, 0, 0:S], c_parts[:, u * KCH + k, :], ws[:, p % SLOTS, k, :],
                                       start=(u == 0 and k == 0 and i == 0), stop=(u == 1 and k == KCH - 1 and i == 1))
                mm.then_inc(units_used, 1)

            def turn_chunk(name, c, dst):
                job = J[name]
                b = (c - (16 if name == "ada0b" else 0)) // 2
                pe.wait_ge(acc_free, job.taken(None, b // job.per, b % job.per))
                return pe.matmul(dst, ada_s[0:4, c * P:(c + 1) * P], sel[0:4, :], start=True, stop=True)

            def norm(n, half):
                pe.wait_ge(sq_ok, n + 1)
                src = nf if not half or isinstance(n, int) else nf_m
                for c in range(DC):
                    mm = pe.matmul(wk[:, 3, 0:S], ones[:, :], src[:, c, :], start=(c == 0), stop=(c == DC - 1))
                mm.then_inc(ss_ok, 1)

            def turn_in(src, s, bank0):
                pe.wait_ge(s, 32)
                for g in range(4):
                    dst = (wk[:, g] if bank0 == 0 else acc[:, g // 2, g % 2]).rearrange("p (c t) -> p c t", c=2)
                    for c in range(2):
                        for r in range(2):
                            f = r * D + (2 * g + c) * P
                            mm = pe.transpose(dst[:, c, r * P:(r + 1) * P], src[:, f:f + P], ident[:, :])
                    mm.then_inc(turned, 1)

            def attention(which, groups, l=None, beside=None, turns={}):
                first, pair0 = attn_base(which, l)
                again = which != "first"
                items = [(g, r) for g in range(len(groups)) for r in range(2)]
                for i in attn_steps(groups):
                    if i < len(items):
                        g, r = items[i]
                        G = groups[g]
                        if i >= 2 or again:
                            pe.wait_ge(m_raw, first + i - 1)
                        pe.matmul(sc_ps[i % 2][:, 0:G["nk"]], G["q"][r], G["k"], start=True, stop=True).then_inc(s_ok, 1)
                    j = i - T_LAG
                    if 0 <= j < len(items):
                        g, r = items[j]
                        G = groups[g]
                        pe.wait_ge(pn_ok, first + j + 1)
                        if j >= 2 or again:
                            pe.wait_ge(pt_ok, first + j - 1)
                        for t in range(G["nk"] // P):
                            mm = pe.transpose(pt_ps[j % 2][:, t * P:(t + 1) * P], G["probs"][:, j % 4, t * P:(t + 1) * P], ident[:, :])
                        for n, (name, c) in enumerate(turns.get(j, [])):
                            mm = turn_chunk(name, c, pt_ps[j % 2][:, S + 2 * n:S + 2 * n + 2])
                        mm.then_inc(t_ok, 1)
                    g = group_at(i, O_LAG, groups)
                    if g is not None:
                        G = groups[g]
                        tiles = G["nk"] // P
                        pe.wait_ge(pt_ok, first + 2 * g + 2)
                        if G["pair"] >= 2 or again:
                            pe.wait_ge(o_done, pair0 + G["pair"] - 1)
                        for t in range(tiles):
                            mm = pe.matmul(G["out"], G["v"][t], G["probs_t"][:, g % 2, t, :], start=(t == 0),
                                           stop=(t == tiles - 1), skip_group_check=True)
                        mm.then_inc(o_ok, 1)
                    if beside:
                        beside(i)

            def beside_first(i):
                for k in range(SIDE_UNITS):
                    if side_step(k) + 2 == i:
                        modulation_unit(*side_unit(k))

            pe.wait_ge(in_const, 16 * 5)
            pe.wait_ge(in_prm0, 64)
            pe.wait_ge(in_prm, 16 * PRM_DMAS)
            pe.wait_ge(setup, 2)
            for t, n in enumerate((P, CUR, CUR, PRM3)):
                mm = pe.transpose(wk[:, 3, t * P:t * P + n], prm_rows[0:n, t, :], ident[0:n, 0:n])
            mm.then_inc(prm_t, 1)
            turn_in(rows, in_x, 1)
            pe.wait_ge(x_done, 4)
            turn_in(rows_c, in_c, 1)
            pe.wait_ge(x_done, X_START)
            pe.wait_ge(c_lo_ok, 1)
            with pe.Fori(0, J["ada0a"].iters) as it:
                for p in range(J["ada0a"].body):
                    modulation_unit("ada0a", it, p)
            for c in range(16):
                mm = turn_chunk("ada0a", c, wk[:, 2, 2 * c:2 * c + 2])
            mm.then_inc(ada_sum, 1)
            norm(0, 0)
            norm(1, 1)
            both = slice(0, 2 * S)
            product("q0", tok=both, needs=lambda u: (h_ok, 16))
            product("kv0", tok=both, rows_of=lambda b: range(4) if b else None)
            pe.wait_ge(in_attn, 96)
            for c in range(10):
                pe.wait_ge(hsq, c + 1)
                pe.matmul(wk[0:20, 0, :], headsum[:, c, :], sq_b[:, c % 2, :], start=(c == 0), stop=(c == 9)).then_inc(hss, 1)
            pe.wait_ge(hrec, 1)
            part_ps = [wk[:, 3], acc[:, 0, 1]]
            for c in range(11):
                if c < 10:
                    if c >= 2:
                        pe.wait_ge(hn, c - 1)
                    pe.matmul(wk[:, 1 + c % 2, :], headback[0:20, c, :], sd_b[0:20, 0, :], start=True, stop=True).then_inc(hback, 1)
                if c:
                    b = c - 1
                    pe.wait_ge(hn, b + 1)
                    if b >= 2:
                        pe.wait_ge(hrot, b - 1)
                    pe.matmul(part_ps[b % 2][:, 0:S], partner[:, :], qk[:, b, 0:S], start=True, stop=True).then_inc(hperm, 1)
                beside_first(c - 11)
            pe.wait_ge(hqk, 10)
            pe.wait_ge(kd_ok, 8)
            pe.wait_ge(acc_free, J["kv0"].done())
            attention("first", groups_first(), None, beside_first, SIDE_TURNS)
            product("wo0", tok=both, needs=lambda u: (o_done, PAIRS0))
            norm(2, 0)
            norm(3, 1)
            product("gu0", tok=both, needs=lambda u: (h_ok, 8 * 4))
            product("dn0", hi=hid_hi, lo=hid_lo, tok=both, needs=lambda u: (hid_ok, 11))
            norm(4, 0)
            norm(5, 1)
            product("rq", needs=lambda u: (h_ok, 8 * 4 + 4 * u + 4))
            product("rk", tok=both, needs=lambda u: (h_ok, 8 * 6))
            product("rv", rows_of=range(4))
            product("rg")

            def scores(h):
                pe.wait_ge(rope_ok, 8)
                for kt in range(4):
                    if h and kt % 2 == 0:
                        pe.wait_ge(rp_ok, 2 * (h - 1) + kt // 2 + 1)
                    for d in range(2):
                        mm = pe.matmul(wk[:, kt // 2, (kt % 2) * S:(kt % 2) * S + S], r_k[:, 2 * h + d, kt * P:(kt + 1) * P],
                                       r_q[:, 2 * h + d, :], start=(d == 0), stop=(d == 1))
                    if kt % 2:
                        mm.then_inc(rs_ok, 1)

            def values(h):
                pe.wait_ge(acc_free, J["rv"].done())
                pe.wait_ge(rp_ok, 2 * h + 2)
                for r in range(2):
                    if h:
                        pe.wait_ge(y_ok, 2 * (h - 1) + r + 1)
                    for kt in range(4):
                        mm = pe.matmul(wk[:, 2 + r, :], r_p[:, kt, r * P:(r + 1) * P], r_v[:, kt, RV * h:RV * (h + 1)],
                                       start=(kt == 0), stop=(kt == 3))
                    mm.then_inc(ro_ok, 1)

            def turn_y(h):
                if h:
                    pe.wait_ge(z_ok, h)
                else:
                    pe.wait_ge(acc_free, J["rg"].block(None, J["rg"].iters - 1, 1) + 3)
                for r in range(2):
                    pe.wait_ge(y_ok, 2 * h + r + 1)
                    for c in range(4):
                        o = acc[:, 0, c // 2, (c % 2) * S + r * P:(c % 2) * S + (r + 1) * P]
                        mm = pe.transpose(o, r_y[:, r, c * P:(c + 1) * P], ident[:, :])
                mm.then_inc(yt_ok, 1)

            for h in range(RH):
                scores(h)
                if h:
                    turn_y(h - 1)
                values(h)
            turn_y(RH - 1)
            product("rwo", hi=z_hi, lo=z_lo, needs=lambda u: (z_done, RH))
            norm(6, 0)
            product("gu1", needs=lambda u: (h_ok, 8 * 6 + 4 * u + 4))
            product("dn1", hi=hid_hi, lo=hid_lo, needs=lambda u: (hid_ok, 22))
            pe.wait_ge(acc_free, J["dn1"].done())
            turn_in(rows, in_m, 1)
            pe.wait_ge(x_done, X_MEM)

            mem = slice(S, 2 * S)
            with pe.Fori(0, LAYERS2) as l:
                n0 = NORMS1 + l * 4
                norm(n0, 0)
                product("gua", l, needs=lambda u: (h_ok, 8 * NORMS1 + 4 * u + 4 + l * 32))
                norm(n0 + 1, 1)
                product("dna", l, hi=hid_hi, lo=hid_lo, needs=lambda u: (hid_ok, 33 + l * 22))
                product("memk", l, tok=mem, needs=lambda u: (h_ok, 8 * (NORMS1 + 2) + l * 32))
                norm(n0 + 2, 0)
                product("memv", l, rows_of=range(2, 4))
                product("xr", l, needs=lambda u: (h_ok, 8 * (NORMS1 + 2) + 4 * u + 4 + l * 32))
                product("yr", l)
                product("gates", l)
                job = J["kvlru"]
                slot_free(job, l, 0, 0)
                slot_free(job, l, 0, 1)
                for p in range(2):
                    unit_ready(job, l, 0, p)
                    for cb in range(2):
                        for k in range(KCH):
                            for i, (ws, xs) in enumerate(((w_hi, h_hi), (w_hi, h_lo), (w_lo, h_hi))):
                                mm = pe.matmul(acc[:, cb, 0, 0:S], ws[:, p, k, cb * P:(cb + 1) * P], xs[:, p * KCH + k, 0:S],
                                               start=(p == 0 and k == 0 and i == 0), stop=(p == 1 and k == KCH - 1 and i == 2))
                    mm.then_inc(units_used, 1)
                pe.wait_ge(xc_ok, 1 + l)
                for p in range(2, 4):
                    unit_ready(job, l, 0, p)
                    wh, wl = [w[:, p].rearrange("p k n -> p (k n)") for w in (w_hi, w_lo)]
                    for c in range(DC):
                        b = 2 * (p - 1) + c // 4
                        if c % 4 == 0:
                            slot_free(job, l, 0, b)
                        o = acc[:, b % 2, (c % 4) // 2, (c % 2) * S:(c % 2) * S + S]
                        for i, (w, x) in enumerate(((wh, h_hi), (wh, h_lo), (wl, h_hi))):
                            mm = pe.matmul(o, w[:, c * P:(c + 1) * P], x[:, c, mem], start=(i == 0), stop=(i == 2))
                    mm.then_inc(units_used, 1)
                product("q", l)
                product("cq", l)
                pe.wait_ge(acc_free, J["cq"].done(l))
                for r in range(2):
                    mm = pe.transpose(wk[:, 3, r * P:(r + 1) * P], v_T[:, r * P:(r + 1) * P], ident[:, :])
                mm.then_inc(vt_ok, 1)
                pe.wait_ge(v2_ok, 1 + l)
                attention("second", groups_window() + groups_memory(), l)
                _, pair0 = attn_base("second", l)
                product("attn_out", l, needs=lambda u: (o_done, pair0 + PAIRS_WIN + PAIRS_MEM))
                product("lru_out", l, tok=mem, needs=lambda u: (lru_done, 1 + l))
                product("mem_out", l, hi=h_hi[:, 4:8, :], lo=h_lo[:, 4:8, :],
                        needs=None)
                product("w_out", l, tok=mem, needs=lambda u: (mg_done, 4 + l * 4))
                norm(n0 + 3, 0)
                product("gub", l, needs=lambda u: (h_ok, 8 * (NORMS1 + 3) + 4 * u + 4 + l * 32))
                product("dnb", l, hi=hid_hi, lo=hid_lo, needs=lambda u: (hid_ok, 44 + l * 22))
            norm(NORM_LAST, 0)
            pe.wait_ge(nf_ok, 8 * (NORM_LAST + 1))
            for r in range(2):
                for c in range(DC):
                    g = 2 * r + c // 4
                    mm = pe.transpose(wk[:, g, (c % 4) * P:(c % 4 + 1) * P] if g < 3 else acc[:, 0, 0, (c % 4) * P:(c % 4 + 1) * P],
                                      nf[:, c, r * P:(r + 1) * P], ident[:, :])
                    if c % 4 == 3:
                        mm.then_inc(fin_t, 1)

        @block.scalar
        def _(act):
            def split(job, l, it, p):
                s, nk = p % SLOTS, job.unit_chunks[p]
                act.wait_ge(load[s], job.loaded(l, it, p))
                act.wait_ge(units_used, job.unit(l, it, p) + 1)
                act.copy(w_hi[:, s, 0:nk, :], raw[:, s, 0:nk, :]).then_inc(hi_done, 1)

            def split_diag(job, l, p):
                act.wait_ge(load[p], job.loaded(l, 0, p))
                act.wait_ge(zero_ok, 1 + (p - 2) + l * 2)
                src = raw[:, p, 0:2, :].rearrange("p k n -> p (k n)").rearrange("p (c j) -> p c j", j=64)
                dst = w_hi[:, p].rearrange("p k n -> p (k n)").rearrange("p (c j) -> p c j", j=P)
                act.copy(dst[0:64, :, 0:64], src[0:64])
                act.copy(dst[64:128, :, 64:128], src[64:128]).then_inc(hi_done, 1)

            def block_done(job, l, it, b):
                act.wait_ge(units_used, job.unit(l, it, job.ends[b]) + SLOTS + 1)

            def ending(job, e):
                return [b for b in range(job.per) if job.ends[b] == e]

            def step(name, evac, l, it, p):
                job = J[name]
                if name == "kvlru" and p >= 2:
                    split_diag(job, l, p)
                else:
                    split(job, l, it, p)

            def evacuate(name, evac, l, it, e):
                for b in ending(J[name], e):
                    if evac:
                        block_done(J[name], l, it, b)
                        evac(l, it, b)

            def head(name, l=None, prev=None, prev_evac=None):
                for p in range(LAG):
                    step(name, None, l, 0, p)
                    if prev:
                        evacuate(prev, prev_evac, l, J[prev].iters - 1, J[prev].body + p - LAG)

            def rest(name, evac, l=None, table=None):
                job = J[name]
                if table:
                    act.preload_act_table(table)
                for p in range(LAG, job.body):
                    step(name, evac, l, 0, p)
                    evacuate(name, evac, l, 0, p - LAG)
                if job.iters > 1:
                    with act.Fori(1, job.iters) as it:
                        for p in range(job.body):
                            step(name, evac, l, it, p)
                            if p < LAG:
                                evacuate(name, evac, l, it - 1, job.body + p - LAG)
                            else:
                                evacuate(name, evac, l, it, p - LAG)

            def tail(prev, evac, l=None):
                for p in range(LAG):
                    evacuate(prev, evac, l, J[prev].iters - 1, J[prev].body + p - LAG)

            def squares(n, half, x_from):
                t = slice(half * S, half * S + S)
                act.preload_act_table(ACT.Sqrt)
                act.wait_ge(*x_from)
                if not (isinstance(n, int) and n == 0):
                    act.wait_ge(h_ok, 8 * n)
                act.activation(normed_in(n, half)[:], xT[:, :, t], ACT.Square).then_inc(sq_ok, 1)

            def normed_in(n, half):
                return nf if not half or isinstance(n, int) else nf_m

            def norm(n, half, x_from, shift=None, split_out=True, layer=0):
                squares(n, half, x_from)
                deviations(n, half, shift, split_out, layer)

            def deviations(n, half, shift=None, split_out=True, layer=0):
                t = slice(half * S, half * S + S)
                src = normed_in(n, half)
                act.wait_ge(ss_ok, n + 1)
                act.activation(std[:], wk[:, 3, 0:S], ACT.Sqrt, bias=eps[:, 0:1], scale=1.0 / D).then_inc(std_ok, 1)
                if split_out:
                    for c in range(DC):
                        act.wait_ge(nf_ok, n * 8 + c + 1)
                        if shift is not None:
                            act.activation(h_hi[:, c, t], src[:, c, :], ACT.Identity, bias=mod[:, layer, shift * 8 + c, half:half + 1])\
                                .then_inc(nh_ok, 1)
                        else:
                            act.copy(h_hi[:, c, t], src[:, c, :]).then_inc(nh_ok, 1)

            def attention(which, groups, l=None, beside=None, turns={}):
                first, pair0 = attn_base(which, l)
                again = which != "first"
                group0 = first // 2 if which == "first" else ITEMS0 // 2 + l * ((ITEMS_WIN + ITEMS_MEM) // 2)
                items = [(g, r) for g in range(len(groups)) for r in range(2)]
                for i in attn_steps(groups):
                    if beside:
                        beside(i)
                    if i < len(items):
                        g, r = items[i]
                        G = groups[g]
                        act.wait_ge(m_ok, first + i + 1)
                        pr = G["probs"][:, i % 4, 0:G["nk"]]
                        act.activation(pr, pr, ACT.Exp, bias=snm[:, i % 8:i % 8 + 1], accum_out=ssum[:, i % 8:i % 8 + 1])\
                            .then_inc(p_ok, 1)
                        if G["sink"] is not None:
                            act.activation(ses[:, i % 8:i % 8 + 1], G["sink"], ACT.Exp, bias=snm[:, i % 8:i % 8 + 1]).then_inc(p_ok, 1)
                        else:
                            act.activation(ses[:, i % 8:i % 8 + 1], nomask[:, 0:1], ACT.Copy).then_inc(p_ok, 1)
                    j = i - T_LAG
                    if 0 <= j < len(items):
                        g, r = items[j]
                        G = groups[g]
                        tiles = G["nk"] // P
                        act.wait_ge(t_ok, first + j + 1)
                        if g >= 2 or again:
                            act.wait_ge(o_ok, group0 + g - 1)
                        for n, (name, c) in enumerate(turns.get(j, [])):
                            act.copy(mod[:, SIDE.index(name), c, :], pt_ps[j % 2][:, S + 2 * n:S + 2 * n + 2])
                        act.copy(G["probs_t"][:, g % 2, 0:tiles, r * P:(r + 1) * P],
                                 pt_ps[j % 2][:, 0:tiles * P].rearrange("p (t q) -> p t q", q=P)).then_inc(pt_ok, 1)
                    g = group_at(i, H_LAG, groups)
                    if g is not None and groups[g]["last"]:
                        act.wait_ge(o_ok, group0 + g + 1)
                        act.copy(groups[g]["hi"], groups[g]["acc"]).then_inc(o_hi_ok, 1)

            def beside_first(i):
                for k in range(SIDE_UNITS):
                    if side_step(k) == i:
                        name, it, p = side_unit(k)
                        split(J[name], None, it, p)
                for k in range(1, SIDE_UNITS, 2):
                    name, it, p = side_unit(k)
                    if side_step(k) + 3 == i:
                        c = 2 * (it * J[name].per + p // 2)
                        if name == "ada1" and c >= 16:
                            item = [n for n, cs in SIDE_TURNS.items() if ("ada0b", c + 1) in cs][0]
                            act.wait_ge(t_ok, item + 1)
                        block_done(J[name], None, it, p // 2)
                        c += 16 if name == "ada0b" else 0
                        act.copy(ada_s[0:4, c * P:(c + 2) * P], acc[0:4, p // 2 % 2, 0, 0:S]).then_inc(acc_free, 1)

            def q0(l, it, b):
                act.copy(qk[:, bass.ts(it, 4), :][:, 2 * b:2 * b + 2, :], acc[:, b % 2]).then_inc(acc_free, 1)

            def kv0(l, it, b):
                if b == 0:
                    act.copy(qk[:, 8:10, :], acc[:, 0]).then_inc(acc_free, 1)
                else:
                    act.copy(v_tok[:].rearrange("p t n -> p (t n)"), acc[:, 1].rearrange("p a n -> p (a n)"))\
                        .then_inc(acc_free, 1)

            def gate_up(name, T, n0):
                def evac(l, it, b):
                    n = n0 + it + (l * 22 if l is not None else 0)
                    buf = act_buf[:, :, 0:T]
                    if b == 0:
                        if not (isinstance(n, int) and n == 0):
                            act.wait_ge(hid_ok, n)
                        act.activation(buf, acc[:, 0, :, 0:T], ACT.Silu).then_inc(acc_free, 1)
                    else:
                        act.wait_ge(acc_free, J[name].taken(l, it, 1))
                        act.copy(hid_hi[:, bass.ts(it, 2), 0:T], buf).then_inc(hid_hi_ok, 1)
                return evac

            def rope(n0, keys):
                def evac(l, it, b):
                    o = acc[:, b % 2]
                    n = n0 + 2 * it + b
                    if keys:
                        act.copy(r_k[:, bass.ts(it, 4), S:2 * S][:, 2 * b:2 * b + 2, :], o[:, :, S:2 * S])
                    if not (isinstance(n, int) and n == 0):
                        act.wait_ge(rope_ok, n)
                    act.copy(swp[0:64], o[64:128, :, 0:S])
                    act.copy(swp[64:128], o[0:64, :, 0:S]).then_inc(swp_ok, 1)
                return evac

            def rv(l, it, b):
                act.wait_ge(rope_ok, 8)
                act.copy(r_v[:, :, bass.ts(it, 2 * COLS)][:, :, b * COLS:(b + 1) * COLS],
                         acc[:, b % 2].rearrange("p a (r n) -> p (a r) n", r=2)).then_inc(acc_free, 1)

            def rg(l, it, b):
                act.activation(r_g[:, bass.ts(it, 4), :][:, 2 * b:2 * b + 2, :], acc[:, b % 2, :, 0:S], ACT.Silu)\
                    .then_inc(acc_free, 1)

            def memk(l, it, b):
                act.copy(km[:, 2 * b:2 * b + 2, :], acc[:, b, :, 0:S]).then_inc(acc_free, 1)

            def memv(l, it, b):
                act.copy(vm[:, :, b * COLS:(b + 1) * COLS], acc[:, b, :, 0:S]).then_inc(acc_free, 1)

            def xr(l, it, b):
                act.copy(XR[:, bass.ts(it, 4), 4:4 + S][:, 2 * b:2 * b + 2, :], acc[:, b, :, 0:S]).then_inc(acc_free, 1)

            def yr(l, it, b):
                act.activation(gy[:, bass.ts(it, 4), :][:, 2 * b:2 * b + 2, :], acc[:, b, :, 0:S], ACT.Gelu_apprx_tanh)\
                    .then_inc(acc_free, 1)

            def gates_e(l, it, b):
                for cb in range(2):
                    col = cur[:, bass.ts(it, 4)][:, 2 * b + cb:2 * b + cb + 1]
                    ins = act.activation(gates[:, bass.ts(it, 4), :][:, 2 * b + cb, :], acc[:, b, cb, 0:S], ACT.Sigmoid, bias=col)
                ins.then_inc(acc_free, 1)

            def kvlru(l, it, b):
                if b == 0:
                    for g in range(2):
                        for half in range(2):
                            ins = act.copy(k_d[64 * half:64 * half + 64, g, :], acc[64 * g:64 * g + 64, 0, 0, 0:S])
                    ins.then_inc(acc_free, 1)
                elif b == 1:
                    act.copy(v_T[:], acc[:, 1, 0, 0:S]).then_inc(acc_free, 1)
                else:
                    dst, bias = (R, BA) if b < 4 else (GI, BX)
                    for c in range(4):
                        cc = 4 * (b % 2) + c
                        ins = act.activation(dst[:, cc, :], acc[:, b % 2, c // 2, (c % 2) * S:(c % 2) * S + S], ACT.Sigmoid,
                                             bias=cur[:, bias + cc:bias + cc + 1])
                    ins.then_inc(acc_free, 1)

            def q_e(l, it, b):
                act.copy(q_2[:, 2 * b:2 * b + 2, :], acc[:, b, :, 0:S]).then_inc(acc_free, 1)

            def cq_e(l, it, b):
                act.copy(cq_2[:, 2 * b:2 * b + 2, :], acc[:, b, :, 0:S]).then_inc(acc_free, 1)

            def mem_out(l, it, b):
                act.wait_ge(mg_ok, 1 + b + l * 4)
                act.copy(h_hi[:, 2 * b:2 * b + 2, S:2 * S], gates[:, 2 * b:2 * b + 2, :]).then_inc(mgh_ok, 1)

            act.wait_ge(setup, 2)
            act.wait_ge(prm_ok, 3)
            act.activation(c_act[:], prm[:, 0, C_COL:C_COL + 16], ACT.Silu).then_inc(c_ok, 1)
            act.wait_ge(c_ok, 1)
            cc = c_act[:].rearrange("p (w k) -> p k w", w=2)
            act.copy(c_parts[:].rearrange("p k (w s) -> p k w s", s=2)[:, :, :, 0], cc).then_inc(c_hi_ok, 1)
            head("ada0a")
            act.wait_ge(soft_v, 1)
            act.activation(soft_e[:], soft_t[:], ACT.Exp).then_inc(soft_a, 1)
            rest("ada0a", None)
            head("q0", None, "ada0a", None)
            norm(0, 0, (x_done, X_START), 0)
            norm(1, 1, (x_done, X_START), 0)
            rest("q0", q0)
            head("kv0", None, "q0", q0)
            rest("kv0", kv0)
            tail("kv0", kv0)
            act.preload_act_table(ACT.Sqrt)
            for c in range(10):
                act.wait_ge(acc_free, J["kv0"].taken(None, 0, 0))
                if c >= 2:
                    act.wait_ge(hss, c - 1)
                act.activation(sq_b[:, c % 2, :], qk[:, c, :], ACT.Square).then_inc(hsq, 1)
            act.wait_ge(hss, 10)
            act.activation(sd_b[0:20, 0, :], wk[0:20, 0, :], ACT.Sqrt, bias=eps[0:20, 0:1], scale=1.0 / HD).then_inc(hstd, 1)
            for i in range(-SIDE_START - 1, 0):
                beside_first(i)
            for c in range(2):
                act.wait_ge(hqk, 9 + c)
                for g in range(2):
                    for half in range(2):
                        act.copy(k_dup[64 * half:64 * half + 64, 2 * c + g, :], qk[64 * g:64 * g + 64, 8 + c, :]).then_inc(kd_ok, 1)
            attention("first", groups_first(), None, beside_first, SIDE_TURNS)
            head("wo0")
            rest("wo0", None)
            head("gu0", None, "wo0", None)
            norm(2, 0, (acc_free, J["wo0"].done()), 3)
            norm(3, 1, (acc_free, J["wo0"].done()), 3)
            rest("gu0", gate_up("gu0", 2 * S, 0), None, ACT.Silu)
            head("dn0", None, "gu0", gate_up("gu0", 2 * S, 0))
            rest("dn0", None)
            head("rq", None, "dn0", None)
            norm(4, 0, (acc_free, J["dn0"].done()), 0, layer=1)
            norm(5, 1, (acc_free, J["dn0"].done()), 0, layer=1)
            rest("rq", rope(0, False))
            head("rk", None, "rq", rope(0, False))
            rest("rk", rope(4, True))
            head("rv", None, "rk", rope(4, True))
            rest("rv", rv)
            head("rg", None, "rv", rv)
            rest("rg", rg, None, ACT.Silu)
            head("rwo", None, "rg", rg)

            def decays(h):
                act.wait_ge(dx_in, h + 1)
                act.activation(r_d[:, 0:2, :], r_d[:, 0:2, :], ACT.Exp).then_inc(dx_e, 1)
                act.activation(r_d[:, 2:4, :], since, ACT.Exp, scale=decay[:, 0, h:h + 1]).then_inc(dc_e, 1)
                if h:
                    act.wait_ge(z_done, h)
                act.activation(act_buf[:, 0, :].rearrange("p (m n) -> p m n", m=2), since, ACT.Exp,
                               scale=decay[:, 1, 4 + h:5 + h], bias=decay[:, 2, 4 + h:5 + h]).then_inc(dc_e, 1)

            def gn(h):
                for r in range(2):
                    act.wait_ge(mv_ok, 2 * h + r + 1)
                    act.activation(gstd[:, r:r + 1], mv[:, r, 1:2], ACT.Sqrt, bias=eps[:, 0:1]).then_inc(gs_ok, 1)

            def z_high(h):
                act.wait_ge(z_ok, h + 1)
                act.copy(z_hi[:, 4 * h:4 * h + 4, :], act_buf[:].rearrange("p a (b t) -> p (a b) t", b=2)).then_inc(zh_ok, 1)

            act.wait_ge(in_tabs, 48)
            for h in range(RH):
                decays(h)
                gn(h)
                z_high(h)
            rest("rwo", None)
            head("gu1", None, "rwo", None)
            norm(6, 0, (acc_free, J["rwo"].done()), 3, layer=1)
            rest("gu1", gate_up("gu1", S, 11), None, ACT.Silu)
            head("dn1", None, "gu1", gate_up("gu1", S, 11))
            rest("dn1", None)
            tail("dn1", None)

            with act.Fori(0, LAYERS2) as l:
                n0 = NORMS1 + l * 4
                head("gua", l)
                norm(n0, 0, (acc_free, J["gua"].taken(l, 0, 0) - 1))
                rest("gua", gate_up("gua", S, 22), l, ACT.Silu)
                head("dna", l, "gua", gate_up("gua", S, 22))
                norm(n0 + 1, 1, (x_done, X_MEM))
                rest("dna", None, l)
                head("memk", l, "dna", None)
                squares(n0 + 2, 0, (acc_free, J["dna"].done(l)))
                rest("memk", memk, l)
                head("memv", l, "memk", memk)
                deviations(n0 + 2, 0)
                rest("memv", memv, l)
                head("xr", l, "memv", memv)
                rest("xr", xr, l)
                head("yr", l, "xr", xr)
                rest("yr", yr, l, ACT.Gelu_apprx_tanh)
                head("gates", l, "yr", yr)
                act.wait_ge(conv_ok, 32 + l * 32)
                act.copy(h_hi[:, :, S:2 * S], XC[:]).then_inc(xch_ok, 1)
                rest("gates", gates_e, l, ACT.Sigmoid)
                head("kvlru", l, "gates", gates_e)
                rest("kvlru", kvlru, l)
                head("q", l, "kvlru", kvlru)
                for c in range(DC):
                    act.activation(XR[:, c, 0:S], R[:, c, :], ACT.Exp, scale=cur[:, CUR + 8 + c:CUR + 9 + c]).then_inc(e2_ok, 1)
                rest("q", q_e, l)
                head("cq", l, "q", q_e)
                act.wait_ge(cl_ok, 1 + l)
                act.activation(XR[:, :, 0:S], XR[:, :, 0:S], ACT.Sqrt, scale=-1.0, bias=ones[:, 0:1]).then_inc(mu_ok, 1)
                for c in range(DC):
                    act.activation(R[:, c, :], R[:, c, :], ACT.Exp, scale=cur[:, CUR + c:CUR + c + 1]).then_inc(e2_ok, 1)
                rest("cq", cq_e, l)
                head("attn_out", l, "cq", cq_e)

                def recurrence_high(i):
                    if i == 2 * WH:
                        act.wait_ge(lru_ok, 1 + l)
                        act.copy(h_hi[:, :, S:2 * S], XC[:]).then_inc(lruh_ok, 1)
                attention("second", groups_window() + groups_memory(), l, recurrence_high)
                rest("attn_out", None, l)
                head("lru_out", l, "attn_out", None)
                rest("lru_out", None, l)
                head("mem_out", l, "lru_out", None)
                rest("mem_out", mem_out, l)
                head("w_out", l, "mem_out", mem_out)
                rest("w_out", None, l)
                head("gub", l, "w_out", None)
                norm(n0 + 3, 0, (acc_free, J["w_out"].done(l)))
                rest("gub", gate_up("gub", S, 33), l, ACT.Silu)
                head("dnb", l, "gub", gate_up("gub", S, 33))
                rest("dnb", None, l)
                tail("dnb", None, l)
            norm(NORM_LAST, 0, (acc_free, J["dnb"].done(LAYERS2 - 1)), split_out=False)

        @block.vector
        def _(dve):
            def split(job, l, it, p):
                s, nk = p % SLOTS, job.unit_chunks[p]
                dve.wait_ge(hi_done, job.unit(l, it, p) + 1)
                dve.tensor_tensor(w_lo[:, s, 0:nk, :], raw[:, s, 0:nk, :], w_hi[:, s, 0:nk, :], ALU.subtract).then_inc(lo_done, 1)

            def split_diag(job, l, p):
                dve.wait_ge(units_used, job.unit(l, 0, p) + 1)
                dve.memset(w_hi[:, p].bitcast(F32), 0.0).then_inc(zero_ok, 1)
                dve.memset(w_lo[:, p].bitcast(F32), 0.0).then_inc(clear_ok, 1)
                src = raw[:, p, 0:2, :].rearrange("p k n -> p (k n)").rearrange("p (c j) -> p c j", j=64)
                hi, lo = [w[:, p].rearrange("p k n -> p (k n)").rearrange("p (c j) -> p c j", j=P) for w in (w_hi, w_lo)]
                dve.wait_ge(hi_done, job.unit(l, 0, p) + 1)
                dve.wait_ge(clear_ok, 1 + (p - 2) + l * 2)
                dve.tensor_tensor(lo[0:64, :, 0:64], src[0:64], hi[0:64, :, 0:64], ALU.subtract)
                dve.tensor_tensor(lo[64:128, :, 64:128], src[64:128], hi[64:128, :, 64:128], ALU.subtract).then_inc(lo_done, 1)

            def block_done(job, l, it, b):
                dve.wait_ge(units_used, job.unit(l, it, job.ends[b]) + SLOTS + 1)

            def ending(job, e):
                return [b for b in range(job.per) if job.ends[b] == e]

            def step(name, l, it, p):
                job = J[name]
                if name == "kvlru" and p >= 2:
                    split_diag(job, l, p)
                else:
                    split(job, l, it, p)

            def evacuate(name, evac, l, it, e):
                for b in ending(J[name], e):
                    if evac:
                        block_done(J[name], l, it, b)
                        evac(l, it, b)

            def head(name, l=None, prev=None, prev_evac=None):
                for p in range(LAG):
                    step(name, l, 0, p)
                    if prev:
                        evacuate(prev, prev_evac, l, J[prev].iters - 1, J[prev].body + p - LAG)

            def rest(name, evac, l=None):
                job = J[name]
                for p in range(LAG, job.body):
                    step(name, l, 0, p)
                    evacuate(name, evac, l, 0, p - LAG)
                if job.iters > 1:
                    with dve.Fori(1, job.iters) as it:
                        for p in range(job.body):
                            step(name, l, it, p)
                            if p < LAG:
                                evacuate(name, evac, l, it - 1, job.body + p - LAG)
                            else:
                                evacuate(name, evac, l, it, p - LAG)

            def tail(prev, evac, l=None):
                for p in range(LAG):
                    evacuate(prev, evac, l, J[prev].iters - 1, J[prev].body + p - LAG)

            def norm(n, half, gain_of, shift=None, split_out=True, layer=0):
                t = slice(half * S, half * S + S)
                nf_n = nf if not half or isinstance(n, int) else nf_m
                dve.wait_ge(std_ok, n + 1)
                dve.reciprocal(rstd[:], std[:]).then_inc(rstd_ok, 1)
                dve.wait_ge(rstd_ok, n + 1)

                def normed(c):
                    dve.scalar_tensor_tensor(nf_n[:, c, :], xT[:, c, t], gain_of(c), rstd[:], ALU.mult, ALU.mult).then_inc(nf_ok, 1)

                def low(c):
                    dve.wait_ge(nh_ok, n * 8 + c + 1)
                    if shift is not None:
                        dve.scalar_tensor_tensor(h_lo[:, c, t], nf_n[:, c, :], mod[:, layer, shift * 8 + c, half:half + 1], h_hi[:, c, t],
                                                 ALU.add, ALU.subtract).then_inc(h_ok, 1)
                    else:
                        dve.tensor_tensor(h_lo[:, c, t], nf_n[:, c, :], h_hi[:, c, t], ALU.subtract).then_inc(h_ok, 1)

                for c in range(DC):
                    normed(c)
                    if c and split_out:
                        low(c - 1)
                if split_out:
                    low(DC - 1)

            def attention(which, groups, l=None, beside=None):
                first, pair0 = attn_base(which, l)
                again = which != "first"
                items = [(g, r) for g in range(len(groups)) for r in range(2)]
                for i in attn_steps(groups):
                    if i < len(items):
                        g, r = items[i]
                        G = groups[g]
                        c = i % 8
                        dve.wait_ge(s_ok, first + i + 1)
                        if i >= 4 or again:
                            dve.wait_ge(t_ok, first + i - 3)
                        if G.get("bias"):
                            dve.wait_ge(bias_ok, 1 + g + l * WH)
                        if again:
                            dve.memset(passed[:, c:c + 1], 0.0)
                        dve.tensor_tensor_reduce(G["probs"][:, i % 4, 0:G["nk"]], sc_ps[i % 2][:, 0:G["nk"]], G["mask"][r], G["scale"],
                                                 -3.0e38, ALU.add, ALU.max, smx[:, c:c + 1]).then_inc(m_raw, 1)
                        dve.wait_ge(m_raw, first + i + 1)
                        if G["sink"] is not None:
                            dve.tensor_scalar(snm[:, c:c + 1], smx[:, c:c + 1], G["sink"], -1.0, ALU.max, ALU.mult).then_inc(m_ok, 1)
                        else:
                            dve.tensor_scalar(snm[:, c:c + 1], smx[:, c:c + 1], -1.0, None, ALU.mult).then_inc(m_ok, 1)
                    j = i - N_LAG
                    if 0 <= j < len(items):
                        g, r = items[j]
                        G = groups[g]
                        c = j % 8
                        dve.wait_ge(p_ok, first * 2 + 2 * j + 2)
                        dve.tensor_tensor(sden[:, c:c + 1], ssum[:, c:c + 1], ses[:, c:c + 1], ALU.add).then_inc(den_ok, 1)
                        dve.wait_ge(den_ok, first + j + 1)
                        dve.reciprocal(srec[:, c:c + 1], sden[:, c:c + 1]).then_inc(rec_ok, 1)
                        dve.wait_ge(rec_ok, first + j + 1)
                        pr = G["probs"][:, j % 4, 0:G["nk"]]
                        dve.tensor_scalar(pr, pr, srec[:, c:c + 1], None, ALU.mult).then_inc(pn_ok, 1)
                    g = group_at(i, L_LAG, groups)
                    if g is not None and groups[g]["last"]:
                        G = groups[g]
                        dve.wait_ge(o_hi_ok, pair0 + G["pair"] + 1)
                        dve.tensor_tensor(G["lo"], G["acc"], G["hi"], ALU.subtract).then_inc(o_done, 1)
                    if beside:
                        beside(i)

            def beside_first(i):
                for k in range(SIDE_UNITS):
                    if side_step(k) == i:
                        name, it, p = side_unit(k)
                        split(J[name], None, it, p)

            def ada(l, it, b):
                dve.tensor_copy(ada_s[0:4, bass.ts(it, 2 * COLS)][:, b * COLS:(b + 1) * COLS], acc[0:4, b, 0, 0:S]).then_inc(acc_free, 1)

            def residual(layer, gate, both, bpi):
                def evac(l, it, b):
                    x = xT[:, bass.ts(it, 2 * bpi), :]
                    for cb in range(2):
                        for half in range(2 if both else 1):
                            t = slice(half * S, half * S + S)
                            col = mod[:, layer, bass.ds(gate * 8 + it * 2 * bpi + 2 * b + cb, 1), half]
                            ins = dve.scalar_tensor_tensor(x[:, 2 * b + cb, t], acc[:, b % 2, cb, t], col, x[:, 2 * b + cb, t],
                                                           ALU.mult, ALU.add)
                    ins.then_inc(acc_free, 1)
                return evac

            def residual2(factor, bpi):
                def evac(l, it, b):
                    x = xT[:, bass.ts(it, 2 * bpi), 0:S][:, 2 * b:2 * b + 2, :]
                    dve.scalar_tensor_tensor(x, acc[:, b % 2, :, 0:S], factor, x, ALU.mult, ALU.add)\
                        .then_inc(acc_free, 1)
                return evac

            def gate_up(name, T, n0):
                def evac(l, it, b):
                    if b == 0:
                        return
                    n = n0 + it + (l * 22 if l is not None else 0)
                    buf = act_buf[:, :, 0:T]
                    dve.wait_ge(acc_free, J[name].taken(l, it, 0))
                    dve.tensor_tensor(buf, buf, acc[:, 1, :, 0:T], ALU.mult).then_inc(acc_free, 1)
                    dve.wait_ge(hid_hi_ok, n + 1)
                    dve.tensor_tensor(hid_lo[:, bass.ts(it, 2), 0:T], buf, hid_hi[:, bass.ts(it, 2), 0:T], ALU.subtract).then_inc(hid_ok, 1)
                return evac

            def rope(n0, dst):
                def evac(l, it, b):
                    n = n0 + 2 * it + b
                    dve.wait_ge(swp_ok, n + 1)
                    dve.tensor_tensor(rot[:], acc[:, b % 2, :, 0:S], cos_r[:], ALU.mult).then_inc(acc_free, 1)
                    dve.tensor_tensor(swp[:], swp[:], sin_r[:], ALU.mult).then_inc(rot_ok, 1)
                    dve.wait_ge(rot_ok, n + 1)
                    dve.tensor_tensor(dst[:, bass.ts(it, 4), 0:S][:, 2 * b:2 * b + 2, :], rot[:], swp[:], ALU.add).then_inc(rope_ok, 1)
                return evac

            def branch(i):
                job = J[("attn_out", "lru_out", "mem_out")[i]]

                def evac(l, it, b):
                    bb = (lambda k: gates[:, 8 * k + 2 * b:8 * k + 2 * b + 2, :]) if job.iters == 1 else \
                        (lambda k: gates[:, 8 * k:8 * k + 8, :][:, bass.ts(it, 4), :][:, 2 * b:2 * b + 2, :])
                    dve.tensor_tensor(bb(i), bb(i), acc[:, b % 2, :, 0:S], ALU.mult).then_inc(acc_free, 1)
                    if i:
                        dve.wait_ge(acc_free, job.taken(l, it, b))
                        if i == 2:
                            dve.wait_ge(sum2_ok, 4 + l * 4)
                        dve.tensor_tensor(bb(0), bb(0), bb(i), ALU.add).then_inc(mg_ok if i == 2 else sum2_ok, 1)
                        if i == 2:
                            dve.wait_ge(mgh_ok, 1 + b + l * 4)
                            dve.tensor_tensor(h_lo[:, 2 * b:2 * b + 2, S:2 * S], bb(0), h_hi[:, 2 * b:2 * b + 2, S:2 * S],
                                              ALU.subtract).then_inc(mg_done, 1)
                return evac

            def modulations(n, layer, src, c0, c1):
                dve.tensor_tensor(mod[:, layer, c0:c1, :], src, prm[:, 0, 48 * layer + c0:48 * layer + c1].unsqueeze(2)
                                  .broadcast_to((P, c1 - c0, 2)), ALU.add).then_inc(mod_ok, 1)
                dve.wait_ge(mod_ok, n)
                for k, norm_g in ((0, prm[:, 0, NORM1 + 8 * layer:NORM1 + 8 * layer + 8]), (1, prm[:, 3, NORM2 + 8 * layer:NORM2 + 8 * layer + 8])):
                    if c0 <= 8 + 24 * k < c1:
                        dve.scalar_tensor_tensor(gain[:, layer, k], mod[:, layer, 8 + 24 * k:16 + 24 * k, :], 1.0,
                                                 norm_g.unsqueeze(2).broadcast_to((P, DC, 2)), ALU.add, ALU.mult).then_inc(gain_ok, 1)
                dve.wait_ge(gain_ok, (1, 2, 4)[n - 1])

            def gain_at(layer, k, half):
                return lambda c: gain[:, layer, k, c, half:half + 1]

            dve.memset(eps[:], EPS).then_inc(setup, 1)
            dve.memset(nomask[:], 0.0).then_inc(setup, 1)
            dve.memset(smx[:], 0.0).then_inc(lo_done, SLOTS)
            dve.memset(snm[:], 0.0).then_inc(units_used, SLOTS)
            dve.memset(sden[:], 0.0).then_inc(acc_free, 2)
            dve.wait_ge(prm_t, 1)
            dve.tensor_copy(prm[:, 0, :], wk[:, 3, 0:P]).then_inc(prm_ok, 1)
            dve.tensor_copy(prm[:, 1:3, 0:CUR], wk[:, 3, P:3 * P].rearrange("p (t n) -> p t n", t=2)[:, :, 0:CUR]).then_inc(prm_ok, 1)
            dve.tensor_copy(prm[:, 3, 0:PRM3], wk[:, 3, 3 * P:3 * P + PRM3]).then_inc(prm_ok, 1)

            def turned_in(n0, half):
                for g in range(4):
                    dve.wait_ge(turned, n0 + g + 1)
                    dve.tensor_copy(xT[:, 2 * g:2 * g + 2, half * S:(half + 1) * S],
                                    acc[:, g // 2, g % 2].rearrange("p (c t) -> p c t", c=2)).then_inc(x_done, 1)

            turned_in(0, 0)
            turned_in(4, 1)
            dve.wait_ge(c_hi_ok, 1)
            parts = c_parts[:].rearrange("p k (w s) -> p k w s", s=2)
            dve.tensor_tensor(parts[:, :, :, 1], c_act[:].rearrange("p (w k) -> p k w", w=2), parts[:, :, :, 0], ALU.subtract)\
                .then_inc(c_lo_ok, 1)
            dve.wait_ge(prm_ok, 3)
            dve.tensor_copy(soft_in[:, 8:24].rearrange("p (l n) -> p l n", l=2), prm[:, 1:3, LAM:LAM + 8]).then_inc(soft_ok, 1)
            dve.wait_ge(in_prm, 16 * PRM_DMAS)
            dve.wait_ge(soft_ok, 1)
            dve.scalar_tensor_tensor(soft_t[:], soft_in[:], -1.0, soft_in[:], ALU.mult, ALU.min).then_inc(soft_v, 1)
            head("ada0a")
            dve.wait_ge(soft_a, 1)
            n = [1]

            def chained(ins):
                ins.then_inc(soft_ok, 1)
                n[0] += 1
                dve.wait_ge(soft_ok, n[0])

            chained(dve.tensor_scalar(soft_w[:], soft_e[:], 2.0, None, ALU.add))
            chained(dve.reciprocal(soft_p[:], soft_w[:]))
            chained(dve.tensor_tensor(soft_w[:], soft_e[:], soft_p[:], ALU.mult))
            chained(dve.tensor_tensor(soft_e[:], soft_w[:], soft_w[:], ALU.mult))
            chained(dve.tensor_scalar(soft_p[:], soft_e[:], 1.0 / 15, 1.0 / 13, ALU.mult, ALU.add))
            for k in (11, 9, 7, 5, 3, 1):
                chained(dve.tensor_tensor(soft_p[:], soft_p[:], soft_e[:], ALU.mult))
                chained(dve.tensor_scalar(soft_p[:], soft_p[:], 1.0 / k, None, ALU.add))
            chained(dve.tensor_tensor(soft_p[:], soft_p[:], soft_w[:], ALU.mult))
            chained(dve.tensor_scalar(soft_t[:], soft_in[:], -1.0, 0.0, ALU.mult, ALU.max))
            chained(dve.scalar_tensor_tensor(soft[:], soft_p[:], 2.0, soft_t[:], ALU.mult, ALU.add))
            dve.tensor_scalar(decay[:, 0, :], soft[:, 0:8], -1.0, None, ALU.mult)
            dve.tensor_copy(decay[:, 1, :], soft[:, 0:8])
            dve.tensor_scalar(decay[:, 2, :], soft[:, 0:8], -2.0 * S, None, ALU.mult)
            lam = soft[:, 8:24].rearrange("p (l n) -> p l n", l=2)
            dve.tensor_scalar(lam_s[:, :, 0, :], lam, -8.0, None, ALU.mult)
            chained(dve.tensor_scalar(lam_s[:, :, 1, :], lam, -16.0, None, ALU.mult))

            rest("ada0a", ada)
            head("q0", None, "ada0a", ada)
            dve.wait_ge(ada_sum, 1)
            modulations(1, 0, wk[:, 2, 0:32].rearrange("p (c w) -> p c w", w=2), 0, 16)
            norm(0, 0, gain_at(0, 0, 0), 0)
            norm(1, 1, gain_at(0, 0, 1), 0)
            rest("q0", None)
            head("kv0", None, "q0", None)
            rest("kv0", None)
            dve.wait_ge(in_attn, 96)
            dve.wait_ge(hstd, 1)
            dve.reciprocal(sd_b[0:20, 0, :], sd_b[0:20, 0, :]).then_inc(hrec, 1)
            part_ps = [wk[:, 3], acc[:, 0, 1]]
            for c in range(11):
                if c < 10:
                    dve.wait_ge(hback, c + 1)
                    col = Q_N if c < 8 else K_N
                    dve.scalar_tensor_tensor(qk[:, c, :], qk[:, c, :], prm[:, 3, col:col + 1], wk[:, 1 + c % 2, :], ALU.mult, ALU.mult)\
                        .then_inc(hn, 1)
                if c:
                    b = c - 1
                    dve.wait_ge(hperm, b + 1)
                    dve.tensor_tensor(rot_b[:, b % 2, 0, :], qk[:, b, 0:S], cos_a[:, :], ALU.mult)
                    dve.tensor_tensor(rot_b[:, b % 2, 1, :], part_ps[b % 2][:, 0:S], sin_a[:, :], ALU.mult).then_inc(hrot, 1)
                    dve.wait_ge(hrot, b + 1)
                    dve.tensor_tensor(qk[:, b, 0:S], rot_b[:, b % 2, 0, :], rot_b[:, b % 2, 1, :], ALU.add).then_inc(hqk, 1)
                beside_first(c - 11)
            attention("first", groups_first(), None, beside_first)
            head("wo0")
            dve.wait_ge(pt_ok, ITEMS0)
            modulations(2, 0, mod[:, 0, 16:48, :], 16, 48)
            modulations(3, 1, mod[:, 1], 0, 48)
            rest("wo0", residual(0, 2, True, 2))
            head("gu0", None, "wo0", residual(0, 2, True, 2))
            norm(2, 0, gain_at(0, 1, 0), 3)
            norm(3, 1, gain_at(0, 1, 1), 3)
            rest("gu0", gate_up("gu0", 2 * S, 0))
            head("dn0", None, "gu0", gate_up("gu0", 2 * S, 0))
            rest("dn0", residual(0, 5, True, 2))
            head("rq", None, "dn0", residual(0, 5, True, 2))
            norm(4, 0, gain_at(1, 0, 0), 0, layer=1)
            norm(5, 1, gain_at(1, 0, 1), 0, layer=1)
            dve.wait_ge(in_rope, 32)
            rest("rq", rope(0, r_q))
            head("rk", None, "rq", rope(0, r_q))
            rest("rk", rope(4, r_k))
            head("rv", None, "rk", rope(4, r_k))
            rest("rv", None)
            head("rg", None, "rv", None)
            rest("rg", None)
            head("rwo", None, "rg", None)
            dve.wait_ge(in_tabs, 48)
            for h in range(RH):
                dve.tensor_scalar(r_d[:, 0:2, :], ahead, decay[:, 0, h:h + 1], None, ALU.mult).then_inc(dx_a, 1)
                dve.wait_ge(dx_a, h + 1)
                dve.scalar_tensor_tensor(r_d[:, 0:2, :], behind, decay[:, 0, 4 + h:5 + h], r_d[:, 0:2, :], ALU.mult, ALU.add)\
                    .then_inc(dx_in, 1)
                dve.wait_ge(dx_e, h + 1)
                for kt in range(2):
                    diag = r_d[:, kt, kt * P:(kt + 1) * P]
                    dve.tensor_tensor(diag, diag, ident[:, :], ALU.add)
                dve.wait_ge(dc_e, 2 * h + 2)
                dve.tensor_tensor(r_d[:, 2:4, :], r_d[:, 2:4, :], act_buf[:, 0, :].rearrange("p (m n) -> p m n", m=2), ALU.add)\
                    .then_inc(d_ok, 1)
                dve.wait_ge(d_ok, h + 1)
                for b in range(2):
                    dve.wait_ge(rs_ok, 2 * h + b + 1)
                    if h:
                        dve.wait_ge(ro_ok, 2 * h)
                    dve.scalar_tensor_tensor(r_p[:, 2 * b:2 * b + 2, :], wk[:, b, :].rearrange("p (k n) -> p k n", k=2), RQ ** -0.5,
                                             r_d[:, 2 * b:2 * b + 2, :], ALU.mult, ALU.mult).then_inc(rp_ok, 1)
                for r in range(2):
                    i = 2 * h + r + 1
                    dve.wait_ge(ro_ok, i)
                    dve.bn_stats(stats[:, r, :], wk[:, 2 + r, :]).then_inc(bn_ok, 1)
                    dve.wait_ge(bn_ok, i)
                    dve.bn_aggr(mv[:, r, :], stats[:, r, :]).then_inc(mv_ok, 1)
                for r in range(2):
                    i = 2 * h + r + 1
                    dve.wait_ge(gs_ok, i)
                    dve.reciprocal(gstd[:, r:r + 1], gstd[:, r:r + 1]).then_inc(gr_ok, 1)
                    dve.wait_ge(gr_ok, i)
                    if h:
                        dve.wait_ge(yt_ok, h)
                    dve.tensor_scalar(r_y[:, r, :], wk[:, 2 + r, :], mv[:, r, 0:1], gstd[:, r:r + 1], ALU.subtract, ALU.mult)\
                        .then_inc(y_ok, 1)
                dve.wait_ge(acc_free, J["rg"].done())
                dve.wait_ge(yt_ok, h + 1)
                z = act_buf[:].rearrange("p a (b t) -> p (a b) t", b=2)
                for c in range(4):
                    dve.scalar_tensor_tensor(z[:, c, :], acc[:, 0, c // 2, (c % 2) * S:(c % 2 + 1) * S],
                                             prm[:, 3, GN_G + 4 * h + c:GN_G + 4 * h + c + 1], r_g[:, 4 * h + c, :],
                                             ALU.mult, ALU.mult).then_inc(z_ok if c == 3 else z_part, 1)
                dve.wait_ge(zh_ok, h + 1)
                dve.tensor_tensor(z_lo[:, 4 * h:4 * h + 4, :], z, z_hi[:, 4 * h:4 * h + 4, :], ALU.subtract).then_inc(z_done, 1)
            rest("rwo", residual(1, 2, False, 2))
            head("gu1", None, "rwo", residual(1, 2, False, 2))
            norm(6, 0, gain_at(1, 1, 0), 3, layer=1)
            rest("gu1", gate_up("gu1", S, 11))
            head("dn1", None, "gu1", gate_up("gu1", S, 11))
            rest("dn1", residual(1, 5, False, 2))
            tail("dn1", residual(1, 5, False, 2))
            turned_in(8, 1)

            with dve.Fori(0, LAYERS2) as l:
                n0 = NORMS1 + l * 4
                dve.tensor_copy(cur[:, 0:CUR], prm[:, bass.ds(l + 1, 1), 0:CUR].rearrange("p o n -> p (o n)")).then_inc(cur_ok, 1)
                dve.tensor_copy(cur[:, CUR:CUR + 16], lam_s[:, bass.ds(l, 1)].rearrange("p o w c -> p (o w c)")).then_inc(cur_ok, 1)
                dve.tensor_copy(sink_l[:], sinks[:, 16:32].rearrange("p (l h) -> p l h", l=2)[:, bass.ds(l, 1), :]
                                .rearrange("p o h -> p (o h)")).then_inc(cur_ok, 1)
                dve.wait_ge(cur_ok, 3 + l * 3)

                def gain_in(col):
                    return lambda c: cur[:, col + c:col + c + 1]

                head("gua", l)
                norm(n0, 0, gain_in(FFN1_N))
                rest("gua", gate_up("gua", S, 22), l)
                head("dna", l, "gua", gate_up("gua", S, 22))
                norm(n0 + 1, 1, gain_in(MEM_N))
                rest("dna", residual2(0.5, 2), l)
                head("memk", l, "dna", residual2(0.5, 2))
                rest("memk", None, l)
                head("memv", l, "memk", None)
                norm(n0 + 2, 0, gain_in(MIX_N))
                rest("memv", None, l)
                head("xr", l, "memv", None)
                rest("xr", None, l)
                head("yr", l, "xr", None)

                def conv(w):
                    for c in range(DC):
                        src, tap = XR[:, c, 1 + w:1 + w + S], cur[:, CONV_W + 8 * w + c:CONV_W + 8 * w + c + 1]
                        if w == 0:
                            ins = dve.tensor_scalar(XC[:, c, :], src, tap, cur[:, CONV_B + c:CONV_B + c + 1], ALU.mult, ALU.add)
                        else:
                            dve.wait_ge(conv_ok, 8 * (w - 1) + c + 1 + l * 32)
                            ins = dve.scalar_tensor_tensor(XC[:, c, :], src, tap, XC[:, c, :], ALU.mult, ALU.add)
                        ins.then_inc(conv_ok, 1)

                dve.memset(XR[:, :, 0:4], 0.0).then_inc(pad_ok, 1)
                dve.wait_ge(pad_ok, 1 + l)
                dve.wait_ge(acc_free, J["xr"].done(l))
                conv(0)
                conv(1)
                rest("yr", None, l)
                head("gates", l, "yr", None)
                conv(2)
                conv(3)
                dve.wait_ge(xch_ok, 1 + l)
                dve.tensor_tensor(h_lo[:, :, S:2 * S], XC[:], h_hi[:, :, S:2 * S], ALU.subtract).then_inc(xc_ok, 1)
                rest("gates", None, l)
                head("kvlru", l, "gates", None)
                rest("kvlru", None, l)
                head("q", l, "kvlru", None)
                rest("q", None, l)
                dve.wait_ge(e2_ok, 8 + l * 16)
                dve.tensor_scalar(XR[:, :, 0:S], XR[:, :, 0:S], 1.0, None, ALU.min).then_inc(cl_ok, 1)
                head("cq", l, "q", None)
                dve.wait_ge(mu_ok, 1 + l)
                dve.memset(XR[:, :, 0:1], 1.0).then_inc(b_ok, 1)
                dve.wait_ge(b_ok, 1 + l * 2)
                dve.wait_ge(gx_ok, 1 + l)
                dve.tensor_tensor(GI[:], GI[:], XR[:, :, 0:S], ALU.mult).then_inc(b_ok, 1)
                rest("cq", None, l)
                dve.wait_ge(e2_ok, 16 + l * 16)
                dve.wait_ge(b_ok, 2 + l * 2)
                for c in range(DC):
                    dve.tensor_tensor_scan(XR[:, c, 0:S], R[:, c, :], GI[:, c, :], 0.0, ALU.mult, ALU.add).then_inc(scan_ok, 1)
                head("attn_out", l, "cq", None)
                dve.wait_ge(vt_ok, 1 + l)
                dve.tensor_copy(v_2[:].rearrange("p r n -> p (r n)"), wk[:, 3, 0:S]).then_inc(v2_ok, 1)
                attention("second", groups_window() + groups_memory(), l)
                rest("attn_out", branch(0), l)
                head("lru_out", l, "attn_out", branch(0))
                rest("lru_out", branch(1), l)
                head("mem_out", l, "lru_out", branch(1))
                rest("mem_out", branch(2), l)
                head("w_out", l, "mem_out", branch(2))
                rest("w_out", residual2(1.0, 2), l)
                head("gub", l, "w_out", residual2(1.0, 2))
                norm(n0 + 3, 0, gain_in(FFN2_N))
                rest("gub", gate_up("gub", S, 33), l)
                head("dnb", l, "gub", gate_up("gub", S, 33))
                rest("dnb", residual2(0.5, 2), l)
                tail("dnb", residual2(0.5, 2), l)
            norm(NORM_LAST, 0, lambda c: prm[:, 3, FINAL_N + c:FINAL_N + c + 1], split_out=False)
            for g in range(4):
                dve.wait_ge(fin_t, g + 1)
                dve.tensor_copy(rows[:, g * 512:(g + 1) * 512], wk[:, g, :] if g < 3 else acc[:, 0, 0, :]).then_inc(fin_ok, 1)



INS = ["x", "c", "ctx", "c_ctx", "ada_w", "ada_b", "norm1_g", "norm2_g", "ffn_w_in", "ffn_w_out", "attn_w_qkv",
       "attn_q_norm", "attn_k_norm", "attn_sink", "attn_w_o", "ret_w_qkvg", "ret_decay_logit", "ret_gn_g", "ret_w_o",
       "mem_2", "ffn1_norm_2", "ffn1_w_gate_2", "ffn1_w_up_2", "ffn1_w_down_2", "mix_norm_2", "w_in_2", "gate_bias_2",
       "attn_sinks_2", "w_attn_out_2", "conv_w_2", "conv_b_2", "lru_wa_2", "lru_ba_2", "lru_wx_2", "lru_bx_2",
       "lru_lambda_2", "w_lru_out_2", "mem_norm_2", "w_mem_kv_2", "w_mem_out_2", "w_out_2", "ffn2_norm_2",
       "ffn2_w_gate_2", "ffn2_w_up_2", "ffn2_w_down_2", "final_norm_2"]


def kernel(**inputs):
    import concourse.bacc as bacc
    from concourse.bass_utils import run_bass_kernel_spmd

    nc = bacc.Bacc("TRN2", target_bir_lowering=False, num_devices=1)
    table, const_at = shape_constants()
    arrays, aps = {}, {}
    for name in INS + ["shape_constants"]:
        data = table if name == "shape_constants" else np.ascontiguousarray(inputs[name])
        arrays[f"in_{name}_dram"] = data
        aps[name] = nc.dram_tensor(f"in_{name}_dram", data.shape, mybir.dt.from_np(data.dtype), kind="ExternalInput").ap()
    out = nc.dram_tensor("out_0_dram", (1, S, D), F32, kind="ExternalOutput").ap()
    build(nc, aps, out, const_at)
    r = run_bass_kernel_spmd(nc, [arrays], core_ids=[0])
    return r.results[0]["out_0_dram"]
```

```python
from contextlib import ExitStack

import numpy as np

import concourse.bass as bass
from concourse import mybir

F32 = mybir.dt.float32
F32R = mybir.dt.float32r
ALU = mybir.AluOpType
ACT = mybir.ActivationFunctionType

P = 128
D = 1024
DC = D // P
S = 256
FF = 2816
FC = FF // P
COLS = 256
KCH = 4
SLOTS = 4
LAG = 3
EPS = 1e-6
MASKED = -1e30
HEADS, HD, GROUP = 16, 64, 4
RH, RQ, RV = 4, 256, 512
WH = 8
MH = 4
LAYERS2 = 2
ROPE_BASE = 10000.0
GRID_W = 64



def shape_constants():
    tok = np.arange(S)
    row, col = (tok // GRID_W).astype(np.float32), (tok % GRID_W).astype(np.float32)

    def rope(head_dim, d):
        axis = head_dim // 2
        half = axis // 2
        inv = (np.float32(ROPE_BASE) ** (-np.arange(0, axis, 2, dtype=np.float32) / np.float32(axis))).astype(np.float32)
        pos = np.where((d // axis == 0)[:, None], row[None, :], col[None, :]).astype(np.float32)
        ang = (pos * inv[d % half][:, None]).astype(np.float32)
        sign = np.where(d % axis < half, -1.0, 1.0)[:, None]
        return np.cos(ang), np.sin(ang) * sign

    p = np.arange(P)
    cos_a, sin_a = rope(HD, p % HD)
    rc, rs = zip(*[rope(RQ, p + P * c) for c in range(2)])
    q = p[:, None, None] + P * np.arange(2)[None, :, None]
    k = np.arange(S)[None, None, :]
    window = np.concatenate([np.where(np.abs(k - q) <= P, 0.0, MASKED), np.zeros((P, 2, S))], axis=2)
    back = q // 64 - k // 64
    alibi = np.where((back >= 0) & (back <= 2), np.abs(q - k), -MASKED)
    m = q
    n = k
    parts = {
        "ident": np.eye(P), "ones": np.ones((P, P)), "alibi": alibi.reshape(P, -1),
        "slopes": np.tile(-(2.0 ** -np.arange(1.0, WH + 1)) * HD ** 0.5, (P, 1)),
        "sel": np.repeat(np.eye(2), 2, axis=0)[np.minimum(p, 3)] * (p < 4)[:, None],
        "headsum": (np.arange(20)[None, None, :] == 2 * np.arange(10)[None, :, None] + p[:, None, None] // HD).reshape(P, -1),
        "headback": (p[:, None, None] == 2 * np.arange(10)[None, :, None] + p[None, None, :] // HD).reshape(P, -1),
        "partner": (p[:, None] == (p[None, :] ^ (HD // 4))),
        "cos_a": cos_a, "sin_a": sin_a, "window": window.reshape(P, -1),
        "cos_r": np.concatenate(rc, 1), "sin_r": np.concatenate(rs, 1),
        "ahead": np.maximum(n - m, 0).reshape(P, -1), "behind": np.maximum(m - n, 0).reshape(P, -1),
        "since": (n + S - m).reshape(P, -1),
    }
    at, width = {}, 0
    for name, a in parts.items():
        at[name] = (width, a.shape[1])
        width += a.shape[1]
    return np.concatenate([np.asarray(a, np.float32) for a in parts.values()], axis=1), at




class Job:

    def __init__(self, unit_chunks, ends, iters, acts_from=0):
        self.unit_chunks = unit_chunks
        self.ends = ends
        self.iters = iters
        self.body = len(unit_chunks)
        self.per = len(ends)
        self.unit0 = self.block0 = self.unit_step = self.block_step = 0
        assert self.body % SLOTS == 0 and self.per % 2 == 0

    def unit(self, l, it, p):
        return self.unit0 + p + it * self.body + (l * self.unit_step if self.unit_step else 0)

    def block(self, l, it, b):
        return self.block0 + b + it * self.per + (l * self.block_step if self.block_step else 0)

    def taken(self, l, it, b):
        return self.block(l, it, b) + 3

    def done(self, l=None):
        return self.taken(l, self.iters - 1, self.per - 1)

    def loaded(self, l, it, p):
        return 16 * (self.unit0 // SLOTS + p // SLOTS + 1) + it * (16 * self.body // SLOTS) \
            + (l * (16 * self.unit_step // SLOTS) if self.unit_step else 0)


def columns(k_chunks, n):
    per_block = [KCH] * (k_chunks // KCH) + ([k_chunks % KCH] if k_chunks % KCH else [])
    blocks = 2
    while len(per_block) * blocks % SLOTS:
        blocks += 2
    units = per_block * blocks
    return Job(units, [len(per_block) * (b + 1) - 1 for b in range(blocks)], n // COLS // blocks)


FIRST = ["ada0a", "q0", "kv0", "ada0b", "ada1", "wo0", "gu0", "dn0", "rq", "rk", "rv", "rg", "rwo", "gu1", "dn1"]
SECOND = ["gua", "dna", "memk", "memv", "xr", "yr", "q", "kvlru", "gates", "cq", "lru_out", "attn_out",
          "mem_out", "w_out", "gub", "dnb"]


def plan():
    two = lambda n: columns(DC, n)
    jobs = {
        "ada0a": two(2 * D), "ada0b": two(4 * D), "q0": two(D), "kv0": two(512), "wo0": two(D), "gu0": two(2 * FF), "dn0": columns(FC, D),
        "ada1": two(6 * D), "rq": two(D), "rk": two(D), "rv": two(2 * D), "rg": two(2 * D), "rwo": columns(16, D),
        "gu1": two(2 * FF), "dn1": columns(FC, D),
        "gua": two(2 * FF), "dna": columns(FC, D), "memk": two(512), "memv": two(512), "xr": two(D), "yr": two(D),
        "gates": two(3 * D), "kvlru": Job([4, 4, 2, 2], [1, 1, 2, 2, 3, 3], 1), "q": two(512), "cq": two(512),
        "attn_out": columns(4, D), "lru_out": two(D), "mem_out": columns(4, D), "w_out": two(D),
        "gub": two(2 * FF), "dnb": columns(FC, D),
    }
    u = b = 0
    for name in FIRST + SECOND:
        if name == SECOND[0]:
            u2, b2 = u, b
        jobs[name].unit0, jobs[name].block0 = u, b
        u += jobs[name].iters * jobs[name].body
        b += jobs[name].iters * jobs[name].per
    for name in SECOND:
        jobs[name].unit_step, jobs[name].block_step = u - u2, b - b2
    return jobs


JOBS = plan()

NORMS1 = 7
NORM_LAST = NORMS1 + 4 * LAYERS2
X_START, X_MEM = 8, 12
SIDE = ("ada0b", "ada1")


def side_unit(k):
    first = JOBS[SIDE[0]]
    name = SIDE[0] if k < first.body * first.iters else SIDE[1]
    k -= 0 if name == SIDE[0] else first.body * first.iters
    return name, k // JOBS[name].body, k % JOBS[name].body


SIDE_UNITS = sum(JOBS[n].body * JOBS[n].iters for n in SIDE)
SIDE_START = 10


def side_step(k):
    return k * 9 // 10 - SIDE_START


def side_turns():
    ready = []
    for k in range(1, SIDE_UNITS, 2):
        name, it, p = side_unit(k)
        c = (16 if name == "ada0b" else 0) + 2 * (it * JOBS[name].per + p // 2)
        ready += [(side_step(k) + 4, name, c), (side_step(k) + 4, name, c + 1)]
    turns = {}
    for item in range(4 * 16):
        if item % 4 >= 2:
            turns[item] = [r[1:] for r in ready if r[0] <= item + 3][:6]
            ready = ready[len(turns[item]):]
    assert not ready
    return turns


SIDE_TURNS = side_turns()

ITEMS0, ITEMS_WIN, ITEMS_MEM = 4 * HEADS, 2 * WH, 2 * MH
PAIRS0, PAIRS_WIN, PAIRS_MEM = HEADS // 2, WH // 2, MH

ADA_B, C_COL, CC_COL, NORM1 = 0, 96, 104, 112
GATE_B, CONV_W, FFN1_N, MIX_N, CONV_B, BA, BX, LAM, MEM_N, FFN2_N, CUR = 0, 24, 56, 64, 72, 80, 88, 96, 104, 112, 120
PRM_DMAS = 2 * 10 + 3 + 4 + 3
NORM2, FINAL_N, GN_G, Q_N, K_N, PRM3 = 0, 16, 24, 40, 41, 42


SQUARED1, SQUARED2 = ("wo0", "dn0", "rwo", "dn1"), ("dna", "w_out", "dnb")


def squared_before(name, l):
    if name in SQUARED1:
        return 4 * SQUARED1.index(name)
    return 4 * len(SQUARED1) + 4 * SQUARED2.index(name) + l * 4 * len(SQUARED2)


def build(nc, a, out, const_at):
    J = JOBS
    st = ExitStack()
    with st:
        def sb(name, shape, dt=F32, on=st):
            return on.enter_context(nc.sbuf_tensor(name, shape, dt))

        def sem(name):
            return st.enter_context(nc.semaphore(name))

        raw = sb("raw", [P, SLOTS, KCH, COLS])
        w_hi = sb("w_hi", [P, SLOTS, KCH, COLS], F32R)
        w_lo = sb("w_lo", [P, SLOTS, KCH, COLS], F32R)
        xT = sb("xT", [P, DC, 2 * S])
        h_hi = sb("h_hi", [P, DC, 2 * S], F32R)
        h_lo = sb("h_lo", [P, DC, 2 * S], F32R)
        rows = sb("rows", [P, 2 * D])
        prm = sb("prm", [P, 4, P])
        cur = sb("cur", [P, CUR + 16])
        mod = sb("mod", [P, 2, 48, 2])
        gain = sb("gain", [P, 2, 2, DC, 2])
        ident = sb("ident", [P, P])
        ones = sb("ones", [P, P])
        alibi = sb("alibi", [P, 2 * S])
        nomask = sb("nomask", [P, S])
        sel = sb("sel", [P, 2])
        slopes = sb("slopes", [P, WH])
        c_parts = sb("c_parts", [P, DC, 4], F32R)
        c_act = sb("c_act", [P, 16])
        std = sb("std", [P, S])
        rstd = sb("rstd", [P, S])
        act_buf = sb("act_buf", [P, 2, 2 * S])
        eps = sb("eps", [P, 1])
        soft_in = sb("soft_in", [P, 24])
        soft_e = sb("soft_e", [P, 24])
        soft_t = sb("soft_t", [P, 24])
        soft_w = sb("soft_w", [P, 24])
        soft_p = sb("soft_p", [P, 24])
        soft = sb("soft", [P, 24])
        decay = sb("decay", [P, 3, 8])
        lam_s = sb("lam_s", [P, 2, 2, 8])
        sinks = sb("sinks", [P, 16 + 16])
        sink_l = sb("sink_l", [P, WH])
        smx, snm, ssum, ses, sden, srec = [sb(f"soft_{k}", [P, 8]) for k in ("mx", "nm", "sum", "es", "den", "rec")]
        passed = sb("passed", [P, 8])
        stats = sb("stats", [P, 2, 6])
        mv = sb("mv", [P, 2, 2])
        gstd = sb("gstd", [P, 2])

        def arena(*parts):
            with ExitStack() as on:
                return [sb(n, s, d, on) for n, s, d in parts]

        hid_hi, hid_lo = arena(("hid_hi", [P, FC, 2 * S], F32R), ("hid_lo", [P, FC, 2 * S], F32R))
        nf, nf_c, rows_c, prm_rows, _, ada_s = arena(
            ("nf", [P, DC, S], F32), ("nf_c", [P, DC, S], F32), ("rows_c", [P, 2 * D], F32), ("prm_rows", [P, 4, P], F32),
            ("ada_skip", [P, 2 * FC * 2 * S - 6 * D - 6 * D - 4 * P], F32), ("ada_s", [4, 6 * D], F32))
        (qk, v_tok, k_dup, probs_t, sq_b, sd_b, rot_b, headsum, headback, partner, cos_a, sin_a) = arena(
            ("qk", [P, 10, 2 * S], F32), ("v_tok", [P, 4, 256], F32), ("k_dup", [P, 4, 2 * S], F32),
            ("probs_t", [P, 2, 4, S], F32), ("sq_b", [P, 2, 2 * S], F32),
            ("sd_b", [P, 2, 2 * S], F32), ("rot_b", [P, 2, 2, S], F32),
            ("headsum", [P, 10, 20], F32), ("headback", [P, 10, P], F32), ("partner", [P, P], F32), ("cos_a", [P, S], F32), ("sin_a", [P, S], F32))
        probs = arena(("p_skip", [P, 10 * 2 * S + 4 * 256 + 4 * 2 * S + 8 * S], F32), ("probs", [P, 4, 2 * S], F32))[1]
        r_q, r_k, r_v, r_g, cos_r, sin_r, swp, rot, r_d, r_p = arena(
            ("r_q", [P, DC, S], F32), ("r_k", [P, DC, 2 * S], F32), ("r_v", [P, 4, 2 * D], F32), ("r_g", [P, 16, S], F32),
            ("cos_r", [P, 2, S], F32), ("sin_r", [P, 2, S], F32), ("swp", [P, 2, S], F32), ("rot", [P, 2, S], F32),
            ("r_d", [P, 4, S], F32), ("r_p", [P, 4, S], F32))
        r_d2 = arena(("d_skip", [P, 72 * S], F32), ("r_d2", [P, 4, S], F32))[1]
        r_ds = [r_d, r_d2]
        r_y = arena(("r_skip", [P, 72 * S + 4 * S], F32), ("r_y", [P, 2, 2 * S], F32))[1]
        (gates, gy, XR, XC, R, GI, k_d, v_2, km, vm, probs2, probs_t2, bias2) = arena(
            ("gates", [P, 24, S], F32), ("gy", [P, DC, S], F32), ("XR", [P, DC, S + 4], F32), ("XC", [P, DC, S], F32),
            ("R", [P, DC, S], F32), ("GI", [P, DC, S], F32), ("k_d", [P, 2, S], F32),
            ("v_2", [P, 2, P], F32), ("km", [P, MH, S], F32), ("vm", [P, 2, 512], F32), ("probs2", [P, 4, S], F32),
            ("probs_t2", [P, 2, 2, S], F32), ("bias2", [P, 2, 2 * S], F32))
        w_diag = arena(("g_skip", [P, 8 * S], F32), ("w_diag", [P, 2, 2, D], F32R))[1]
        std_c, rstd_c = rows_c[:, 0:S], rows_c[:, S:2 * S]
        tabs = rows[:, 0:3 * 2 * S].rearrange("p (t m n) -> p t m n", t=3, m=2)
        ahead, behind, since = tabs[:, 0], tabs[:, 1], tabs[:, 2]
        back_c = rows[:, 3 * 2 * S:4 * 2 * S].rearrange("p (m n) -> p m n", m=2)
        q_2 = rows[:, 0:D].rearrange("p (c t) -> p c t", c=4)
        cq_2 = rows[:, D:2 * D].rearrange("p (c t) -> p c t", c=4)
        window = act_buf
        sq_of = act_buf[:].rearrange("p a (c t) -> p a c t", c=2)
        v_T = std
        nf_m = rows[:, 0:2 * D].rearrange("p (c t) -> p c t", t=S)
        z_hi = h_hi[:].rearrange("p c (u t) -> p (c u) t", u=2)
        z_lo = h_lo[:].rearrange("p c (u t) -> p (c u) t", u=2)

        acc = st.enter_context(nc.psum_tensor("acc", [P, 2, 2, 512], F32))
        wk = st.enter_context(nc.psum_tensor("wk", [P, 4, 512], F32))
        sc_ps = [wk[:, 0], wk[:, 1]]
        pt_ps = [wk[:, 2], acc[:, 0, 1]]
        o_ps = [wk[:, 3], acc[:, 1, 1]]
        ro_ps = [[wk[:, 2], wk[:, 3]], [acc[:, 1, 0], acc[:, 1, 1]]]
        ry_ps = [[acc[:, 0, 0], acc[:, 0, 1]]] * (RH - 1) + [[wk[:, 0], wk[:, 1]]]

        load = [sem(f"load{k}") for k in range(SLOTS)]
        hi_done = sem("hi_done")
        lo_done = sem("lo_done")
        units_used = sem("units_used")
        acc_free = sem("acc_free")
        x_done = sem("x_done")
        in_x, in_c, in_m = sem("in_x"), sem("in_c"), sem("in_m")
        in_prm0, in_prm, in_ones, in_const = sem("in_prm0"), sem("in_prm"), sem("in_ones"), sem("in_const")
        in_attn, in_tabs, in_rope = sem("in_attn"), sem("in_tabs"), sem("in_rope")
        setup = sem("setup")
        prm_t, prm_ok = sem("prm_t"), sem("prm_ok")
        turned = sem("turned")
        c_ok, c_hi_ok, c_lo_ok = sem("c_ok"), sem("c_hi_ok"), sem("c_lo_ok")
        soft_a, soft_v = sem("soft_a"), sem("soft_v")
        ada_sum, mod_ok, gain_ok = sem("ada_sum"), sem("mod_ok"), sem("gain_ok")
        sq_ok = sem("sq_ok")
        sqb_ok = sem("sqb_ok")
        ss_ok = sem("ss_ok")
        std_ok, rstd_ok = sem("std_ok"), sem("rstd_ok")
        nf_ok, nh_ok, h_ok = sem("nf_ok"), sem("nh_ok"), sem("h_ok")
        hsq, hss, hstd, hrec, hback, hn, hperm, hrot, hqk, kd_ok = [sem(k) for k in (
            "hsq", "hss", "hstd", "hrec", "hback", "hn", "hperm", "hrot", "hqk", "kd_ok")]
        s_ok, m_raw, m_ok, p_ok, den_ok, rec_ok, pn_ok, t_ok, pt_ok = [sem(k) for k in (
            "s_ok", "m_raw", "m_ok", "p_ok", "den_ok", "rec_ok", "pn_ok", "t_ok", "pt_ok")]
        o_ok, o_hi_ok, o_done = sem("o_ok"), sem("o_hi_ok"), sem("o_done")
        hid_hi_ok, hid_ok = sem("hid_hi_ok"), sem("hid_ok")
        swp_ok, rot_ok, rope_ok = sem("swp_ok"), sem("rot_ok"), sem("rope_ok")
        dx_in, dx_e, dc_e, d_ok, rs_ok, rp_ok, ro_ok = [sem(k) for k in ("dx_in", "dx_e", "dc_e", "d_ok", "rs_ok", "rp_ok", "ro_ok")]
        dx_a, bn_ok, mv_ok, gs_ok, gr_ok, y_ok, yt_ok, z_ok, zh_ok, z_done = [sem(k) for k in (
            "dx_a", "bn_ok", "mv_ok", "gs_ok", "gr_ok", "y_ok", "yt_ok", "z_ok", "zh_ok", "z_done")]
        sums_ok = sem("sums_ok")
        cur_ok, conv_ok, xch_ok, xc_ok, zero_ok = [sem(k) for k in ("cur_ok", "conv_ok", "xch_ok", "xc_ok", "zero_ok")]
        e2_ok, cl_ok, mu_ok, gx_ok, b_ok, scan_ok, lru_ok, lruh_ok, lru_done = [sem(k) for k in (
            "e2_ok", "cl_ok", "mu_ok", "gx_ok", "b_ok", "scan_ok", "lru_ok", "lruh_ok", "lru_done")]
        vt_ok, v2_ok, bias_ok = sem("vt_ok"), sem("v2_ok"), sem("bias_ok")
        sum2_ok, mg_ok, mgh_ok, mg_done = [sem(k) for k in ("sum2_ok", "mg_ok", "mgh_ok", "mg_done")]
        soft_ok, pad_ok, z_part = [sem(k) for k in ("soft_ok", "pad_ok", "z_part")]
        fin_t, stored = sem("fin_t"), sem("stored")
        fin_ok = [sem("fin_ok_0"), sem("fin_ok_1")]

        def const(name):
            o, n = const_at[name]
            return a["shape_constants"][:, o:o + n]

        def chunks(w, k0, nk):
            return w[k0 * P:(k0 + nk) * P, :].rearrange("(k p) n -> p k n", p=P)

        def groups_first():
            gs = []
            for h in range(HEADS):
                for ctx in range(2):
                    half = slice(64 * (h % 2), 64 * (h % 2) + 64)
                    keys = slice(S, 2 * S) if ctx else slice(0, 2 * S)
                    tiles = range(2, 4) if ctx else range(4)
                    gs.append(dict(
                        q=[qk[half, h // 2, ctx * S + r * P:ctx * S + (r + 1) * P] for r in range(2)],
                        k=k_dup[half, h // GROUP, keys], nk=keys.stop - keys.start,
                        mask=[window[:, r, keys] for r in range(2)], sink=sinks[:, h:h + 1], scale=HD ** -0.5,
                        v=[v_tok[:, t, 64 * (h // GROUP):64 * (h // GROUP) + 64] for t in tiles],
                        out=o_ps[h // 2 % 2][half, ctx * S:(ctx + 1) * S], pair=h // 2, last=(h % 2 and ctx),
                        probs=probs, probs_t=probs_t, acc=o_ps[h // 2 % 2][:, 0:2 * S],
                        hi=h_hi[:, h // 2, :], lo=h_lo[:, h // 2, :]))
            return gs

        def groups_window():
            gs = []
            for h in range(WH):
                half = slice(64 * (h % 2), 64 * (h % 2) + 64)
                gs.append(dict(
                    q=[q_2[half, h // 2, r * P:(r + 1) * P] for r in range(2)], k=k_d[half, h // 4, :], nk=S,
                    mask=[bias2[:, h % 2, r * S:(r + 1) * S] for r in range(2)], bias=True, sink=sink_l[:, h:h + 1],
                    scale=HD ** -0.5, v=[v_2[:, t, 64 * (h // 4):64 * (h // 4) + 64] for t in range(2)],
                    out=o_ps[h // 2 % 2][half, 0:S], pair=h // 2, last=h % 2, probs=probs2, probs_t=probs_t2,
                    acc=o_ps[h // 2 % 2][:, 0:S], hi=h_hi[:, h // 2, 0:S], lo=h_lo[:, h // 2, 0:S]))
            return gs

        def groups_memory():
            gs = []
            for h in range(MH):
                gs.append(dict(
                    q=[cq_2[:, h, r * P:(r + 1) * P] for r in range(2)], k=km[:, h, :], nk=S, mask=[nomask[:, :]] * 2,
                    sink=None, scale=P ** -0.5, v=[vm[:, t, P * h:P * h + P] for t in range(2)],
                    out=o_ps[h % 2][:, 0:S], pair=PAIRS_WIN + h, last=True, probs=probs2, probs_t=probs_t2, acc=o_ps[h % 2][:, 0:S],
                    hi=h_hi[:, 4 + h, 0:S], lo=h_lo[:, 4 + h, 0:S]))
            return gs

        def normed_in(n, half):
            return nf if not half else nf_c if isinstance(n, int) else nf_m

        def norm_sums(n, half):
            return wk[:, 2 if half else 3, 0:S]

        def attn_base(which, l):
            if which == "first":
                return 0, 0
            return ITEMS0 + l * (ITEMS_WIN + ITEMS_MEM), PAIRS0 + l * (PAIRS_WIN + PAIRS_MEM)

        T_LAG, N_LAG, O_LAG, H_LAG, L_LAG = 3, 2, 5, 7, 8

        def attn_steps(groups):
            return range(2 * len(groups) - 2 + L_LAG + 1)

        def group_at(i, lag, groups):
            return (i - lag) // 2 if (i - lag) % 2 == 0 and 0 <= (i - lag) // 2 < len(groups) else None

        OUT_UNITS = J["lru_out"].body * J["lru_out"].iters

        def split_step(k):
            return min(max(4 * (k - SLOTS) + 3, 0), 4 * OUT_UNITS - 2)

        HEAD_ORDER = [8, 9] + list(range(8))

        fin_ps = [[wk[:, 0], wk[:, 1]], [wk[:, 2], acc[:, 0, 0]]]

        block = st.enter_context(nc.Block())

        @block.sync
        def _(sp):
            def stream(name, src, l=None):
                job = J[name]

                def one(it):
                    for p in range(job.body):
                        sp.wait_ge(lo_done, job.unit(l, it, p) + 1)
                        s = src(l, it, p)
                        slot = raw[:, p % SLOTS]
                        dst = slot[:, 0:s.shape[1], :] if s.shape[2] == COLS else \
                            slot[:, 0:2, :].rearrange("p k n -> p (k n)").rearrange("p (c j) -> p c j", j=64)
                        sp.dma_start(dst, s).then_inc(load[p % SLOTS], 16)

                if job.iters == 1:
                    one(0)
                else:
                    with sp.Fori(0, job.iters) as it:
                        one(it)

            def plain(w, k_chunks, col0=0, n=None):
                per = -(-k_chunks // KCH)
                n = n or w.shape[-1]

                def src(l, it, p):
                    m = w if l is None else w[l]
                    b, u = divmod(p, per)
                    blocks = 2
                    while per * blocks % SLOTS:
                        blocks += 2
                    k0 = u * KCH
                    view = chunks(m, k0, min(KCH, k_chunks - k0))[:, :, col0:col0 + n]
                    wide = view[:, :, bass.ts(it, blocks * COLS)]
                    return wide[:, :, b * COLS:(b + 1) * COLS]
                return src

            def gate_up(gate, up):
                def src(l, it, p):
                    b, u = divmod(p, 2)
                    m = (gate, up)[b] if l is None else (gate, up)[b][l]
                    return chunks(m, u * KCH, KCH)[:, :, bass.ts(it, COLS)]
                return src

            sp.dma_start(ident[:, :], const("ident")).then_inc(in_prm0, 16)
            sp.dma_start(prm_rows[0:96, 0, :], a["ada_b"].rearrange("l (r f) -> (l r) f", f=P)).then_inc(in_prm0, 16)
            sp.dma_start(prm_rows[96:104, 0, :], a["c"].rearrange("l (r f) -> (l r) f", f=P)).then_inc(in_prm0, 16)
            sp.dma_start(prm_rows[104:112, 0, :], a["c_ctx"].rearrange("(r f) -> r f", f=P)).then_inc(in_prm0, 16)
            sp.dma_start(prm_rows[112:128, 0, :], a["norm1_g"].rearrange("l (r f) -> (l r) f", f=P)).then_inc(in_prm0, 16)
            stream("ada0a", plain(a["ada_w"][0], DC, 0, 2 * D))
            wqkv = a["attn_w_qkv"][0]
            stream("q0", plain(wqkv, DC, 0, D))
            stream("kv0", plain(wqkv, DC, D, 512))
            stream("ada0b", plain(a["ada_w"][0], DC, 2 * D, 4 * D))
            stream("ada1", plain(a["ada_w"][1], DC))
            stream("wo0", plain(a["attn_w_o"][0], DC))
            stream("gu0", gate_up(a["ffn_w_in"][0][:, 0:FF], a["ffn_w_in"][0][:, FF:2 * FF]))
            stream("dn0", plain(a["ffn_w_out"][0], FC))
            wr = a["ret_w_qkvg"][0]
            stream("rq", plain(wr, DC, 0, D))
            stream("rk", plain(wr, DC, D, D))
            stream("rv", plain(wr, DC, 2 * D, 2 * D))
            stream("rg", plain(wr, DC, 4 * D, 2 * D))
            stream("rwo", plain(a["ret_w_o"][0], 16))
            stream("gu1", gate_up(a["ffn_w_in"][1][:, 0:FF], a["ffn_w_in"][1][:, FF:2 * FF]))
            stream("dn1", plain(a["ffn_w_out"][1], FC))
            with sp.Fori(0, LAYERS2) as l:
                stream("gua", gate_up(a["ffn1_w_gate_2"], a["ffn1_w_up_2"]), l)
                stream("dna", plain(a["ffn1_w_down_2"], FC), l)
                stream("memk", plain(a["w_mem_kv_2"], DC, 0, 512), l)
                stream("memv", plain(a["w_mem_kv_2"], DC, 512, 512), l)
                w_in = a["w_in_2"]
                stream("xr", plain(w_in, DC, 768, D), l)
                stream("yr", plain(w_in, DC, 768 + D, D), l)

                def q_unit(l, it, p):
                    rows_l = w_in.rearrange("l k n -> (l k) n")[bass.ds(l * D + p % 2 * KCH * P, KCH * P), :]
                    return chunks(rows_l, 0, KCH)[:, :, p // 2 * COLS:(p // 2 + 1) * COLS]
                stream("q", q_unit, l)

                def kvlru(l, it, p):
                    if p < 2:
                        return chunks(w_in[l], p * KCH, KCH)[:, :, 512:768]
                    return a[("lru_wa_2", "lru_wx_2")[p - 2]][l].rearrange("(c two) i j -> (two i) c j", two=2)
                stream("kvlru", kvlru, l)
                stream("gates", plain(w_in, DC, 1280 + 2 * D, 3 * D), l)
                stream("cq", plain(w_in, DC, 768 + 2 * D, 512), l)
                stream("lru_out", plain(a["w_lru_out_2"], DC), l)
                stream("attn_out", plain(a["w_attn_out_2"], 4), l)
                stream("mem_out", plain(a["w_mem_out_2"], 4), l)
                stream("w_out", plain(a["w_out_2"], DC), l)
                stream("gub", gate_up(a["ffn2_w_gate_2"], a["ffn2_w_up_2"]), l)
                stream("dnb", plain(a["ffn2_w_down_2"], FC), l)
            for r in range(2):
                sp.wait_ge(fin_ok[r], 2)
                sp.dma_start(out[0, r * P:(r + 1) * P, :], rows[:, r * D:(r + 1) * D]).then_inc(stored, 16)
            sp.wait_ge(stored, 32)

        @block.gpsimd
        def _(pool):
            def tokens(dst, src, s):
                for r in range(2):
                    pool.dma_start(dst[:, r * D:(r + 1) * D], src[0, r * P:(r + 1) * P, :]).then_inc(s, 16)

            for name, t in (("sel", sel), ("ones", ones)):
                pool.dma_start(t[:, :], const(name)).then_inc(in_ones, 16)
            tokens(rows, a["x"], in_x)
            tokens(rows_c, a["ctx"], in_c)
            for name, t in (("alibi", alibi), ("slopes", slopes)):
                pool.dma_start(t[:, :], const(name)).then_inc(in_const, 16)
            for l in range(LAYERS2):
                at = 0
                for name, n in (("gate_bias_2", 24), ("conv_w_2", 32), ("ffn1_norm_2", 8), ("mix_norm_2", 8), ("conv_b_2", 8),
                                ("lru_ba_2", 8), ("lru_bx_2", 8), ("lru_lambda_2", 8), ("mem_norm_2", 8), ("ffn2_norm_2", 8)):
                    src = a[name][l].rearrange("w (r f) -> (w r) f", f=P) if name == "conv_w_2" else \
                        a[name][l].rearrange("(r f) -> r f", f=P)
                    pool.dma_start(prm_rows[at:at + n, 1 + l, :], src).then_inc(in_prm, 16)
                    at += n
            pool.dma_start(prm_rows[NORM2:NORM2 + 16, 3, :], a["norm2_g"].rearrange("l (r f) -> (l r) f", f=P)).then_inc(in_prm, 16)
            pool.dma_start(prm_rows[FINAL_N:FINAL_N + 8, 3, :], a["final_norm_2"].rearrange("(r f) -> r f", f=P)).then_inc(in_prm, 16)
            pool.dma_start(prm_rows[GN_G:GN_G + 16, 3, :], a["ret_gn_g"].rearrange("l (r f) -> (l r) f", f=P)).then_inc(in_prm, 16)
            for name, at in (("attn_q_norm", Q_N), ("attn_k_norm", K_N)):
                for half in range(2):
                    pool.dma_start(prm_rows[at:at + 1, 3, half * HD:(half + 1) * HD], a[name]).then_inc(in_prm, 16)
            pool.dma_start(soft_in[:, 0:8], a["ret_decay_logit"].rearrange("o d h -> o (d h)").broadcast_to((P, 8))).then_inc(in_prm, 16)
            pool.dma_start(sinks[:, 0:16], a["attn_sink"].broadcast_to((P, 16))).then_inc(in_prm, 16)
            pool.dma_start(sinks[:, 16:32], a["attn_sinks_2"].rearrange("l (o h) -> o (l h)", o=1).broadcast_to((P, 16))).then_inc(in_prm, 16)
            pool.dma_start(headsum[:].rearrange("p c h -> p (c h)"), const("headsum")).then_inc(in_attn, 16)
            pool.dma_start(headback[:].rearrange("p c h -> p (c h)"), const("headback")).then_inc(in_attn, 16)
            for name, t in (("partner", partner), ("cos_a", cos_a), ("sin_a", sin_a)):
                pool.dma_start(t[:, :], const(name)).then_inc(in_attn, 16)
            pool.dma_start(window[:].rearrange("p r k -> p (r k)"), const("window")).then_inc(in_attn, 16)
            pool.wait_ge(x_done, X_START)
            for n, name in enumerate(("ahead", "behind", "since")):
                pool.dma_start(rows[:, n * 512:(n + 1) * 512], const(name)).then_inc(in_tabs, 16)
            pool.wait_ge(acc_free, J["dn0"].done())
            for name, t in (("cos_r", cos_r), ("sin_r", sin_r)):
                pool.dma_start(t[:].rearrange("p c t -> p (c t)"), const(name)).then_inc(in_rope, 16)
            pool.wait_ge(d_ok, RH)
            tokens(rows, a["mem_2"], in_m)
            with pool.Fori(0, LAYERS2) as l:
                pool.wait_ge(xch_ok, 1 + l)
                pool.tensor_tensor(h_lo[:, :, S:2 * S], XC[:], h_hi[:, :, S:2 * S], ALU.subtract).then_inc(xc_ok, 1)
                pool.wait_ge(acc_free, J["kvlru"].done(l))
                pool.tensor_tensor(GI[:], GI[:], XC[:], ALU.mult).then_inc(gx_ok, 1)
                first, _ = attn_base("second", l)
                for h in range(WH):
                    if h == 2:
                        pool.wait_ge(scan_ok, 8 + l * 8)
                        pool.tensor_tensor(XC[:], XR[:, :, 0:S], gy[:], ALU.mult).then_inc(lru_ok, 1)
                        pool.wait_ge(lruh_ok, 1 + l)
                        pool.tensor_tensor(h_lo[:, :, S:2 * S], XC[:], h_hi[:, :, S:2 * S], ALU.subtract).then_inc(lru_done, 1)
                    if h >= 2:
                        pool.wait_ge(m_raw, first + 2 * (h - 2) + 2)
                    pool.wait_ge(in_const, 16 * 2)
                    pool.tensor_tensor(bias2[:, h % 2, :], alibi[:, :], slopes[:, h:h + 1].broadcast_to((P, 2 * S)), ALU.mult)\
                        .then_inc(bias_ok, 1)
                for b in range(J["mem_out"].per):
                    pool.wait_ge(mgh_ok, 1 + b + l * 4)
                    pool.tensor_tensor(h_lo[:, 2 * b:2 * b + 2, S:2 * S], gates[:, 2 * b:2 * b + 2, :], h_hi[:, 2 * b:2 * b + 2, S:2 * S],
                                       ALU.subtract).then_inc(mg_done, 1)

        @block.tensor
        def _(pe):
            def unit_ready(job, l, it, p):
                pe.wait_ge(lo_done, job.unit(l, it, p) + SLOTS + 1)

            def slot_free(job, l, it, b):
                pe.wait_ge(acc_free, job.block(l, it, b) + 1)

            def product(name, l=None, hi=h_hi, lo=h_lo, tok=slice(0, S), rows_of=None, needs=None, normed=None, squared=False,
                        after=None):
                job = J[name]
                per = job.body // job.per

                def one(it, start=0):
                    for p in range(start, job.body):
                        b, u = divmod(p, per)
                        if u == 0:
                            slot_free(job, l, it, b)
                        if needs:
                            pe.wait_ge(*needs(u, b))
                        unit_ready(job, l, it, p)
                        nk, s, last = job.unit_chunks[p], p % SLOTS, u == per - 1
                        tokens_major = rows_of if not callable(rows_of) else rows_of(b)
                        if tokens_major:
                            for n, r in enumerate(tokens_major):
                                packed = len(tokens_major) > 2
                                o = acc[:, b % 2, n // 2, (n % 2) * S:(n % 2) * S + S] if packed else acc[:, b % 2, n, 0:S]
                                for k in range(nk):
                                    x = slice(r * P, (r + 1) * P)
                                    kk = u * KCH + k
                                    for i, (xs, ws) in enumerate(((hi, w_hi), (hi, w_lo), (lo, w_hi))):
                                        mm = pe.matmul(o, xs[:, kk, x], ws[:, s, k, :],
                                                       start=(u == 0 and k == 0 and i == 0 and not (packed and n % 2)),
                                                       stop=(last and k == nk - 1 and i == 2), skip_group_check=packed)
                        else:
                            t = tok if not callable(tok) else tok(b)
                            for cb in range(2):
                                o = acc[:, b % 2, cb, 0:t.stop - t.start]
                                for k in range(nk):
                                    kk = u * KCH + k
                                    if normed is not None and not isinstance(normed, tuple) and cb == 0 and b == 0:
                                        pe.wait_ge(h_ok, normed + kk + 1)
                                    c = slice(cb * P, (cb + 1) * P)
                                    for i, (ws, xs) in enumerate(((w_hi, hi), (w_hi, lo), (w_lo, hi))):
                                        mm = pe.matmul(o, ws[:, s, k, c], xs[:, kk, t],
                                                       start=(u == 0 and k == 0 and i == 0),
                                                       stop=(last and k == nk - 1 and i == 2))
                        mm.then_inc(units_used, 1)
                        if after:
                            after(p)
                        if squared and u == per - 1 and it * job.per + b:
                            sum_squares(name, l, it * job.per + b - 1)

                if isinstance(normed, tuple):
                    slot_free(job, l, 0, 0)
                    for half in range(2):
                        t = slice(half * S, half * S + S)
                        for p in range(per):
                            if not half:
                                unit_ready(job, l, 0, p)
                            for cb in range(2):
                                for k in range(KCH):
                                    if cb == 0:
                                        pe.wait_ge(h_ok, normed[half] + p * KCH + k + 1)
                                    c = slice(cb * P, (cb + 1) * P)
                                    for i, (ws, xs) in enumerate(((w_hi, hi), (w_hi, lo), (w_lo, hi))):
                                        mm = pe.matmul(acc[:, 0, cb, t], ws[:, p % SLOTS, k, c], xs[:, p * KCH + k, t],
                                                       start=(p == 0 and k == 0 and i == 0),
                                                       stop=(p == per - 1 and k == KCH - 1 and i == 2), skip_group_check=True)
                            if half:
                                mm.then_inc(units_used, 1)
                    one(0, per)
                    with pe.Fori(1, job.iters) as it:
                        one(it)
                elif squared:
                    for it in range(job.iters):
                        one(it)
                    sum_squares(name, l, job.iters * job.per - 1)
                elif job.iters == 1:
                    one(0)
                else:
                    with pe.Fori(0, job.iters) as it:
                        one(it)

            def modulation_unit(name, it, p):
                job = J[name]
                b, u = divmod(p, 2)
                if u == 0:
                    slot_free(job, None, it, b)
                unit_ready(job, None, it, p)
                for k in range(KCH):
                    for i, ws in enumerate((w_hi, w_lo)):
                        mm = pe.matmul(acc[0:4, b % 2, 0, 0:S], c_parts[:, u * KCH + k, :], ws[:, p % SLOTS, k, :],
                                       start=(u == 0 and k == 0 and i == 0), stop=(u == 1 and k == KCH - 1 and i == 1))
                mm.then_inc(units_used, 1)

            def turn_chunk(name, c, dst):
                job = J[name]
                b = (c - (16 if name == "ada0b" else 0)) // 2
                pe.wait_ge(acc_free, job.taken(None, b // job.per, b % job.per))
                return pe.matmul(dst, ada_s[0:4, c * P:(c + 1) * P], sel[0:4, :], start=True, stop=True)

            def sum_squares(name, l, n):
                blocks = J[name].iters * J[name].per
                pe.wait_ge(sqb_ok, squared_before(name, l) + n + 1)
                both = name in ("wo0", "dn0")
                for half in range(2 if both else 1):
                    for c in range(2):
                        src = act_buf[:, c, half * S:(half + 1) * S] if both else sq_of[:, n % 2, c, :]
                        mm = pe.matmul(norm_sums(None, half), ones[:, :], src, start=(n == 0 and c == 0),
                                       stop=(n == blocks - 1 and c == 1))
                    if n == blocks - 1:
                        mm.then_inc(ss_ok, 1)
                    elif both and half:
                        mm.then_inc(sums_ok, 1)

            def norm(n, half, l=None):
                pe.wait_ge(sq_ok, n + 1 if l is None else 3 + l)
                src, dst = normed_in(n, half), norm_sums(n, half)
                for c in range(DC):
                    mm = pe.matmul(dst, ones[:, :], src[:, c, :], start=(c == 0), stop=(c == DC - 1))
                mm.then_inc(ss_ok, 1)

            def turn_in(src, s, banks):
                pe.wait_ge(s, 32)
                for g in range(4):
                    if s is in_c:
                        pe.wait_ge(x_done, g + 1)
                    if s is in_m and g == 3:
                        pe.wait_ge(x_done, X_START + 1)
                    dst = banks[g].rearrange("p (c t) -> p c t", c=2)
                    for c in range(2):
                        for r in range(2):
                            f = r * D + (2 * g + c) * P
                            mm = pe.transpose(dst[:, c, r * P:(r + 1) * P], src[:, f:f + P], ident[:, :])
                    mm.then_inc(turned, 1)

            def attention(which, groups, l=None, beside=None, turns={}):
                first, pair0 = attn_base(which, l)
                again = which != "first"
                items = [(g, r) for g in range(len(groups)) for r in range(2)]
                for i in attn_steps(groups):
                    if i < len(items):
                        g, r = items[i]
                        G = groups[g]
                        if i >= 2 or again:
                            pe.wait_ge(m_raw, first + i - 1)
                        pe.matmul(sc_ps[i % 2][:, 0:G["nk"]], G["q"][r], G["k"], start=True, stop=True).then_inc(s_ok, 1)
                    if beside:
                        beside(i)
                    j = i - T_LAG
                    if 0 <= j < len(items):
                        g, r = items[j]
                        G = groups[g]
                        pe.wait_ge(pn_ok, first + j + 1)
                        if j >= 2 or again:
                            pe.wait_ge(pt_ok, first + j - 1)
                        for t in range(G["nk"] // P):
                            mm = pe.transpose(pt_ps[j % 2][:, t * P:(t + 1) * P], G["probs"][:, j % 4, t * P:(t + 1) * P], ident[:, :])
                        for n, (name, c) in enumerate(turns.get(j, [])):
                            mm = turn_chunk(name, c, pt_ps[j % 2][:, S + 2 * n:S + 2 * n + 2])
                        mm.then_inc(t_ok, 1)
                    g = group_at(i, O_LAG, groups)
                    if g is not None:
                        G = groups[g]
                        tiles = G["nk"] // P
                        pe.wait_ge(pt_ok, first + 2 * g + 2)
                        if G["pair"] >= 2 or again:
                            pe.wait_ge(o_done, pair0 + G["pair"] - 1)
                        for t in range(tiles):
                            mm = pe.matmul(G["out"], G["v"][t], G["probs_t"][:, g % 2, t, :], start=(t == 0),
                                           stop=(t == tiles - 1), skip_group_check=True)
                        mm.then_inc(o_ok, 1)

            def beside_first(i):
                for k in range(SIDE_UNITS):
                    if side_step(k) + 2 == i:
                        modulation_unit(*side_unit(k))

            pe.wait_ge(in_prm0, 16 * 5)

            def turn_parameters(dst, tiles):
                for t in tiles:
                    n = (P, CUR, CUR, PRM3)[t]
                    mm = pe.transpose(dst[:, t * P:t * P + n], prm_rows[0:n, t, :], ident[0:n, 0:n])
                mm.then_inc(prm_t, 1)

            turn_parameters(wk[:, 3], range(1))
            pe.wait_ge(c_lo_ok, 1)
            for it in range(2):
                for p in range(J["ada0a"].body):
                    modulation_unit("ada0a", it, p)
            turn_in(rows, in_x, [wk[:, 0], wk[:, 1], wk[:, 2], acc[:, 0, 1]])
            turn_in(rows_c, in_c, [wk[:, 0], wk[:, 1], wk[:, 2], acc[:, 0, 1]])
            for it in range(2, J["ada0a"].iters):
                for p in range(J["ada0a"].body):
                    modulation_unit("ada0a", it, p)
            pe.wait_ge(x_done, X_START)
            pe.wait_ge(in_ones, 16 * 2)
            for c in range(12):
                turn_chunk("ada0a", c, wk[:, 0, 2 * c:2 * c + 2])
            norm(0, 0)
            norm(1, 1)
            for c in range(12, 16):
                mm = turn_chunk("ada0a", c, wk[:, 0, 2 * c:2 * c + 2])
            mm.then_inc(ada_sum, 1)
            pe.wait_ge(in_prm, 16 * PRM_DMAS)
            pe.wait_ge(mod_ok, 1)
            turn_parameters(wk[:, 0], range(1, 4))
            both = slice(0, 2 * S)
            product("q0", tok=both, normed=(0, 8))

            def head_sums(cs):
                pe.wait_ge(in_attn, 96)
                for c in cs:
                    pe.wait_ge(hsq, c + 1)
                    pe.matmul(wk[0:20, 0, :], headsum[:, c, :], sq_b[:, c % 2, :], start=(c == 0), stop=(c == 9)).then_inc(hss, 1)

            product("kv0", tok=both, rows_of=lambda b: range(4) if b else None, after=lambda p: head_sums((2 * p, 2 * p + 1)))
            head_sums((8, 9))
            pe.wait_ge(hrec, 1)
            part_ps = [wk[:, 3], acc[:, 0, 1]]
            for c in range(11):
                if c < 10:
                    if c >= 2:
                        pe.wait_ge(hn, c - 1)
                    pe.matmul(wk[:, 1 + c % 2, :], headback[0:20, HEAD_ORDER[c], :], sd_b[0:20, 0, :], start=True, stop=True).then_inc(hback, 1)
                if c:
                    b = c - 1
                    pe.wait_ge(hn, b + 1)
                    if b >= 2:
                        pe.wait_ge(hrot, b - 1)
                    pe.matmul(part_ps[b % 2][:, 0:S], partner[:, :], qk[:, HEAD_ORDER[b], 0:S], start=True, stop=True).then_inc(hperm, 1)
                beside_first(c - 11)
            pe.wait_ge(hqk, 10)
            pe.wait_ge(kd_ok, 8)
            pe.wait_ge(acc_free, J["kv0"].done())
            attention("first", groups_first(), None, beside_first, SIDE_TURNS)
            product("wo0", tok=both, needs=lambda u, b: (o_done, PAIRS0), squared=True)
            product("gu0", tok=both, normed=(8 * 2, 8 * 3))
            product("dn0", hi=hid_hi, lo=hid_lo, tok=both, needs=lambda u, b: (hid_ok, min(2 * u + 2, 11)), squared=True)
            product("rq", normed=8 * 4)
            product("rk", tok=both, needs=lambda u, b: (h_ok, 8 * 6))
            product("rv", rows_of=range(4))
            product("rg")

            def scores(h):
                pe.wait_ge(rope_ok, 8)
                for kt in range(4):
                    if h and kt % 2 == 0:
                        pe.wait_ge(rp_ok, 2 * (h - 1) + kt // 2 + 1)
                    for d in range(2):
                        mm = pe.matmul(wk[:, kt // 2, (kt % 2) * S:(kt % 2) * S + S], r_k[:, 2 * h + d, kt * P:(kt + 1) * P],
                                       r_q[:, 2 * h + d, :], start=(d == 0), stop=(d == 1))
                    if kt % 2:
                        mm.then_inc(rs_ok, 1)

            def values(h):
                pe.wait_ge(acc_free, J["rv"].done())
                pe.wait_ge(rp_ok, 2 * h + 2)
                if h == 1:
                    pe.wait_ge(acc_free, J["rg"].done())
                for r in range(2):
                    if h >= 2:
                        pe.wait_ge(y_ok, 2 * (h - 2) + r + 1)
                    for kt in range(4):
                        mm = pe.matmul(ro_ps[h % 2][r], r_p[:, kt, r * P:(r + 1) * P], r_v[:, kt, RV * h:RV * (h + 1)],
                                       start=(kt == 0), stop=(kt == 3))
                    mm.then_inc(ro_ok, 1)

            def turn_y(h):
                if h:
                    pe.wait_ge(z_ok, h)
                else:
                    pe.wait_ge(acc_free, J["rg"].done())
                for r in range(2):
                    pe.wait_ge(y_ok, 2 * h + r + 1)
                    for c in range(4):
                        o = ry_ps[h][c // 2][:, (c % 2) * S + r * P:(c % 2) * S + (r + 1) * P]
                        mm = pe.transpose(o, r_y[:, r, c * P:(c + 1) * P], ident[:, :])
                mm.then_inc(yt_ok, 1)

            for h in range(RH):
                scores(h)
                values(h)
                if h:
                    turn_y(h - 1)
            turn_y(RH - 1)
            pe.wait_ge(z_ok, RH - 1)
            product("rwo", hi=z_hi, lo=z_lo, needs=lambda u, b: (z_done, u + 1), squared=True)
            turn_in(rows, in_m, [wk[:, 0], wk[:, 1], wk[:, 2], wk[:, 0]])
            product("gu1", normed=8 * 6)
            product("dn1", hi=hid_hi, lo=hid_lo, needs=lambda u, b: (hid_ok, 11 + min(2 * u + 2, 11)), squared=True)

            mem = slice(S, 2 * S)
            with pe.Fori(0, LAYERS2) as l:
                n0 = NORMS1 + l * 4
                product("gua", l, normed=8 * NORMS1 + l * 32)
                norm(n0 + 1, 1, l)
                product("dna", l, hi=hid_hi, lo=hid_lo, needs=lambda u, b: (hid_ok, 22 + min(2 * u + 2, 11) + l * 22), squared=True)
                product("memk", l, tok=mem, needs=lambda u, b: (h_ok, 8 * (NORMS1 + 2) + l * 32))
                product("memv", l, rows_of=range(2, 4))
                product("xr", l, normed=8 * (NORMS1 + 2) + l * 32)
                product("yr", l)
                product("q", l)
                job = J["kvlru"]
                slot_free(job, l, 0, 0)
                slot_free(job, l, 0, 1)
                for p in range(2):
                    unit_ready(job, l, 0, p)
                    for cb in range(2):
                        for k in range(KCH):
                            for i, (ws, xs) in enumerate(((w_hi, h_hi), (w_hi, h_lo), (w_lo, h_hi))):
                                mm = pe.matmul(acc[:, 1 - cb, 0, 0:S], ws[:, p, k, cb * P:(cb + 1) * P], xs[:, p * KCH + k, 0:S],
                                               start=(p == 0 and k == 0 and i == 0), stop=(p == 1 and k == KCH - 1 and i == 2))
                    mm.then_inc(units_used, 1)
                pe.wait_ge(xc_ok, 1 + l)
                for p in range(2, 4):
                    unit_ready(job, l, 0, p)
                    wh, wl = w_diag[:, p - 2, 0], w_diag[:, p - 2, 1]
                    for c in range(DC):
                        b = 2 * (p - 1) + c // 4
                        if c % 4 == 0:
                            slot_free(job, l, 0, b)
                        o = acc[:, b % 2, (c % 4) // 2, (c % 2) * S:(c % 2) * S + S]
                        for i, (w, x) in enumerate(((wh, h_hi), (wh, h_lo), (wl, h_hi))):
                            mm = pe.matmul(o, w[:, c * P:(c + 1) * P], x[:, c, mem], start=(i == 0), stop=(i == 2))
                    mm.then_inc(units_used, 1)
                product("gates", l)
                pe.wait_ge(acc_free, J["kvlru"].done(l))
                for r in range(2):
                    mm = pe.transpose(wk[:, 3, r * P:(r + 1) * P], v_T[:, r * P:(r + 1) * P], ident[:, :])
                mm.then_inc(vt_ok, 1)
                product("cq", l)
                pe.wait_ge(acc_free, J["cq"].done(l))
                pe.wait_ge(lru_done, 1 + l)
                pe.wait_ge(v2_ok, 1 + l)

                def recurrence_out(i):
                    k, quarter = divmod(i + 1, 4)
                    job, (it, p) = J["lru_out"], divmod(k, J["lru_out"].body)
                    (b, u), (cb, half) = divmod(p, 2), divmod(quarter, 2)
                    if u == 0 and quarter == 0:
                        slot_free(job, l, it, b)
                    if quarter == 0:
                        unit_ready(job, l, it, p)
                    o, c = acc[:, b % 2, 0, cb * S:(cb + 1) * S], slice(cb * P, (cb + 1) * P)
                    for k in range(half * KCH // 2, (half + 1) * KCH // 2):
                        for n, (ws, xs) in enumerate(((w_hi, h_hi), (w_hi, h_lo), (w_lo, h_hi))):
                            mm = pe.matmul(o, ws[:, p % SLOTS, k, c], xs[:, u * KCH + k, mem],
                                           start=(u == 0 and cb == 0 and k == 0 and n == 0),
                                           stop=(u == 1 and k == KCH - 1 and n == 2), skip_group_check=True)
                    if quarter == 3:
                        mm.then_inc(units_used, 1)
                recurrence_out(-1)
                attention("second", groups_window() + groups_memory(), l, recurrence_out)
                _, pair0 = attn_base("second", l)
                product("attn_out", l, needs=lambda u, b: (o_done, pair0 + PAIRS_WIN + (PAIRS_MEM if b else 0)))
                product("mem_out", l, hi=h_hi[:, 4:8, :], lo=h_lo[:, 4:8, :])
                product("w_out", l, tok=mem, needs=lambda u, b: (mg_done, 2 * u + 2 + l * 4), squared=True)
                product("gub", l, normed=8 * (NORMS1 + 3) + l * 32)
                product("dnb", l, hi=hid_hi, lo=hid_lo, needs=lambda u, b: (hid_ok, 33 + min(2 * u + 2, 11) + l * 22), squared=True)
            for c in range(DC):
                pe.wait_ge(nf_ok, 8 * NORM_LAST + c + 1)
                for r in range(2):
                    mm = pe.transpose(fin_ps[r][c // 4][:, (c % 4) * P:(c % 4 + 1) * P], nf[:, c, r * P:(r + 1) * P], ident[:, :])
                    if c % 4 == 3:
                        mm.then_inc(fin_t, 1)

        @block.scalar
        def _(act):
            def split(job, l, it, p):
                s, nk = p % SLOTS, job.unit_chunks[p]
                act.wait_ge(load[s], job.loaded(l, it, p))
                act.wait_ge(units_used, job.unit(l, it, p) + 1)
                act.copy(w_hi[:, s, 0:nk, :], raw[:, s, 0:nk, :]).then_inc(hi_done, 1)

            def split_diag(job, l, p):
                act.wait_ge(load[p], job.loaded(l, 0, p))
                act.wait_ge(zero_ok, 1 + l)
                src = raw[:, p, 0:2, :].rearrange("p k n -> p (k n)").rearrange("p (c j) -> p c j", j=64)
                dst = w_diag[:, p - 2, 0].rearrange("p (c j) -> p c j", j=P)
                act.copy(dst[0:64, :, 0:64], src[0:64])
                act.copy(dst[64:128, :, 64:128], src[64:128]).then_inc(hi_done, 1)

            def block_done(job, l, it, b):
                act.wait_ge(units_used, job.unit(l, it, job.ends[b]) + SLOTS + 1)

            def ending(job, e):
                return [b for b in range(job.per) if job.ends[b] == e]

            def step(name, evac, l, it, p):
                job = J[name]
                if name == "kvlru" and p >= 2:
                    split_diag(job, l, p)
                else:
                    split(job, l, it, p)

            def evacuate(name, evac, l, it, e):
                for b in ending(J[name], e):
                    if evac:
                        block_done(J[name], l, it, b)
                        evac(l, it, b)

            def head(name, l=None, prev=None, prev_evac=None):
                for p in range(LAG):
                    step(name, None, l, 0, p)
                    if prev:
                        evacuate(prev, prev_evac, l, J[prev].iters - 1, J[prev].body + p - LAG)

            def rest(name, evac, l=None, table=None, between=(), first=LAG):
                job = J[name]
                if table:
                    act.preload_act_table(table)
                for p in range(first, job.body):
                    step(name, evac, l, 0, p)
                    evacuate(name, evac, l, 0, p - LAG)
                def one(it):
                    for p in range(job.body):
                        step(name, evac, l, it, p)
                        if p < LAG:
                            evacuate(name, evac, l, it - 1, job.body + p - LAG)
                        else:
                            evacuate(name, evac, l, it, p - LAG)

                for n, other in enumerate(between):
                    if n:
                        one(n)
                    other()
                start = max(len(between), 1)
                if job.iters > start:
                    with act.Fori(start, job.iters) as it:
                        one(it)

            def tail(prev, evac, l=None):
                for p in range(LAG):
                    evacuate(prev, evac, l, J[prev].iters - 1, J[prev].body + p - LAG)

            def squares(n, half, x_from):
                t = slice(half * S, half * S + S)
                act.preload_act_table(ACT.Sqrt)
                act.wait_ge(*x_from)
                if isinstance(n, int) and half:
                    if n > 1:
                        act.wait_ge(h_ok, 8 * (n - 1))
                elif not (isinstance(n, int) and n == 0):
                    act.wait_ge(h_ok, 8 * n)
                act.activation(normed_in(n, half)[:], xT[:, :, t], ACT.Square).then_inc(sq_ok, 1)

            def norm(n, half, x_from, shift=None, split_out=True, layer=0):
                squares(n, half, x_from)
                deviations(n, half, shift, split_out, layer)

            def deviations(n, half, shift=None, split_out=True, layer=0, between=None):
                t = slice(half * S, half * S + S)
                src = normed_in(n, half)
                act.wait_ge(ss_ok, n + 1)
                if not (isinstance(n, int) and n == 0):
                    act.wait_ge(rstd_ok, n)
                act.activation(std[:], norm_sums(n, half), ACT.Sqrt, bias=eps[:, 0:1], scale=1.0 / D).then_inc(std_ok, 1)
                if split_out:
                    for c in range(DC):
                        act.wait_ge(nf_ok, n * 8 + c + 1)
                        if shift is not None:
                            act.activation(h_hi[:, c, t], src[:, c, :], ACT.Identity, bias=mod[:, layer, shift * 8 + c, half:half + 1])\
                                .then_inc(nh_ok, 1)
                        else:
                            act.copy(h_hi[:, c, t], src[:, c, :]).then_inc(nh_ok, 1)
                        if between:
                            between(c)

            def pair_deviations(n, shift, layer=0, between=None):
                act.wait_ge(ss_ok, n + 2)
                if n:
                    act.wait_ge(rstd_ok, n)
                for half, dst in enumerate((std, std_c)):
                    act.activation(dst[:], norm_sums(n + half, half), ACT.Sqrt, bias=eps[:, 0:1], scale=1.0 / D).then_inc(std_ok, 1)
                for half in range(2):
                    if half and between:
                        between()
                    for c in range(DC):
                        act.wait_ge(nf_ok, (n + half) * 8 + c + 1)
                        act.activation(h_hi[:, c, half * S:half * S + S], normed_in(n + half, half)[:, c, :], ACT.Identity,
                                       bias=mod[:, layer, shift * 8 + c, half:half + 1]).then_inc(nh_ok, 1)

            def squared_both(name, n0):
                def evac(l, it, b):
                    n = it * J[name].per + b
                    act.wait_ge(acc_free, J[name].taken(l, it, b))
                    if n:
                        act.wait_ge(sums_ok, n0 + n)
                    act.activation(act_buf[:], xT[:, 2 * n:2 * n + 2, :], ACT.Square).then_inc(sqb_ok, 1)
                return evac

            def attention(which, groups, l=None, beside=None, turns={}):
                first, pair0 = attn_base(which, l)
                again = which != "first"
                group0 = first // 2 if which == "first" else ITEMS0 // 2 + l * ((ITEMS_WIN + ITEMS_MEM) // 2)
                items = [(g, r) for g in range(len(groups)) for r in range(2)]
                for i in attn_steps(groups):
                    if beside:
                        beside(i)
                    if i < len(items):
                        g, r = items[i]
                        G = groups[g]
                        act.wait_ge(m_ok, first + i + 1)
                        pr = G["probs"][:, i % 4, 0:G["nk"]]
                        act.activation(pr, pr, ACT.Exp, bias=snm[:, i % 8:i % 8 + 1], accum_out=ssum[:, i % 8:i % 8 + 1])\
                            .then_inc(p_ok, 1)
                        if G["sink"] is not None:
                            act.activation(ses[:, i % 8:i % 8 + 1], G["sink"], ACT.Exp, bias=snm[:, i % 8:i % 8 + 1]).then_inc(p_ok, 1)
                        else:
                            act.activation(ses[:, i % 8:i % 8 + 1], nomask[:, 0:1], ACT.Copy).then_inc(p_ok, 1)
                    j = i - T_LAG
                    if 0 <= j < len(items):
                        g, r = items[j]
                        G = groups[g]
                        tiles = G["nk"] // P
                        act.wait_ge(t_ok, first + j + 1)
                        if g >= 2 or again:
                            act.wait_ge(o_ok, group0 + g - 1)
                        turned = turns.get(j, [])
                        for name in SIDE:
                            cs = [c for other, c in turned if other == name]
                            if cs:
                                n = turned.index((name, cs[0]))
                                act.copy(mod[:, SIDE.index(name), cs[0]:cs[0] + len(cs), :],
                                         pt_ps[j % 2][:, S + 2 * n:S + 2 * (n + len(cs))].rearrange("p (c w) -> p c w", w=2))
                        act.copy(G["probs_t"][:, g % 2, 0:tiles, r * P:(r + 1) * P],
                                 pt_ps[j % 2][:, 0:tiles * P].rearrange("p (t q) -> p t q", q=P)).then_inc(pt_ok, 1)
                    g = group_at(i, H_LAG, groups)
                    if g is not None and groups[g]["last"]:
                        act.wait_ge(o_ok, group0 + g + 1)
                        act.copy(groups[g]["hi"], groups[g]["acc"]).then_inc(o_hi_ok, 1)

            def beside_first(i):
                for k in range(SIDE_UNITS):
                    if side_step(k) == i:
                        name, it, p = side_unit(k)
                        split(J[name], None, it, p)
                for k in range(1, SIDE_UNITS, 2):
                    name, it, p = side_unit(k)
                    if side_step(k) + 3 == i:
                        c = 2 * (it * J[name].per + p // 2)
                        if name == "ada1" and c >= 16:
                            item = [n for n, cs in SIDE_TURNS.items() if ("ada0b", c + 1) in cs][0]
                            act.wait_ge(t_ok, item + 1)
                        block_done(J[name], None, it, p // 2)
                        c += 16 if name == "ada0b" else 0
                        act.copy(ada_s[0:4, c * P:(c + 2) * P], acc[0:4, p // 2 % 2, 0, 0:S]).then_inc(acc_free, 1)

            def squared(name):
                def evac(l, it, b):
                    x = xT[:, bass.ts(it, 2 * J[name].per), 0:S][:, 2 * b:2 * b + 2, :]
                    act.wait_ge(acc_free, J[name].taken(l, it, b))
                    act.activation(sq_of[:, b % 2], x, ACT.Square).then_inc(sqb_ok, 1)
                return evac

            def q0(l, it, b):
                act.copy(qk[:, bass.ts(it, 4), :][:, 2 * b:2 * b + 2, :], acc[:, b % 2]).then_inc(acc_free, 1)

            def kv0(l, it, b):
                if b == 0:
                    act.copy(qk[:, 8:10, :], acc[:, 0]).then_inc(acc_free, 1)
                else:
                    act.copy(v_tok[:].rearrange("p t n -> p (t n)"), acc[:, 1].rearrange("p a n -> p (a n)"))\
                        .then_inc(acc_free, 1)

            def gate_up(name, T, n0):
                def evac(l, it, b):
                    n = n0 + it + (l * 22 if l is not None else 0)
                    buf = act_buf[:, :, 0:T]
                    if b == 0:
                        if not (isinstance(n, int) and n == 0):
                            act.wait_ge(hid_ok, n)
                        act.activation(buf, acc[:, 0, :, 0:T], ACT.Silu).then_inc(acc_free, 1)
                    else:
                        act.wait_ge(acc_free, J[name].taken(l, it, 1))
                        act.copy(hid_hi[:, bass.ts(it, 2), 0:T], buf).then_inc(hid_hi_ok, 1)
                return evac

            def rope(n0, keys):
                def evac(l, it, b):
                    o = acc[:, b % 2]
                    n = n0 + 2 * it + b
                    if keys:
                        act.copy(r_k[:, bass.ts(it, 4), S:2 * S][:, 2 * b:2 * b + 2, :], o[:, :, S:2 * S])
                    if not (isinstance(n, int) and n == 0):
                        act.wait_ge(rope_ok, n)
                    act.copy(swp[0:64], o[64:128, :, 0:S])
                    act.copy(swp[64:128], o[0:64, :, 0:S]).then_inc(swp_ok, 1)
                return evac

            def rv(l, it, b):
                act.wait_ge(rope_ok, 8)
                act.copy(r_v[:, :, bass.ts(it, 2 * COLS)][:, :, b * COLS:(b + 1) * COLS],
                         acc[:, b % 2].rearrange("p a (r n) -> p (a r) n", r=2)).then_inc(acc_free, 1)

            def rg(l, it, b):
                act.activation(r_g[:, bass.ts(it, 4), :][:, 2 * b:2 * b + 2, :], acc[:, b % 2, :, 0:S], ACT.Silu)\
                    .then_inc(acc_free, 1)

            def memk(l, it, b):
                act.copy(km[:, 2 * b:2 * b + 2, :], acc[:, b, :, 0:S]).then_inc(acc_free, 1)

            def memv(l, it, b):
                act.copy(vm[:, :, b * COLS:(b + 1) * COLS], acc[:, b, :, 0:S]).then_inc(acc_free, 1)

            def xr(l, it, b):
                act.copy(XR[:, bass.ts(it, 4), 4:4 + S][:, 2 * b:2 * b + 2, :], acc[:, b, :, 0:S]).then_inc(acc_free, 1)

            def yr(l, it, b):
                act.activation(gy[:, bass.ts(it, 4), :][:, 2 * b:2 * b + 2, :], acc[:, b, :, 0:S], ACT.Gelu_apprx_tanh)\
                    .then_inc(acc_free, 1)

            def gates_e(l, it, b):
                for cb in range(2):
                    col = cur[:, bass.ts(it, 4)][:, 2 * b + cb:2 * b + cb + 1]
                    ins = act.activation(gates[:, bass.ts(it, 4), :][:, 2 * b + cb, :], acc[:, b, cb, 0:S], ACT.Sigmoid, bias=col)
                ins.then_inc(acc_free, 1)

            def kvlru(l, it, b):
                if b == 0:
                    act.copy(v_T[:], acc[:, 0, 0, 0:S]).then_inc(acc_free, 1)
                elif b == 1:
                    for g in range(2):
                        for half in range(2):
                            ins = act.copy(k_d[64 * half:64 * half + 64, g, :], acc[64 * g:64 * g + 64, 1, 0, 0:S])
                    ins.then_inc(acc_free, 1)
                else:
                    dst, bias = (R, BA) if b < 4 else (GI, BX)
                    for c in range(4):
                        cc = 4 * (b % 2) + c
                        ins = act.activation(dst[:, cc, :], acc[:, b % 2, c // 2, (c % 2) * S:(c % 2) * S + S], ACT.Sigmoid,
                                             bias=cur[:, bias + cc:bias + cc + 1])
                    ins.then_inc(acc_free, 1)

            def q_e(l, it, b):
                act.copy(q_2[:, 2 * b:2 * b + 2, :], acc[:, b, :, 0:S]).then_inc(acc_free, 1)

            def cq_e(l, it, b):
                act.copy(cq_2[:, 2 * b:2 * b + 2, :], acc[:, b, :, 0:S]).then_inc(acc_free, 1)

            def mem_out(l, it, b):
                act.wait_ge(mg_ok, 1 + b + l * 4)
                act.copy(h_hi[:, 2 * b:2 * b + 2, S:2 * S], gates[:, 2 * b:2 * b + 2, :]).then_inc(mgh_ok, 1)

            act.wait_ge(setup, 2)
            act.wait_ge(prm_ok, 1)
            act.activation(c_act[:], prm[:, 0, C_COL:C_COL + 16], ACT.Silu).then_inc(c_ok, 1)
            act.wait_ge(c_ok, 1)
            cc = c_act[:].rearrange("p (w k) -> p k w", w=2)
            act.copy(c_parts[:].rearrange("p k (w s) -> p k w s", s=2)[:, :, :, 0], cc).then_inc(c_hi_ok, 1)
            head("ada0a")
            rest("ada0a", None)
            squares(0, 0, (x_done, 4))
            squares(1, 1, (x_done, X_START))
            head("q0", None, "ada0a", None)
            pair_deviations(0, 0)
            rest("q0", q0)
            act.wait_ge(soft_v, 1)
            act.activation(soft_e[:], soft_t[:], ACT.Exp).then_inc(soft_a, 1)
            head("kv0", None, "q0", q0)
            rest("kv0", kv0)
            act.preload_act_table(ACT.Sqrt)
            for c in range(10):
                if c == 8:
                    tail("kv0", kv0)
                act.wait_ge(acc_free, J["kv0"].taken(None, 0, 0) if c >= 8 else J["q0"].done())
                if c >= 2:
                    act.wait_ge(hss, c - 1)
                act.activation(sq_b[:, c % 2, :], qk[:, c, :], ACT.Square).then_inc(hsq, 1)
            act.wait_ge(hss, 10)
            act.activation(sd_b[0:20, 0, :], wk[0:20, 0, :], ACT.Sqrt, bias=eps[0:20, 0:1], scale=1.0 / HD).then_inc(hstd, 1)
            act.preload_act_table(ACT.Exp)
            for i in range(-SIDE_START - 1, 0):
                beside_first(i)
                c = {-7: 0, -5: 1}.get(i)
                if c is not None:
                    act.wait_ge(hqk, c + 1)
                    for g in range(2):
                        for half in range(2):
                            act.copy(k_dup[64 * half:64 * half + 64, 2 * c + g, :], qk[64 * g:64 * g + 64, 8 + c, :]).then_inc(kd_ok, 1)
            attention("first", groups_first(), None, beside_first, SIDE_TURNS)
            head("wo0")
            rest("wo0", squared_both("wo0", 0), None, None, [lambda: None] * J["wo0"].iters)
            act.preload_act_table(ACT.Sqrt)
            head("gu0", None, "wo0", squared_both("wo0", 0))
            pair_deviations(2, 3)
            rest("gu0", gate_up("gu0", 2 * S, 0), None, ACT.Silu)
            head("dn0", None, "gu0", gate_up("gu0", 2 * S, 0))
            rest("dn0", squared_both("dn0", 3))
            act.preload_act_table(ACT.Sqrt)
            head("rq", None, "dn0", squared_both("dn0", 3))
            pair_deviations(4, 0, 1, lambda: step("rq", None, None, 0, 3))
            rest("rq", rope(0, False), first=4)
            head("rk", None, "rq", rope(0, False))
            rest("rk", rope(4, True))
            head("rv", None, "rk", rope(4, True))
            def decays(h):
                d = r_ds[h % 2]
                act.wait_ge(dx_in, h + 1)
                act.activation(d[:, 0:2, :], d[:, 0:2, :], ACT.Exp).then_inc(dx_e, 1)
                act.activation(d[:, 2:4, :], since, ACT.Exp, scale=decay[:, 0, h:h + 1]).then_inc(dc_e, 1)
                if h:
                    act.wait_ge(d_ok, h)
                act.activation(back_c, since, ACT.Exp, scale=decay[:, 1, 4 + h:5 + h], bias=decay[:, 2, 4 + h:5 + h]).then_inc(dc_e, 1)

            def gn(h):
                for r in range(2):
                    act.wait_ge(mv_ok, 2 * h + r + 1)
                    act.activation(gstd[:, r:r + 1], mv[:, r, 1:2], ACT.Sqrt, bias=eps[:, 0:1]).then_inc(gs_ok, 1)

            def z_high(h):
                act.wait_ge(z_ok, h + 1)
                act.copy(z_hi[:, 4 * h:4 * h + 4, :], act_buf[:].rearrange("p a (b t) -> p (a b) t", b=2)).then_inc(zh_ok, 1)

            act.wait_ge(in_tabs, 48)
            decays(0)
            decays(1)
            rest("rv", rv)
            head("rg", None, "rv", rv)
            rest("rg", rg, None, ACT.Silu)
            head("rwo", None, "rg", rg)

            for h in range(RH + 2):
                if 2 <= h + 2 < RH:
                    decays(h + 2)
                if h >= 2:
                    z_high(h - 2)
                if h < RH:
                    gn(h)
            rest("rwo", squared("rwo"))
            act.preload_act_table(ACT.Sqrt)
            head("gu1", None, "rwo", squared("rwo"))
            deviations(6, 0, 3, layer=1)
            rest("gu1", gate_up("gu1", S, 11), None, ACT.Silu)
            head("dn1", None, "gu1", gate_up("gu1", S, 11))
            rest("dn1", squared("dn1"))

            with act.Fori(0, LAYERS2) as l:
                n0 = NORMS1 + l * 4
                step("gua", None, l, 0, 0)
                act.preload_act_table(ACT.Sqrt)
                deviations(n0, 0, between=lambda c: step("gua", None, l, 0, c // 2) if c in (2, 4) else None)
                rest("gua", gate_up("gua", S, 22), l, ACT.Silu)
                squares(n0 + 1, 1, (x_done, X_MEM))
                head("dna", l, "gua", gate_up("gua", S, 22))
                deviations(n0 + 1, 1, between=lambda c: step("dna", None, l, 0, 2 + c // 2) if c in (2, 4) else None)
                rest("dna", squared("dna"), l, first=5)
                head("memk", l, "dna", squared("dna"))
                rest("memk", memk, l)
                head("memv", l, "memk", memk)
                act.preload_act_table(ACT.Sqrt)

                def memv_xr(c):
                    if c == 1:
                        step("memv", None, l, 0, 3)
                    if c in (3, 5, 7):
                        step("xr", None, l, 0, (c - 3) // 2)
                        evacuate("memv", memv, l, 0, (c - 3) // 2 + 1)
                deviations(n0 + 2, 0, between=memv_xr)
                rest("xr", xr, l)
                head("yr", l, "xr", xr)
                rest("yr", yr, l, ACT.Gelu_apprx_tanh)
                head("q", l, "yr", yr)
                act.preload_act_table(ACT.Sigmoid)
                act.wait_ge(conv_ok, 32 + l * 32)
                act.copy(h_hi[:, :, S:2 * S], XC[:]).then_inc(xch_ok, 1)
                rest("q", q_e, l)
                head("kvlru", l, "q", q_e)
                rest("kvlru", kvlru, l)
                head("gates", l, "kvlru", kvlru)

                def a_squared():
                    for c in range(DC):
                        act.activation(XR[:, c, 0:S], R[:, c, :], ACT.Exp, scale=cur[:, CUR + 8 + c:CUR + 9 + c]).then_inc(e2_ok, 1)

                def a_itself():
                    for c in range(DC):
                        act.activation(R[:, c, :], R[:, c, :], ACT.Exp, scale=cur[:, CUR + c:CUR + c + 1]).then_inc(e2_ok, 1)

                def multiplier():
                    act.wait_ge(cl_ok, 1 + l)
                    act.activation(XR[:, :, 0:S], XR[:, :, 0:S], ACT.Sqrt, scale=-1.0, bias=ones[:, 0:1]).then_inc(mu_ok, 1)

                rest("gates", gates_e, l, ACT.Sigmoid, [a_squared, a_itself, multiplier])
                head("cq", l, "gates", gates_e)
                act.wait_ge(lru_ok, 1 + l)
                act.copy(h_hi[:, :, S:2 * S], XC[:]).then_inc(lruh_ok, 1)
                rest("cq", cq_e, l)
                head("lru_out", l, "cq", cq_e)

                def recurrence_out(i):
                    for k in range(OUT_UNITS + LAG):
                        it, p = divmod(k, J["lru_out"].body)
                        if k >= LAG and split_step(k) == i:
                            if k < OUT_UNITS:
                                step("lru_out", None, l, it, p)
                            else:
                                step("attn_out", None, l, 0, k - OUT_UNITS)

                attention("second", groups_window() + groups_memory(), l, recurrence_out)
                rest("attn_out", None, l)
                head("mem_out", l, "attn_out", None)
                rest("mem_out", None, l)
                for p in range(SLOTS):
                    step("w_out", None, l, 0, p)
                    mem_out(l, 0, p)
                rest("w_out", squared("w_out"), l, first=SLOTS)
                act.preload_act_table(ACT.Sqrt)
                head("gub", l, "w_out", squared("w_out"))
                deviations(n0 + 3, 0)
                rest("gub", gate_up("gub", S, 33), l, ACT.Silu)
                head("dnb", l, "gub", gate_up("gub", S, 33))
                rest("dnb", squared("dnb"), l)
            act.preload_act_table(ACT.Sqrt)
            deviations(NORM_LAST, 0, split_out=False)
            for n, r, half in ((1, 0, 0), (2, 1, 0), (4, 1, 1)):
                act.wait_ge(fin_t, n)
                act.copy(rows[:, r * D + half * 512:r * D + (half + 1) * 512], fin_ps[r][half]).then_inc(fin_ok[r], 1)

        @block.vector
        def _(dve):
            def split(job, l, it, p):
                s, nk = p % SLOTS, job.unit_chunks[p]
                dve.wait_ge(hi_done, job.unit(l, it, p) + 1)
                dve.tensor_tensor(w_lo[:, s, 0:nk, :], raw[:, s, 0:nk, :], w_hi[:, s, 0:nk, :], ALU.subtract).then_inc(lo_done, 1)

            def split_diag(job, l, p):
                src = raw[:, p, 0:2, :].rearrange("p k n -> p (k n)").rearrange("p (c j) -> p c j", j=64)
                hi, lo = [w_diag[:, p - 2, n].rearrange("p (c j) -> p c j", j=P) for n in range(2)]
                dve.wait_ge(hi_done, job.unit(l, 0, p) + 1)
                dve.tensor_tensor(lo[0:64, :, 0:64], src[0:64], hi[0:64, :, 0:64], ALU.subtract)
                dve.tensor_tensor(lo[64:128, :, 64:128], src[64:128], hi[64:128, :, 64:128], ALU.subtract).then_inc(lo_done, 1)

            def block_done(job, l, it, b):
                dve.wait_ge(units_used, job.unit(l, it, job.ends[b]) + SLOTS + 1)

            def ending(job, e):
                return [b for b in range(job.per) if job.ends[b] == e]

            def step(name, l, it, p):
                job = J[name]
                if name == "kvlru" and p >= 2:
                    split_diag(job, l, p)
                else:
                    split(job, l, it, p)

            def evacuate(name, evac, l, it, e):
                for b in ending(J[name], e):
                    if evac:
                        block_done(J[name], l, it, b)
                        evac(l, it, b)

            def head(name, l=None, prev=None, prev_evac=None):
                for p in range(LAG):
                    step(name, l, 0, p)
                    if prev:
                        evacuate(prev, prev_evac, l, J[prev].iters - 1, J[prev].body + p - LAG)

            def rest(name, evac, l=None, between=(), first=LAG):
                job = J[name]
                for p in range(first, job.body):
                    step(name, l, 0, p)
                    evacuate(name, evac, l, 0, p - LAG)

                def one(it):
                    for p in range(job.body):
                        step(name, l, it, p)
                        if p < LAG:
                            evacuate(name, evac, l, it - 1, job.body + p - LAG)
                        else:
                            evacuate(name, evac, l, it, p - LAG)

                for n, other in enumerate(between):
                    if n:
                        one(n)
                    other()
                start = max(len(between), 1)
                if job.iters > start:
                    with dve.Fori(start, job.iters) as it:
                        one(it)

            def tail(prev, evac, l=None):
                for p in range(LAG):
                    evacuate(prev, evac, l, J[prev].iters - 1, J[prev].body + p - LAG)

            def norm(n, half, gain_of, shift=None, split_out=True, layer=0, between=None):
                dve.wait_ge(std_ok, n + 1)
                dve.reciprocal(rstd[:], std[:]).then_inc(rstd_ok, 1)
                dve.wait_ge(rstd_ok, n + 1)
                normed_chunks(n, half, gain_of, rstd, shift, split_out, layer, between)

            def pair_norm(n, gain_of, shift, layer=0, before=None, between=None):
                def inverse(half):
                    dve.wait_ge(std_ok, n + half + 1)
                    dve.reciprocal((rstd, rstd_c)[half][:], (std, std_c)[half][:]).then_inc(rstd_ok, 1)

                inverse(0)
                if before:
                    inverse(1)
                    before()
                for half, r in enumerate((rstd, rstd_c)):
                    if half and not before:
                        inverse(1)
                    dve.wait_ge(rstd_ok, n + half + 1)
                    normed_chunks(n + half, half, gain_of(half), r, shift, True, layer)
                    if not half and between:
                        between()

            def normed_chunks(n, half, gain_of, r, shift, split_out, layer, between=None):
                t = slice(half * S, half * S + S)
                nf_n = normed_in(n, half)

                def normed(c):
                    dve.scalar_tensor_tensor(nf_n[:, c, :], xT[:, c, t], gain_of(c), r[:], ALU.mult, ALU.mult).then_inc(nf_ok, 1)

                def low(c):
                    dve.wait_ge(nh_ok, n * 8 + c + 1)
                    if shift is not None:
                        dve.scalar_tensor_tensor(h_lo[:, c, t], nf_n[:, c, :], mod[:, layer, shift * 8 + c, half:half + 1], h_hi[:, c, t],
                                                 ALU.add, ALU.subtract).then_inc(h_ok, 1)
                    else:
                        dve.tensor_tensor(h_lo[:, c, t], nf_n[:, c, :], h_hi[:, c, t], ALU.subtract).then_inc(h_ok, 1)

                for c in range(DC):
                    normed(c)
                    if c and split_out:
                        low(c - 1)
                    if between:
                        between(c)
                if split_out:
                    low(DC - 1)

            def attention(which, groups, l=None, beside=None):
                first, pair0 = attn_base(which, l)
                again = which != "first"
                items = [(g, r) for g in range(len(groups)) for r in range(2)]
                for i in attn_steps(groups):
                    if i < len(items):
                        g, r = items[i]
                        G = groups[g]
                        c = i % 8
                        dve.wait_ge(s_ok, first + i + 1)
                        if i >= 4 or again:
                            dve.wait_ge(t_ok, first + i - 3)
                        if G.get("bias"):
                            dve.wait_ge(bias_ok, 1 + g + l * WH)
                        if again:
                            dve.memset(passed[:, c:c + 1], 0.0)
                        dve.tensor_tensor_reduce(G["probs"][:, i % 4, 0:G["nk"]], sc_ps[i % 2][:, 0:G["nk"]], G["mask"][r], G["scale"],
                                                 -3.0e38, ALU.add, ALU.max, smx[:, c:c + 1]).then_inc(m_raw, 1)
                    j = i - N_LAG
                    done = 0 <= j < len(items)
                    k = j % 8
                    if done:
                        dve.wait_ge(p_ok, first * 2 + 2 * j + 2)
                        dve.tensor_tensor(sden[:, k:k + 1], ssum[:, k:k + 1], ses[:, k:k + 1], ALU.add).then_inc(den_ok, 1)
                    if i < len(items):
                        dve.wait_ge(m_raw, first + i + 1)
                        if G["sink"] is not None:
                            dve.tensor_scalar(snm[:, c:c + 1], smx[:, c:c + 1], G["sink"], -1.0, ALU.max, ALU.mult).then_inc(m_ok, 1)
                        else:
                            dve.tensor_scalar(snm[:, c:c + 1], smx[:, c:c + 1], -1.0, None, ALU.mult).then_inc(m_ok, 1)
                    if done:
                        dve.wait_ge(den_ok, first + j + 1)
                        dve.reciprocal(srec[:, k:k + 1], sden[:, k:k + 1]).then_inc(rec_ok, 1)
                    if done:
                        g, r = items[j]
                        dve.wait_ge(rec_ok, first + j + 1)
                        pr = groups[g]["probs"][:, j % 4, 0:groups[g]["nk"]]
                        dve.tensor_scalar(pr, pr, srec[:, k:k + 1], None, ALU.mult).then_inc(pn_ok, 1)
                    g = group_at(i, L_LAG, groups)
                    if g is not None and groups[g]["last"]:
                        G = groups[g]
                        dve.wait_ge(o_hi_ok, pair0 + G["pair"] + 1)
                        dve.tensor_tensor(G["lo"], G["acc"], G["hi"], ALU.subtract).then_inc(o_done, 1)
                    if beside:
                        beside(i)

            def beside_first(i):
                for k in range(SIDE_UNITS):
                    if side_step(k) == i:
                        name, it, p = side_unit(k)
                        split(J[name], None, it, p)

            def ada(l, it, b):
                dve.tensor_copy(ada_s[0:4, bass.ts(it, 2 * COLS)][:, b * COLS:(b + 1) * COLS], acc[0:4, b, 0, 0:S]).then_inc(acc_free, 1)

            def square_last(name, l=None):
                n = J[name].iters * J[name].per - 1
                dve.wait_ge(acc_free, J[name].done(l))
                dve.wait_ge(sqb_ok, squared_before(name, l) + n)
                x = xT[:, 2 * n:2 * n + 2, 0:S]
                dve.tensor_tensor(sq_of[:, n % 2], x, x, ALU.mult).then_inc(sqb_ok, 1)

            def residual(layer, gate, both, bpi):
                def evac(l, it, b):
                    x = xT[:, bass.ts(it, 2 * bpi), :]
                    for cb in range(2):
                        for half in range(2 if both else 1):
                            t = slice(half * S, half * S + S)
                            col = mod[:, layer, bass.ds(gate * 8 + it * 2 * bpi + 2 * b + cb, 1), half]
                            ins = dve.scalar_tensor_tensor(x[:, 2 * b + cb, t], acc[:, b % 2, cb, t], col, x[:, 2 * b + cb, t],
                                                           ALU.mult, ALU.add)
                    ins.then_inc(acc_free, 1)
                return evac

            def residual2(factor, bpi):
                def evac(l, it, b):
                    x = xT[:, bass.ts(it, 2 * bpi), 0:S][:, 2 * b:2 * b + 2, :]
                    dve.scalar_tensor_tensor(x, acc[:, b % 2, :, 0:S], factor, x, ALU.mult, ALU.add)\
                        .then_inc(acc_free, 1)
                return evac

            def gate_up(name, T, n0):
                def evac(l, it, b):
                    if b == 0:
                        return
                    n = n0 + it + (l * 22 if l is not None else 0)
                    buf = act_buf[:, :, 0:T]
                    dve.wait_ge(acc_free, J[name].taken(l, it, 0))
                    dve.tensor_tensor(buf, buf, acc[:, 1, :, 0:T], ALU.mult).then_inc(acc_free, 1)
                    dve.wait_ge(hid_hi_ok, n + 1)
                    dve.tensor_tensor(hid_lo[:, bass.ts(it, 2), 0:T], buf, hid_hi[:, bass.ts(it, 2), 0:T], ALU.subtract).then_inc(hid_ok, 1)
                return evac

            def rope(n0, dst):
                def evac(l, it, b):
                    n = n0 + 2 * it + b
                    dve.wait_ge(swp_ok, n + 1)
                    dve.tensor_tensor(rot[:], acc[:, b % 2, :, 0:S], cos_r[:], ALU.mult).then_inc(acc_free, 1)
                    dve.tensor_tensor(swp[:], swp[:], sin_r[:], ALU.mult).then_inc(rot_ok, 1)
                    dve.wait_ge(rot_ok, n + 1)
                    dve.tensor_tensor(dst[:, bass.ts(it, 4), 0:S][:, 2 * b:2 * b + 2, :], rot[:], swp[:], ALU.add).then_inc(rope_ok, 1)
                return evac

            def branch(i):
                job = J[("attn_out", "lru_out", "mem_out")[i]]

                def evac(l, it, b):
                    bb = (lambda k: gates[:, 8 * k + 2 * b:8 * k + 2 * b + 2, :]) if job.iters == 1 else \
                        (lambda k: gates[:, 8 * k:8 * k + 8, :][:, bass.ts(it, 4), :][:, 2 * b:2 * b + 2, :])
                    out = acc[:, b % 2, 0, :].rearrange("p (c t) -> p c t", c=2) if i == 1 else acc[:, b % 2, :, 0:S]
                    dve.tensor_tensor(bb(i), bb(i), out, ALU.mult).then_inc(acc_free, 1)
                    if i == 0:
                        dve.wait_ge(acc_free, job.taken(l, it, b))
                        dve.tensor_tensor(bb(0), bb(0), bb(1), ALU.add).then_inc(sum2_ok, 1)
                    if i == 2:
                        dve.wait_ge(acc_free, job.taken(l, it, b))
                        dve.wait_ge(sum2_ok, 1 + b + l * 4)
                        dve.tensor_tensor(bb(0), bb(0), bb(2), ALU.add).then_inc(mg_ok, 1)
                return evac

            def modulations(n, layer, src, c0, c1):
                dve.tensor_tensor(mod[:, layer, c0:c1, :], src, prm[:, 0, 48 * layer + c0:48 * layer + c1].unsqueeze(2)
                                  .broadcast_to((P, c1 - c0, 2)), ALU.add).then_inc(mod_ok, 1)
                dve.wait_ge(mod_ok, n)
                for k, norm_g in ((0, prm[:, 0, NORM1 + 8 * layer:NORM1 + 8 * layer + 8]), (1, prm[:, 3, NORM2 + 8 * layer:NORM2 + 8 * layer + 8])):
                    if c0 <= 8 + 24 * k < c1:
                        dve.scalar_tensor_tensor(gain[:, layer, k], mod[:, layer, 8 + 24 * k:16 + 24 * k, :], 1.0,
                                                 norm_g.unsqueeze(2).broadcast_to((P, DC, 2)), ALU.add, ALU.mult).then_inc(gain_ok, 1)
                dve.wait_ge(gain_ok, (1, 2, 4)[n - 1])

            def inputs():
                banks = [wk[:, 0], wk[:, 1], wk[:, 2], acc[:, 0, 1]]
                turned_in(0, 0, banks)
                turned_in(4, 1, banks)

            def gain_at(layer, k):
                return lambda half: lambda c: gain[:, layer, k, c, half:half + 1]

            dve.memset(eps[:], EPS).then_inc(setup, 1)
            dve.memset(nomask[:], 0.0).then_inc(setup, 1)
            dve.memset(smx[:], 0.0).then_inc(lo_done, SLOTS)
            dve.memset(snm[:], 0.0).then_inc(units_used, SLOTS)
            dve.memset(sden[:], 0.0).then_inc(acc_free, 2)
            dve.wait_ge(prm_t, 1)
            dve.tensor_copy(prm[:, 0, :], wk[:, 3, 0:P]).then_inc(prm_ok, 1)

            def turned_in(n0, half, banks):
                for g in range(4):
                    dve.wait_ge(turned, n0 + g + 1)
                    dve.tensor_copy(xT[:, 2 * g:2 * g + 2, half * S:(half + 1) * S],
                                    banks[g].rearrange("p (c t) -> p c t", c=2)).then_inc(x_done, 1)

            dve.wait_ge(c_hi_ok, 1)
            parts = c_parts[:].rearrange("p k (w s) -> p k w s", s=2)
            dve.tensor_tensor(parts[:, :, :, 1], c_act[:].rearrange("p (w k) -> p k w", w=2), parts[:, :, :, 0], ALU.subtract)\
                .then_inc(c_lo_ok, 1)
            head("ada0a")

            rest("ada0a", ada, None, [lambda: None, inputs])
            head("q0", None, "ada0a", ada)

            def first_modulations():
                dve.wait_ge(ada_sum, 1)
                modulations(1, 0, wk[:, 0, 0:32].rearrange("p (c w) -> p c w", w=2), 0, 16)
            pair_norm(0, gain_at(0, 0), 0, before=first_modulations)
            dve.wait_ge(prm_t, 2)
            dve.tensor_copy(prm[:, 1:3, 0:CUR], wk[:, 0, P:3 * P].rearrange("p (t n) -> p t n", t=2)[:, :, 0:CUR]).then_inc(prm_ok, 1)
            dve.tensor_copy(prm[:, 3, 0:PRM3], wk[:, 0, 3 * P:3 * P + PRM3]).then_inc(prm_ok, 1)
            dve.wait_ge(prm_ok, 3)
            dve.tensor_copy(soft_in[:, 8:24].rearrange("p (l n) -> p l n", l=2), prm[:, 1:3, LAM:LAM + 8]).then_inc(soft_ok, 1)
            dve.wait_ge(in_prm, 16 * PRM_DMAS)
            dve.wait_ge(soft_ok, 1)
            dve.scalar_tensor_tensor(soft_t[:], soft_in[:], -1.0, soft_in[:], ALU.mult, ALU.min).then_inc(soft_v, 1)
            rest("q0", None)
            dve.wait_ge(soft_a, 1)
            n = [1]

            def chained(ins):
                ins.then_inc(soft_ok, 1)
                n[0] += 1
                dve.wait_ge(soft_ok, n[0])

            chained(dve.tensor_scalar(soft_w[:], soft_e[:], 2.0, None, ALU.add))
            chained(dve.reciprocal(soft_p[:], soft_w[:]))
            chained(dve.tensor_tensor(soft_w[:], soft_e[:], soft_p[:], ALU.mult))
            chained(dve.tensor_tensor(soft_e[:], soft_w[:], soft_w[:], ALU.mult))
            chained(dve.tensor_scalar(soft_p[:], soft_e[:], 1.0 / 15, 1.0 / 13, ALU.mult, ALU.add))
            for k in (11, 9, 7, 5, 3, 1):
                chained(dve.tensor_tensor(soft_p[:], soft_p[:], soft_e[:], ALU.mult))
                chained(dve.tensor_scalar(soft_p[:], soft_p[:], 1.0 / k, None, ALU.add))
            chained(dve.tensor_tensor(soft_p[:], soft_p[:], soft_w[:], ALU.mult))
            chained(dve.tensor_scalar(soft_t[:], soft_in[:], -1.0, 0.0, ALU.mult, ALU.max))
            chained(dve.scalar_tensor_tensor(soft[:], soft_p[:], 2.0, soft_t[:], ALU.mult, ALU.add))
            dve.tensor_scalar(decay[:, 0, :], soft[:, 0:8], -1.0, None, ALU.mult)
            dve.tensor_copy(decay[:, 1, :], soft[:, 0:8])
            dve.tensor_scalar(decay[:, 2, :], soft[:, 0:8], -2.0 * S, None, ALU.mult)
            lam = soft[:, 8:24].rearrange("p (l n) -> p l n", l=2)
            dve.tensor_scalar(lam_s[:, :, 0, :], lam, -8.0, None, ALU.mult)
            chained(dve.tensor_scalar(lam_s[:, :, 1, :], lam, -16.0, None, ALU.mult))

            head("kv0", None, "q0", None)
            rest("kv0", None)
            dve.wait_ge(in_attn, 96)
            dve.wait_ge(hstd, 1)
            dve.reciprocal(sd_b[0:20, 0, :], sd_b[0:20, 0, :]).then_inc(hrec, 1)
            part_ps = [wk[:, 3], acc[:, 0, 1]]
            for c in range(11):
                if c < 10:
                    dve.wait_ge(hback, c + 1)
                    n = HEAD_ORDER[c]
                    col = Q_N if n < 8 else K_N
                    dve.scalar_tensor_tensor(qk[:, n, :], qk[:, n, :], prm[:, 3, col:col + 1], wk[:, 1 + c % 2, :], ALU.mult, ALU.mult)\
                        .then_inc(hn, 1)
                if c:
                    b = c - 1
                    dve.wait_ge(hperm, b + 1)
                    n = HEAD_ORDER[b]
                    dve.tensor_tensor(rot_b[:, b % 2, 0, :], qk[:, n, 0:S], cos_a[:, :], ALU.mult)
                    dve.tensor_tensor(rot_b[:, b % 2, 1, :], part_ps[b % 2][:, 0:S], sin_a[:, :], ALU.mult).then_inc(hrot, 1)
                    dve.wait_ge(hrot, b + 1)
                    dve.tensor_tensor(qk[:, n, 0:S], rot_b[:, b % 2, 0, :], rot_b[:, b % 2, 1, :], ALU.add).then_inc(hqk, 1)
                beside_first(c - 11)
            attention("first", groups_first(), None, beside_first)
            head("wo0")
            dve.wait_ge(pt_ok, ITEMS0)
            modulations(2, 0, mod[:, 0, 16:48, :], 16, 48)
            modulations(3, 1, mod[:, 1], 0, 48)
            rest("wo0", residual(0, 2, True, 2))
            head("gu0", None, "wo0", residual(0, 2, True, 2))
            pair_norm(2, gain_at(0, 1), 3)
            rest("gu0", gate_up("gu0", 2 * S, 0))
            head("dn0", None, "gu0", gate_up("gu0", 2 * S, 0))
            rest("dn0", residual(0, 5, True, 2))
            head("rq", None, "dn0", residual(0, 5, True, 2))
            pair_norm(4, gain_at(1, 0), 0, layer=1, between=lambda: step("rq", None, 0, 3))
            dve.wait_ge(in_rope, 32)
            rest("rq", rope(0, r_q), first=4)
            head("rk", None, "rq", rope(0, r_q))
            rest("rk", rope(4, r_k))
            head("rv", None, "rk", rope(4, r_k))
            def decays(h):
                d = r_ds[h % 2]
                if h >= 2:
                    dve.wait_ge(rp_ok, 2 * h - 2)
                dve.tensor_scalar(d[:, 0:2, :], ahead, decay[:, 0, h:h + 1], None, ALU.mult).then_inc(dx_a, 1)
                dve.wait_ge(dx_a, h + 1)
                dve.scalar_tensor_tensor(d[:, 0:2, :], behind, decay[:, 0, 4 + h:5 + h], d[:, 0:2, :], ALU.mult, ALU.add)\
                    .then_inc(dx_in, 1)
                dve.wait_ge(dx_e, h + 1)
                for kt in range(2):
                    diag = d[:, kt, kt * P:(kt + 1) * P]
                    dve.tensor_tensor(diag, diag, ident[:, :], ALU.add)
                dve.wait_ge(dc_e, 2 * h + 2)
                dve.tensor_tensor(d[:, 2:4, :], d[:, 2:4, :], back_c, ALU.add).then_inc(d_ok, 1)

            dve.wait_ge(in_tabs, 48)
            decays(0)
            decays(1)
            rest("rv", None)
            head("rg", None, "rv", None)
            rest("rg", None)
            head("rwo", None, "rg", None)
            z = act_buf[:].rearrange("p a (b t) -> p (a b) t", b=2)
            for h in range(RH + 2):
                if h < RH:
                    dve.wait_ge(d_ok, h + 1)
                    for b in range(2):
                        dve.wait_ge(rs_ok, 2 * h + b + 1)
                        if h:
                            dve.wait_ge(ro_ok, 2 * h)
                        dve.scalar_tensor_tensor(r_p[:, 2 * b:2 * b + 2, :], wk[:, b, :].rearrange("p (k n) -> p k n", k=2), RQ ** -0.5,
                                                 r_ds[h % 2][:, 2 * b:2 * b + 2, :], ALU.mult, ALU.mult).then_inc(rp_ok, 1)
                if 1 <= h <= RH:
                    g = h - 1
                    for r in range(2):
                        i = 2 * g + r + 1
                        dve.wait_ge(gs_ok, i)
                        dve.reciprocal(gstd[:, r:r + 1], gstd[:, r:r + 1]).then_inc(gr_ok, 1)
                        dve.wait_ge(gr_ok, i)
                        if g:
                            dve.wait_ge(yt_ok, g)
                        dve.tensor_scalar(r_y[:, r, :], ro_ps[g % 2][r], mv[:, r, 0:1], gstd[:, r:r + 1], ALU.subtract, ALU.mult)\
                            .then_inc(y_ok, 1)
                if h + 2 < RH:
                    decays(h + 2)
                if h >= 2:
                    g = h - 2
                    dve.wait_ge(acc_free, J["rg"].done())
                    dve.wait_ge(yt_ok, g + 1)
                    if g:
                        dve.wait_ge(z_done, g)
                    for c in range(4):
                        dve.scalar_tensor_tensor(z[:, c, :], ry_ps[g][c // 2][:, (c % 2) * S:(c % 2 + 1) * S],
                                                 prm[:, 3, GN_G + 4 * g + c:GN_G + 4 * g + c + 1], r_g[:, 4 * g + c, :],
                                                 ALU.mult, ALU.mult).then_inc(z_ok if c == 3 else z_part, 1)
                if h < RH:
                    for r in range(2):
                        i = 2 * h + r + 1
                        dve.wait_ge(ro_ok, i)
                        dve.bn_stats(stats[:, r, :], ro_ps[h % 2][r]).then_inc(bn_ok, 1)
                        dve.wait_ge(bn_ok, i)
                        dve.bn_aggr(mv[:, r, :], stats[:, r, :]).then_inc(mv_ok, 1)
                if h >= 2:
                    dve.wait_ge(zh_ok, g + 1)
                    dve.tensor_tensor(z_lo[:, 4 * g:4 * g + 4, :], z, z_hi[:, 4 * g:4 * g + 4, :], ALU.subtract).then_inc(z_done, 1)
            rest("rwo", residual(1, 2, False, 2))
            head("gu1", None, "rwo", residual(1, 2, False, 2))
            turned_in(8, 1, [wk[:, 0], wk[:, 1], wk[:, 2], wk[:, 0]])
            norm(6, 0, gain_at(1, 1)(0), 3, layer=1)
            rest("gu1", gate_up("gu1", S, 11))
            head("dn1", None, "gu1", gate_up("gu1", S, 11))
            rest("dn1", residual(1, 5, False, 2))
            tail("dn1", residual(1, 5, False, 2))
            square_last("dn1")

            with dve.Fori(0, LAYERS2) as l:
                n0 = NORMS1 + l * 4
                dve.tensor_copy(cur[:, 0:CUR], prm[:, bass.ds(l + 1, 1), 0:CUR].rearrange("p o n -> p (o n)")).then_inc(cur_ok, 1)
                dve.tensor_copy(cur[:, CUR:CUR + 16], lam_s[:, bass.ds(l, 1)].rearrange("p o w c -> p (o w c)")).then_inc(cur_ok, 1)
                dve.tensor_copy(sink_l[:], sinks[:, 16:32].rearrange("p (l h) -> p l h", l=2)[:, bass.ds(l, 1), :]
                                .rearrange("p o h -> p (o h)")).then_inc(cur_ok, 1)
                dve.wait_ge(cur_ok, 3 + l * 3)

                def gain_in(col):
                    return lambda c: cur[:, col + c:col + c + 1]

                step("gua", l, 0, 0)
                norm(n0, 0, gain_in(FFN1_N), between=lambda c: step("gua", l, 0, c // 2 - 1) if c in (4, 6) else None)
                rest("gua", gate_up("gua", S, 22), l)
                head("dna", l, "gua", gate_up("gua", S, 22))
                norm(n0 + 1, 1, gain_in(MEM_N), between=lambda c: step("dna", l, 0, 2 + c // 2) if c in (2, 4) else None)
                rest("dna", residual2(0.5, 2), l, first=5)
                head("memk", l, "dna", residual2(0.5, 2))
                dve.memset(w_diag[:].bitcast(F32), 0.0).then_inc(zero_ok, 1)
                rest("memk", None, l)
                head("memv", l, "memk", None)

                def memv_xr(c):
                    if c == 2:
                        step("memv", l, 0, 3)
                    if c in (4, 6, 7):
                        step("xr", l, 0, (c - 3) // 2)
                norm(n0 + 2, 0, gain_in(MIX_N), between=memv_xr)
                rest("xr", None, l)
                head("yr", l, "xr", None)

                def conv(w):
                    for c in range(DC):
                        src, tap = XR[:, c, 1 + w:1 + w + S], cur[:, CONV_W + 8 * w + c:CONV_W + 8 * w + c + 1]
                        if w == 0:
                            ins = dve.tensor_scalar(XC[:, c, :], src, tap, cur[:, CONV_B + c:CONV_B + c + 1], ALU.mult, ALU.add)
                        else:
                            dve.wait_ge(conv_ok, 8 * (w - 1) + c + 1 + l * 32)
                            ins = dve.scalar_tensor_tensor(XC[:, c, :], src, tap, XC[:, c, :], ALU.mult, ALU.add)
                        ins.then_inc(conv_ok, 1)

                dve.memset(XR[:, :, 0:4], 0.0).then_inc(pad_ok, 1)
                dve.wait_ge(pad_ok, 1 + l)
                dve.wait_ge(acc_free, J["xr"].done(l))
                conv(0)
                rest("yr", None, l, [lambda: conv(1), lambda: conv(2)])
                head("q", l, "yr", None)
                conv(3)
                rest("q", None, l)
                head("kvlru", l, "q", None)
                rest("kvlru", None, l)
                head("gates", l, "kvlru", None)

                def clamp():
                    dve.wait_ge(e2_ok, 8 + l * 16)
                    dve.tensor_scalar(XR[:, :, 0:S], XR[:, :, 0:S], 1.0, None, ALU.min).then_inc(cl_ok, 1)

                def multiply():
                    dve.wait_ge(mu_ok, 1 + l)
                    dve.memset(XR[:, :, 0:1], 1.0).then_inc(b_ok, 1)
                    dve.wait_ge(b_ok, 1 + l * 2)
                    dve.wait_ge(gx_ok, 1 + l)
                    dve.tensor_tensor(GI[:], GI[:], XR[:, :, 0:S], ALU.mult).then_inc(b_ok, 1)

                def scan():
                    dve.wait_ge(e2_ok, 16 + l * 16)
                    dve.wait_ge(b_ok, 2 + l * 2)
                    for c in range(DC):
                        dve.tensor_tensor_scan(XR[:, c, 0:S], R[:, c, :], GI[:, c, :], 0.0, ALU.mult, ALU.add).then_inc(scan_ok, 1)

                rest("gates", None, l, [lambda: None, clamp, multiply, scan])
                head("cq", l, "gates", None)
                dve.wait_ge(vt_ok, 1 + l)
                dve.tensor_copy(v_2[:].rearrange("p r n -> p (r n)"), wk[:, 3, 0:S]).then_inc(v2_ok, 1)
                rest("cq", None, l)
                head("lru_out", l, "cq", None)

                def recurrence_out(i):
                    for k in range(OUT_UNITS + LAG):
                        it, p = divmod(k, J["lru_out"].body)
                        if k >= LAG and split_step(k) == i:
                            if k < OUT_UNITS:
                                step("lru_out", l, it, p)
                            else:
                                step("attn_out", l, 0, k - OUT_UNITS)
                        if k < OUT_UNITS and p % 2 and min(4 * k + 3, 4 * OUT_UNITS - 2) == i:
                            block_done(J["lru_out"], l, it, p // 2)
                            branch(1)(l, it, p // 2)

                attention("second", groups_window() + groups_memory(), l, recurrence_out)
                rest("attn_out", branch(0), l)
                head("mem_out", l, "attn_out", branch(0))
                rest("mem_out", branch(2), l)
                head("w_out", l, "mem_out", branch(2))
                rest("w_out", residual2(1.0, 2), l)
                head("gub", l, "w_out", residual2(1.0, 2))
                norm(n0 + 3, 0, gain_in(FFN2_N))
                rest("gub", gate_up("gub", S, 33), l)
                head("dnb", l, "gub", gate_up("gub", S, 33))
                rest("dnb", residual2(0.5, 2), l)
                tail("dnb", residual2(0.5, 2), l)
                square_last("dnb", l)
            norm(NORM_LAST, 0, lambda c: prm[:, 3, FINAL_N + c:FINAL_N + c + 1], split_out=False)
            dve.wait_ge(fin_t, 3)
            dve.tensor_copy(rows[:, 512:D], fin_ps[0][1]).then_inc(fin_ok[0], 1)



INS = ["x", "c", "ctx", "c_ctx", "ada_w", "ada_b", "norm1_g", "norm2_g", "ffn_w_in", "ffn_w_out", "attn_w_qkv",
       "attn_q_norm", "attn_k_norm", "attn_sink", "attn_w_o", "ret_w_qkvg", "ret_decay_logit", "ret_gn_g", "ret_w_o",
       "mem_2", "ffn1_norm_2", "ffn1_w_gate_2", "ffn1_w_up_2", "ffn1_w_down_2", "mix_norm_2", "w_in_2", "gate_bias_2",
       "attn_sinks_2", "w_attn_out_2", "conv_w_2", "conv_b_2", "lru_wa_2", "lru_ba_2", "lru_wx_2", "lru_bx_2",
       "lru_lambda_2", "w_lru_out_2", "mem_norm_2", "w_mem_kv_2", "w_mem_out_2", "w_out_2", "ffn2_norm_2",
       "ffn2_w_gate_2", "ffn2_w_up_2", "ffn2_w_down_2", "final_norm_2"]


def kernel(**inputs):
    import concourse.bacc as bacc
    from concourse.bass_utils import run_bass_kernel_spmd

    nc = bacc.Bacc("TRN2", target_bir_lowering=False, num_devices=1)
    table, const_at = shape_constants()
    arrays, aps = {}, {}
    for name in INS + ["shape_constants"]:
        data = table if name == "shape_constants" else np.ascontiguousarray(inputs[name])
        arrays[f"in_{name}_dram"] = data
        aps[name] = nc.dram_tensor(f"in_{name}_dram", data.shape, mybir.dt.from_np(data.dtype), kind="ExternalInput").ap()
    out = nc.dram_tensor("out_0_dram", (1, S, D), F32, kind="ExternalOutput").ap()
    build(nc, aps, out, const_at)
    r = run_bass_kernel_spmd(nc, [arrays], core_ids=[0])
    return r.results[0]["out_0_dram"]
```
